# Optimizing a Trainium2 kernel written in Bass

```python
import math
import jax, jax.numpy as jnp
from jax import lax
import numpy as np
import jax
import jax.numpy as jnp

D_MODEL = 1024
BATCH = 1
SEQ = 2048
DEPTH = 1

D_MIX = D_MODEL
ATTN_WIDTH = D_MIX // 2
SSM_WIDTH = D_MIX - ATTN_WIDTH
QK_NOPE_DIM = 128
QK_ROPE_DIM = 64
V_HEAD_DIM = 128
N_ATTN_HEADS = ATTN_WIDTH // V_HEAD_DIM
Q_RANK = D_MODEL // 4
KV_RANK = D_MODEL // 8
ROPE_THETA = 10000.0
Q_BLOCK = 128
SSM_GROUP_CH = 16
SSM_GROUPS = SSM_WIDTH // SSM_GROUP_CH
SSM_STATE = 64
DT_MIN = 1e-3
DT_MAX = 1e-1
EPS = 1e-6
SPLITS = (Q_RANK, KV_RANK, QK_ROPE_DIM, ATTN_WIDTH, SSM_WIDTH, SSM_WIDTH)
D_IN = sum(SPLITS)


def _rms_norm(x, g):
    xf = x.astype(jnp.float32)
    y = xf * lax.rsqrt(jnp.mean(xf * xf, axis=-1, keepdims=True) + EPS)
    return (y * g.astype(jnp.float32)).astype(x.dtype)

def _rope_tables(positions, dim):
    inv_freq = ROPE_THETA ** (-jnp.arange(0, dim, 2, dtype=jnp.float32) / dim)
    ang = positions.astype(jnp.float32)[..., None] * inv_freq
    return jnp.cos(ang), jnp.sin(ang)

def _apply_rope(t, cos, sin):
    tf = t.astype(jnp.float32)
    t1, t2 = jnp.split(tf, 2, axis=-1)
    return jnp.concatenate([t1 * cos - t2 * sin, t1 * sin + t2 * cos], axis=-1).astype(t.dtype)

def _mla_attention(z_q, z_kv, z_kr, positions, q_norm_g, w_uq, kv_norm_g, w_ukv):
    bsz, seq, _ = z_q.shape
    q = (_rms_norm(z_q, q_norm_g) @ w_uq).reshape(bsz, seq, N_ATTN_HEADS, QK_NOPE_DIM + QK_ROPE_DIM)
    q_nope, q_rope = q[..., :QK_NOPE_DIM], q[..., QK_NOPE_DIM:]
    kv = (_rms_norm(z_kv, kv_norm_g) @ w_ukv).reshape(bsz, seq, N_ATTN_HEADS, QK_NOPE_DIM + V_HEAD_DIM)
    k_nope, v = kv[..., :QK_NOPE_DIM], kv[..., QK_NOPE_DIM:]
    cos, sin = _rope_tables(positions, QK_ROPE_DIM)
    q_rope = _apply_rope(q_rope, cos[:, :, None, :], sin[:, :, None, :])
    k_rope = _apply_rope(z_kr, cos, sin)
    n_blocks = seq // Q_BLOCK
    scale = (QK_NOPE_DIM + QK_ROPE_DIM) ** -0.5

    def to_blocks(t):
        return t.reshape(bsz, n_blocks, Q_BLOCK, *t.shape[2:]).swapaxes(0, 1)

    def attend_block(args):
        qn, qr = args
        s = (jnp.einsum('bqhd,bkhd->bhqk', qn, k_nope, preferred_element_type=jnp.float32)
             + jnp.einsum('bqhr,bkr->bhqk', qr, k_rope, preferred_element_type=jnp.float32))
        p = jax.nn.softmax(s * scale, axis=-1).astype(v.dtype)
        return jnp.einsum('bhqk,bkhd->bqhd', p, v)

    o = lax.map(attend_block, (to_blocks(q_nope), to_blocks(q_rope)))
    return o.swapaxes(0, 1).reshape(bsz, seq, N_ATTN_HEADS * V_HEAD_DIM)

def _diag_scan_op(e_i, e_j):
    a_i, b_i = e_i
    a_j, b_j = e_j
    return a_j * a_i, a_j * b_i + b_j

def _s5_bidirectional(u, lam_re, lam_im, log_dt, b_re, b_im, c_re, c_im, d_skip):
    bsz, seq, _ = u.shape
    u_t = u.astype(jnp.float32).reshape(bsz, seq, SSM_GROUPS, SSM_GROUP_CH).transpose(1, 0, 2, 3)
    u_c = u_t.astype(jnp.complex64)
    y = jnp.zeros_like(u_t)
    for direction, reverse in ((0, False), (1, True)):
        lam = lax.complex(jnp.minimum(lam_re[direction].astype(jnp.float32), -1e-4),
                          lam_im[direction].astype(jnp.float32))
        dt = jnp.exp(log_dt[direction].astype(jnp.float32))[:, None]
        lam_bar = jnp.exp(lam * dt)
        b = lax.complex(b_re[direction].astype(jnp.float32), b_im[direction].astype(jnp.float32))
        b_bar = ((lam_bar - 1.0) / lam)[..., None] * b
        c = lax.complex(c_re[direction].astype(jnp.float32), c_im[direction].astype(jnp.float32))
        bu = jnp.einsum('sbgh,gph->sbgp', u_c, b_bar)
        a = jnp.broadcast_to(lam_bar, (seq, 1, SSM_GROUPS, SSM_STATE))
        _, h = lax.associative_scan(_diag_scan_op, (a, bu), reverse=reverse, axis=0)
        y = y + jnp.real(jnp.einsum('sbgp,ghp->sbgh', h, c))
    y = y + d_skip.astype(jnp.float32).reshape(SSM_GROUPS, SSM_GROUP_CH) * u_t
    return y.transpose(1, 0, 2, 3).reshape(bsz, seq, SSM_WIDTH).astype(u.dtype)

def first_inputs(seed: int = 0) -> dict:
    key = jax.random.key(seed)
    ks = jax.random.split(key, 24)
    f32 = jnp.float32
    L, G, P, H = DEPTH, SSM_GROUPS, SSM_STATE, SSM_GROUP_CH

    def nrm(k, shape, std):
        return jax.random.normal(k, shape, f32) * std

    def gain(k, n):
        return 1.0 + 0.05 * jax.random.normal(k, (L, n), f32)

    x = jax.random.normal(ks[0], (BATCH, SEQ, D_MODEL), f32)
    inc = jax.random.randint(ks[1], (BATCH, SEQ), 1, 3, dtype=jnp.int32)
    positions = jnp.cumsum(inc, axis=1, dtype=jnp.int32) - 1
    n_idx = jnp.arange(P, dtype=f32)
    lam_re = -0.5 + 0.01 * jax.random.normal(ks[2], (L, 2, G, P), f32)
    lam_im = math.pi * n_idx + 0.01 * jax.random.normal(ks[3], (L, 2, G, P), f32)
    log_dt = jax.random.uniform(ks[4], (L, 2, G), f32, math.log(DT_MIN), math.log(DT_MAX))
    return {
        "x": x,
        "positions": positions,
        "pre_norm_g": gain(ks[5], D_MODEL),
        "w_in": nrm(ks[6], (L, D_MODEL, D_IN), D_MODEL ** -0.5),
        "q_norm_g": gain(ks[7], Q_RANK),
        "w_uq": nrm(ks[8], (L, Q_RANK, N_ATTN_HEADS * (QK_NOPE_DIM + QK_ROPE_DIM)), Q_RANK ** -0.5),
        "kv_norm_g": gain(ks[9], KV_RANK),
        "w_ukv": nrm(ks[10], (L, KV_RANK, N_ATTN_HEADS * (QK_NOPE_DIM + V_HEAD_DIM)), KV_RANK ** -0.5),
        "attn_out_g": gain(ks[11], ATTN_WIDTH),
        "s5_lam_re": lam_re,
        "s5_lam_im": lam_im,
        "s5_log_dt": log_dt,
        "s5_b_re": nrm(ks[12], (L, 2, G, P, H), (2.0 * H) ** -0.5),
        "s5_b_im": nrm(ks[13], (L, 2, G, P, H), (2.0 * H) ** -0.5),
        "s5_c_re": nrm(ks[14], (L, 2, G, H, P), (2.0 * P) ** -0.5),
        "s5_c_im": nrm(ks[15], (L, 2, G, H, P), (2.0 * P) ** -0.5),
        "s5_d": nrm(ks[16], (L, SSM_WIDTH), 1.0),
        "w_glu": nrm(ks[17], (L, SSM_WIDTH, SSM_WIDTH), SSM_WIDTH ** -0.5),
        "b_glu": nrm(ks[18], (L, SSM_WIDTH), 0.02),
        "ssm_out_g": gain(ks[19], SSM_WIDTH),
        "w_out": nrm(ks[20], (L, D_MIX, D_MODEL), D_MIX ** -0.5),
        "post_norm_g": gain(ks[21], D_MODEL),
    }

def first_block(x, positions, pre_norm_g, w_in, q_norm_g, w_uq, kv_norm_g, w_ukv, attn_out_g,
              s5_lam_re, s5_lam_im, s5_log_dt, s5_b_re, s5_b_im, s5_c_re, s5_c_im, s5_d,
              w_glu, b_glu, ssm_out_g, w_out, post_norm_g):
    split_points = list(np.cumsum(SPLITS)[:-1])
    for l in range(DEPTH):
        h = _rms_norm(x, pre_norm_g[l])
        z = h @ w_in[l]
        z_q, z_kv, z_kr, g_attn, u_ssm, g_ssm = jnp.split(z, split_points, axis=-1)
        attn = _mla_attention(z_q, z_kv, z_kr, positions, q_norm_g[l], w_uq[l], kv_norm_g[l], w_ukv[l])
        attn = _rms_norm(attn, attn_out_g[l]) * jax.nn.silu(g_attn)
        ssm = _s5_bidirectional(u_ssm, s5_lam_re[l], s5_lam_im[l], s5_log_dt[l], s5_b_re[l], s5_b_im[l],
                                s5_c_re[l], s5_c_im[l], s5_d[l])
        ssm = jax.nn.gelu(ssm)
        ssm = ssm * jax.nn.sigmoid(ssm @ w_glu[l] + b_glu[l])
        ssm = _rms_norm(ssm, ssm_out_g[l]) * jax.nn.silu(g_ssm)
        mixed = jnp.concatenate([attn, ssm], axis=-1) @ w_out[l]
        x = x + _rms_norm(mixed, post_norm_g[l])
    return x


CTX_LEN = 256
GRID_W = 64
HEAD_DIM = 64
ATTN_HEADS = 8
ATTN_KV_HEADS = 2
GQA_GROUP = ATTN_HEADS // ATTN_KV_HEADS
RET_HEADS = 4
RET_QK_DIM = 64
RET_V_DIM = 128
ATTN_WIDTH_2 = ATTN_HEADS * HEAD_DIM
RET_WIDTH = RET_HEADS * RET_V_DIM
MIX_WIDTH = ATTN_WIDTH_2 + RET_WIDTH
PROJ_SIZES = (ATTN_WIDTH_2, ATTN_KV_HEADS * HEAD_DIM, ATTN_KV_HEADS * HEAD_DIM,
              RET_HEADS * RET_QK_DIM, RET_HEADS * RET_QK_DIM, RET_WIDTH, RET_WIDTH)
PROJ_DIM = sum(PROJ_SIZES)
PROJ_SPLITS = tuple(int(v) for v in np.cumsum(PROJ_SIZES)[:-1])
RET_CHUNK = 128
ROPE_AXIS_DIM = HEAD_DIM // 2
N_GROUPS = 4
EXPERTS_PER_GROUP = 8
N_EXPERTS = N_GROUPS * EXPERTS_PER_GROUP
TOP_K_IN_GROUP = 2
D_EXPERT = 512
MOE_BLOCK = 128


def _rmsnorm(x, g):
    xf = x.astype(jnp.float32)
    xf = xf * lax.rsqrt(jnp.mean(xf * xf, axis=-1, keepdims=True) + EPS)
    return xf.astype(x.dtype) * g

def _modulate(xn, shift, scale):
    return xn * (1.0 + scale) + shift

def _axial_rope_tables(rows):
    row = jnp.repeat(jnp.arange(rows), GRID_W).astype(jnp.float32)
    col = jnp.tile(jnp.arange(GRID_W), rows).astype(jnp.float32)
    freqs = ROPE_THETA ** (-jnp.arange(0, ROPE_AXIS_DIM, 2, dtype=jnp.float32) / ROPE_AXIS_DIM)
    ang = jnp.concatenate([row[:, None] * freqs, col[:, None] * freqs], axis=-1)
    return jnp.cos(ang), jnp.sin(ang)

def _rope(x, cos, sin):
    B, L, H, d = x.shape
    xp = x.astype(jnp.float32).reshape(B, L, H, d // 2, 2)
    x0, x1 = xp[..., 0], xp[..., 1]
    c = cos[None, :, None, :]
    s = sin[None, :, None, :]
    out = jnp.stack([x0 * c - x1 * s, x0 * s + x1 * c], axis=-1).reshape(B, L, H, d)
    return out.astype(x.dtype)

def _attend(q, k, v):
    B, L, _, _ = q.shape
    nb = L // Q_BLOCK
    qb = jnp.moveaxis(q.reshape(B, nb, Q_BLOCK, ATTN_KV_HEADS, GQA_GROUP, HEAD_DIM), 1, 0)
    scale = HEAD_DIM ** -0.5

    def one_block(q_blk):
        s = jnp.einsum('bqhgd,bkhd->bhgqk', q_blk, k).astype(jnp.float32) * scale
        p = jax.nn.softmax(s, axis=-1)
        return jnp.einsum('bhgqk,bkhd->bqhgd', p.astype(v.dtype), v)

    o = lax.map(one_block, qb)
    return jnp.moveaxis(o, 0, 1).reshape(B, L, ATTN_WIDTH_2)

def _head_rms(x, g):
    xf = x.astype(jnp.float32)
    xf = xf * lax.rsqrt(jnp.mean(xf * xf, axis=-1, keepdims=True) + EPS)
    return xf.astype(x.dtype) * g

def _ret_heads(q, k, v, cos, sin):
    B, L, _ = q.shape
    q = q.reshape(B, L, RET_HEADS, RET_QK_DIM)
    k = k.reshape(B, L, RET_HEADS, RET_QK_DIM)
    if cos is not None:
        q = _rope(q, cos, sin)
        k = _rope(k, cos, sin)
    q = jnp.transpose(q, (0, 2, 1, 3)).astype(jnp.float32)
    k = jnp.transpose(k, (0, 2, 1, 3)).astype(jnp.float32) * (RET_QK_DIM ** -0.5)
    v = jnp.transpose(v.reshape(B, L, RET_HEADS, RET_V_DIM), (0, 2, 1, 3)).astype(jnp.float32)
    return q, k, v

def _retention_state(k, v, log_g, reverse):
    Lc = k.shape[2]
    m = jnp.arange(Lc, dtype=jnp.float32)
    dist = m if reverse else (Lc - 1 - m)
    w = jnp.exp(log_g[:, None] * dist[None, :])
    return jnp.einsum('bhmk,bhmv,hm->bhkv', k, v, w)

def _retention_chunked(q, k, v, log_g, s0, include_diag):
    B, H, L, dk = q.shape
    dv = v.shape[-1]
    C = RET_CHUNK
    n = L // C
    qc = q.reshape(B, H, n, C, dk)
    kc = k.reshape(B, H, n, C, dk)
    vc = v.reshape(B, H, n, C, dv)
    pos = jnp.arange(C, dtype=jnp.float32)
    diff = pos[:, None] - pos[None, :]
    mask = (diff >= 0) if include_diag else (diff > 0)
    dmat = jnp.where(mask, jnp.exp(log_g[:, None, None] * jnp.where(mask, diff, 0.0)[None]), 0.0)
    scores = jnp.einsum('bhnik,bhnjk->bhnij', qc, kc) * dmat[None, :, None]
    intra = jnp.einsum('bhnij,bhnjv->bhniv', scores, vc)
    zeta = jnp.exp(log_g[:, None] * (C - 1 - pos)[None, :])
    u = jnp.einsum('bhnjk,bhnjv,hj->bhnkv', kc, vc, zeta)
    g_chunk = jnp.exp(log_g * C)[None, :, None, None]

    def step(s, u_n):
        return g_chunk * s + u_n, s

    s_final, s_prev = lax.scan(step, s0, jnp.moveaxis(u, 2, 0))
    xi = jnp.exp(log_g[:, None] * (pos + 1.0)[None, :])
    cross = jnp.einsum('bhnik,nbhkv,hi->bhniv', qc, s_prev, xi)
    return (intra + cross).reshape(B, H, L, dv), s_final

def _retention_latent(q, k, v, k_c, v_c, log_gf, log_gb):
    s_f = _retention_state(k_c, v_c, log_gf, reverse=False)
    s_b = _retention_state(k_c, v_c, log_gb, reverse=True)
    o_f, _ = _retention_chunked(q, k, v, log_gf, s_f, True)
    o_b, _ = _retention_chunked(jnp.flip(q, 2), jnp.flip(k, 2), jnp.flip(v, 2), log_gb, s_b, False)
    return o_f + jnp.flip(o_b, 2)

def _retention_context(q, k, v, log_gf, log_gb):
    B, H, _, dk = q.shape
    s0 = jnp.zeros((B, H, dk, v.shape[-1]), jnp.float32)
    o_f, _ = _retention_chunked(q, k, v, log_gf, s0, True)
    o_b, _ = _retention_chunked(jnp.flip(q, 2), jnp.flip(k, 2), jnp.flip(v, 2), log_gb, s0, False)
    return o_f + jnp.flip(o_b, 2)

def _ret_output(o, gn_g, gn_b, gate, dtype):
    B, H, L, dv = o.shape
    mu = jnp.mean(o, axis=-1, keepdims=True)
    var = jnp.mean(jnp.square(o - mu), axis=-1, keepdims=True)
    on = (o - mu) * lax.rsqrt(var + EPS)
    on = jnp.transpose(on, (0, 2, 1, 3)).reshape(B, L, H * dv).astype(dtype)
    return (on * gn_g + gn_b) * jax.nn.silu(gate)

def _hier_moe(h, w_grp, b_grp, w_exp, b_exp, w_gate, w_up, w_down):
    T, D = h.shape
    grp_p = jax.nn.softmax((h @ w_grp).astype(jnp.float32) + b_grp, axis=-1)
    p_g, g_idx = lax.top_k(grp_p, 1)
    exp_logits = ((h @ w_exp).astype(jnp.float32) + b_exp).reshape(T, N_GROUPS, EXPERTS_PER_GROUP)
    sel = jnp.take_along_axis(exp_logits, jnp.broadcast_to(g_idx[:, :, None], (T, 1, EXPERTS_PER_GROUP)), axis=1)[:, 0]
    p_e, j_idx = lax.top_k(jax.nn.softmax(sel, axis=-1), TOP_K_IN_GROUP)
    weights = p_g * (p_e / jnp.sum(p_e, axis=-1, keepdims=True))
    eid = (g_idx * EXPERTS_PER_GROUP + j_idx).astype(jnp.int32)

    A = T * TOP_K_IN_GROUP
    eid_f = eid.reshape(A)
    tok_f = jnp.repeat(jnp.arange(T, dtype=jnp.int32), TOP_K_IN_GROUP)
    w_f = weights.reshape(A)
    order = jnp.argsort(eid_f)
    e_s, tok_s, w_s = eid_f[order], tok_f[order], w_f[order]
    counts = jnp.zeros((N_EXPERTS,), jnp.int32).at[eid_f].add(1)
    starts = jnp.cumsum(counts) - counts
    pcounts = (counts + MOE_BLOCK - 1) // MOE_BLOCK * MOE_BLOCK
    pends = jnp.cumsum(pcounts)
    pstarts = pends - pcounts
    dest = pstarts[e_s] + (jnp.arange(A, dtype=jnp.int32) - starts[e_s])
    P = A + N_EXPERTS * MOE_BLOCK
    nblk = P // MOE_BLOCK
    buf_tok = jnp.full((P,), T, jnp.int32).at[dest].set(tok_s)
    buf_w = jnp.zeros((P,), jnp.float32).at[dest].set(w_s).astype(h.dtype)
    blk_start = jnp.arange(nblk, dtype=jnp.int32) * MOE_BLOCK
    blk_e = jnp.minimum(jnp.sum(blk_start[:, None] >= pends[None, :], axis=1), N_EXPERTS - 1)
    h_pad = jnp.concatenate([h, jnp.zeros((1, D), h.dtype)], axis=0)
    xb = h_pad[buf_tok].reshape(nblk, MOE_BLOCK, D)

    def expert_block(args):
        x_blk, e = args
        return (jax.nn.silu(x_blk @ w_gate[e]) * (x_blk @ w_up[e])) @ w_down[e]

    yb = lax.map(expert_block, (xb, blk_e)).reshape(P, D)
    out = jnp.zeros((T + 1, D), h.dtype).at[buf_tok].add(yb * buf_w[:, None])
    return out[:T]

def second_inputs(seed: int = 0) -> dict:
    key = jax.random.key(seed)
    ks = jax.random.split(key, 32)
    f32 = jnp.float32

    def nrm(k, shape, scale):
        return jax.random.normal(k, shape, f32) * scale

    base_logit = jnp.asarray(np.log(2.0 ** (5 + np.arange(RET_HEADS)) - 1.0).astype(np.float32))
    return {
        "x": nrm(ks[0], (BATCH, SEQ, D_MODEL), 1.0),
        "c": nrm(ks[1], (BATCH, D_MODEL), 1.0),
        "ctx": nrm(ks[2], (BATCH, CTX_LEN, D_MODEL), 1.0),
        "c_ctx": nrm(ks[3], (D_MODEL,), 1.0),
        "w_ada": nrm(ks[4], (DEPTH, D_MODEL, 6 * D_MODEL), 0.5 * D_MODEL ** -0.5),
        "b_ada": nrm(ks[5], (DEPTH, 6 * D_MODEL), 0.01),
        "norm1_g": 1.0 + nrm(ks[6], (DEPTH, D_MODEL), 0.05),
        "w_in": nrm(ks[7], (DEPTH, D_MODEL, PROJ_DIM), D_MODEL ** -0.5),
        "attn_q_norm": 1.0 + nrm(ks[8], (DEPTH, HEAD_DIM), 0.05),
        "attn_k_norm": 1.0 + nrm(ks[9], (DEPTH, HEAD_DIM), 0.05),
        "ret_decay_fwd": base_logit + nrm(ks[10], (DEPTH, RET_HEADS), 0.1),
        "ret_decay_bwd": base_logit + nrm(ks[11], (DEPTH, RET_HEADS), 0.1),
        "ret_gn_g": 1.0 + nrm(ks[12], (DEPTH, RET_WIDTH), 0.05),
        "ret_gn_b": nrm(ks[13], (DEPTH, RET_WIDTH), 0.01),
        "w_out": nrm(ks[14], (DEPTH, MIX_WIDTH, D_MODEL), MIX_WIDTH ** -0.5),
        "norm2_g": 1.0 + nrm(ks[15], (DEPTH, D_MODEL), 0.05),
        "moe_w_grp": nrm(ks[16], (DEPTH, D_MODEL, N_GROUPS), D_MODEL ** -0.5),
        "moe_b_grp": nrm(ks[17], (DEPTH, N_GROUPS), 0.01),
        "moe_w_exp": nrm(ks[18], (DEPTH, D_MODEL, N_EXPERTS), D_MODEL ** -0.5),
        "moe_b_exp": nrm(ks[19], (DEPTH, N_EXPERTS), 0.01),
        "moe_w_gate": nrm(ks[20], (DEPTH, N_EXPERTS, D_MODEL, D_EXPERT), D_MODEL ** -0.5),
        "moe_w_up": nrm(ks[21], (DEPTH, N_EXPERTS, D_MODEL, D_EXPERT), D_MODEL ** -0.5),
        "moe_w_down": nrm(ks[22], (DEPTH, N_EXPERTS, D_EXPERT, D_MODEL), D_EXPERT ** -0.5),
        "final_norm_g": 1.0 + nrm(ks[23], (D_MODEL,), 0.05),
    }

def second_block(x, c, ctx, c_ctx, w_ada, b_ada, norm1_g, w_in, attn_q_norm, attn_k_norm,
              ret_decay_fwd, ret_decay_bwd, ret_gn_g, ret_gn_b, w_out, norm2_g,
              moe_w_grp, moe_b_grp, moe_w_exp, moe_b_exp, moe_w_gate, moe_w_up, moe_w_down,
              final_norm_g):
    B, L, D = x.shape
    CL = ctx.shape[1]
    ROWS = L // GRID_W
    cos, sin = _axial_rope_tables(ROWS)

    for l in range(DEPTH):
        mod_x = (jax.nn.silu(c) @ w_ada[l] + b_ada[l])[:, None, :]
        mod_c = (jax.nn.silu(c_ctx) @ w_ada[l] + b_ada[l])[None, None, :]
        sh1, sc1, gt1, sh2, sc2, gt2 = jnp.split(mod_x, 6, axis=-1)
        csh1, csc1, cgt1, csh2, csc2, cgt2 = jnp.split(mod_c, 6, axis=-1)
        log_gf = jax.nn.log_sigmoid(ret_decay_fwd[l].astype(jnp.float32))
        log_gb = jax.nn.log_sigmoid(ret_decay_bwd[l].astype(jnp.float32))

        hx = _modulate(_rmsnorm(x, norm1_g[l]), sh1, sc1)
        hc = _modulate(_rmsnorm(ctx, norm1_g[l]), csh1, csc1)
        qa, ka, va, qr, kr, vr, gr = jnp.split(hx @ w_in[l], PROJ_SPLITS, axis=-1)
        qa_c, ka_c, va_c, qr_c, kr_c, vr_c, gr_c = jnp.split(hc @ w_in[l], PROJ_SPLITS, axis=-1)

        qa = _rope(_head_rms(qa.reshape(B, L, ATTN_HEADS, HEAD_DIM), attn_q_norm[l]), cos, sin)
        ka = _rope(_head_rms(ka.reshape(B, L, ATTN_KV_HEADS, HEAD_DIM), attn_k_norm[l]), cos, sin)
        va = va.reshape(B, L, ATTN_KV_HEADS, HEAD_DIM)
        ka_c = _head_rms(ka_c.reshape(B, CL, ATTN_KV_HEADS, HEAD_DIM), attn_k_norm[l])
        va_c = va_c.reshape(B, CL, ATTN_KV_HEADS, HEAD_DIM)
        attn_x = _attend(qa, jnp.concatenate([ka_c, ka], axis=1), jnp.concatenate([va_c, va], axis=1))

        q_r, k_r, v_r = _ret_heads(qr, kr, vr, cos, sin)
        q_rc, k_rc, v_rc = _ret_heads(qr_c, kr_c, vr_c, None, None)
        ret_o = _retention_latent(q_r, k_r, v_r, k_rc, v_rc, log_gf, log_gb)
        ret_x = _ret_output(ret_o, ret_gn_g[l], ret_gn_b[l], gr, x.dtype)

        x_new = x + gt1 * (jnp.concatenate([attn_x, ret_x], axis=-1) @ w_out[l])

        h2 = _modulate(_rmsnorm(x_new, norm2_g[l]), sh2, sc2)
        y = _hier_moe(h2.reshape(B * L, D), moe_w_grp[l], moe_b_grp[l], moe_w_exp[l], moe_b_exp[l],
                      moe_w_gate[l], moe_w_up[l], moe_w_down[l]).reshape(B, L, D)
        x_new = x_new + gt2 * y

        if l + 1 < DEPTH:
            qa_c = _head_rms(qa_c.reshape(B, CL, ATTN_HEADS, HEAD_DIM), attn_q_norm[l])
            attn_c = _attend(qa_c, ka_c, va_c)
            ret_c = _ret_output(_retention_context(q_rc, k_rc, v_rc, log_gf, log_gb),
                                ret_gn_g[l], ret_gn_b[l], gr_c, ctx.dtype)
            ctx_new = ctx + cgt1 * (jnp.concatenate([attn_c, ret_c], axis=-1) @ w_out[l])
            h2c = _modulate(_rmsnorm(ctx_new, norm2_g[l]), csh2, csc2)
            yc = _hier_moe(h2c.reshape(B * CL, D), moe_w_grp[l], moe_b_grp[l], moe_w_exp[l], moe_b_exp[l],
                           moe_w_gate[l], moe_w_up[l], moe_w_down[l]).reshape(B, CL, D)
            ctx = ctx_new + cgt2 * yc
        x = x_new

    return _rmsnorm(x, final_norm_g)


def setup_inputs(seed=0):
    out = dict(first_inputs(seed))
    for name, value in second_inputs(seed + 1).items():
        if name != "x":
            out[name + "_2"] = value
    return out


def reference(
    x, positions, pre_norm_g, w_in, q_norm_g, w_uq, kv_norm_g, w_ukv, attn_out_g, s5_lam_re,
    s5_lam_im, s5_log_dt, s5_b_re, s5_b_im, s5_c_re, s5_c_im, s5_d, w_glu, b_glu, ssm_out_g,
    w_out, post_norm_g, c_2, ctx_2, c_ctx_2, w_ada_2, b_ada_2, norm1_g_2, w_in_2, attn_q_norm_2,
    attn_k_norm_2, ret_decay_fwd_2, ret_decay_bwd_2, ret_gn_g_2, ret_gn_b_2, w_out_2, norm2_g_2,
    moe_w_grp_2, moe_b_grp_2, moe_w_exp_2, moe_b_exp_2, moe_w_gate_2, moe_w_up_2, moe_w_down_2,
    final_norm_g_2,
):
    x = first_block(
        x, positions, pre_norm_g, w_in, q_norm_g, w_uq, kv_norm_g, w_ukv, attn_out_g, s5_lam_re,
        s5_lam_im, s5_log_dt, s5_b_re, s5_b_im, s5_c_re, s5_c_im, s5_d, w_glu, b_glu, ssm_out_g,
        w_out, post_norm_g,
    )
    return second_block(
        x, c_2, ctx_2, c_ctx_2, w_ada_2, b_ada_2, norm1_g_2, w_in_2, attn_q_norm_2,
        attn_k_norm_2, ret_decay_fwd_2, ret_decay_bwd_2, ret_gn_g_2, ret_gn_b_2, w_out_2,
        norm2_g_2, moe_w_grp_2, moe_b_grp_2, moe_w_exp_2, moe_b_exp_2, moe_w_gate_2, moe_w_up_2,
        moe_w_down_2, final_norm_g_2,
    )


_drawn_inputs = setup_inputs


def setup_inputs(seed=0):
    import zlib

    import numpy as np

    out = dict(_drawn_inputs(seed))
    spreads = {}
    factors = {'s5_lam_re': 64.0,
     'b_glu': 8.0,
     'ctx_2': 4.735,
     'c_ctx_2': 4.066,
     'b_ada_2': 6.044,
     'norm1_g_2': 5.173,
     'attn_q_norm_2': 8.0,
     'attn_k_norm_2': 8.0,
     'ret_gn_g_2': 8.0,
     'ret_gn_b_2': 8.0,
     'norm2_g_2': 4.031,
     'moe_b_grp_2': 8.0,
     'moe_b_exp_2': 27.973}
    for name, (base, spread) in spreads.items():
        noise = np.random.default_rng([zlib.crc32(name.encode()), seed]).standard_normal(out[name].shape)
        drawn = base * np.exp(spread * noise) if base else spread * noise
        out[name] = jnp.asarray(drawn.astype(out[name].dtype))
    for name, factor in factors.items():
        out[name] = (out[name] * factor).astype(out[name].dtype)
    return out
```

```python
import math
from contextlib import ExitStack

import numpy as np

import concourse.bass as bass
from concourse import mybir

F32 = mybir.dt.float32
I32 = mybir.dt.int32
U32 = mybir.dt.uint32
ALU = mybir.AluOpType
ACT = mybir.ActivationFunctionType
AX_X = mybir.AxisListType.X
ds = bass.ds

P = 128
BANK = 512
DM = 1024
KC = DM // P
SEQ = 2048
NT = SEQ // P
EPS = 1e-6

QR, KVR, RD = 256, 128, 64
H1, DN, DV = 4, 128, 128
AW = H1 * DV
SW = 512
SM = SW // P
D_IN = QR + KVR + RD + AW + 2 * SW
ZC = QR + KVR + RD
T8 = 8
NCH = SEQ // T8
NG, GC, NS = 32, 16, 64

TWO_PI_A = 6.28125
TWO_PI_B = float(np.float32(np.floor((2 * math.pi - TWO_PI_A) * 2**21) / 2**21))
TWO_PI_C = 2 * math.pi - TWO_PI_A - TWO_PI_B
ROUND = float(1.5 * 2**23)
PI32 = 3.1415925


def bcast(ap, shape):
    return ap.to_broadcast(shape)


class Tile:

    def __init__(self, i, b, n):
        self.i, self.b, self.n, self.first = i, b, n, isinstance(i, int) and i == 0

    def before(self):
        return Tile(self.i - 1, 1 - self.b, self.n if self.b else self.n - 1)

    def tokens(self):
        return ds(self.i * P, P)


def tile_at(i):
    return Tile(i, i % 2, i // 2)


def tiles(eng, n, body, last=1):
    body(tile_at(0))
    turns = (n - 1 - last) // 2
    assert 1 + 2 * turns + last == n
    with eng.Fori(0, turns) as j:
        body(Tile(2 * j + 1, 1, j))
        body(Tile(2 * j + 2, 0, j + 1))
    for i in range(n - last, n):
        body(tile_at(i))


class Kit:

    def __init__(self, nc, ctx, stage):
        self.nc, self.ctx, self.stage, self.sems = nc, ctx, stage, []
        ctx.callback(self.release)

    def release(self):
        if not self.sems:
            return
        with self.nc.Block() as block:
            @block.sync
            def _(sp):
                for sem in self.sems:
                    sp.sem_clear(sem)
        for sem in self.sems:
            self.nc.release_semaphore(sem)

    def sb(self, name, shape, dt=F32):
        return self.ctx.enter_context(self.nc.sbuf_tensor(f"{self.stage}_{name}", shape, dt))

    def ps(self, name, shape=(P, BANK), dt=F32):
        return self.ctx.enter_context(self.nc.psum_tensor(f"{self.stage}_{name}", list(shape), dt))

    def sem(self, name):
        self.sems.append(self.nc.alloc_semaphore(f"{self.stage}_{name}"))
        return self.sems[-1]


def in_turn(eng, sem):
    n = [0]

    def do(ins):
        n[0] += 1
        ins.then_inc(sem, 1)
        eng.wait_ge(sem, n[0])
    return do


def reduce_angle(dve, do, out, k, angle, quarter):
    do(dve.tensor_scalar(k, angle, 1 / (2 * math.pi), 0.25 if quarter else 0.0, ALU.mult, ALU.add))
    do(dve.tensor_scalar(k, k, ROUND, None, ALU.add))
    do(dve.tensor_scalar(k, k, ROUND, None, ALU.subtract))
    do(dve.scalar_tensor_tensor(out, k, -TWO_PI_A, angle, ALU.mult, ALU.add))
    do(dve.scalar_tensor_tensor(out, k, -TWO_PI_B, out, ALU.mult, ALU.add))
    do(dve.scalar_tensor_tensor(out, k, -TWO_PI_C, out, ALU.mult, ALU.add))
    if quarter:
        do(dve.tensor_scalar(out, out, math.pi / 2, None, ALU.add))
    do(dve.tensor_scalar(out, out, PI32, -PI32, ALU.min, ALU.max))


def rope_tables(nc, I, cos1, sin1):
    with ExitStack() as ctx:
        k = Kit(nc, ctx, "rope")
        pos_i = k.sb("pos_i", [P, NT], I32)
        pos_f = k.sb("pos_f", [P, NT])
        freq = k.sb("freq", [P, RD // 2])
        ang = k.sb("rope_ang", [P, NT, RD // 2])
        kk = k.sb("rope_k", [P, NT, RD // 2])
        loaded, step, reduced, done = (k.sem(n) for n in ("pos_loaded", "rope_step", "rope_reduced", "rope_done"))
        block = ctx.enter_context(nc.Block())

        @block.sync
        def _(sp):
            sp.dma_start(pos_i[:], I["positions"]).then_inc(loaded, 16)
            sp.dma_start(freq[:], I["inv_freq"]).then_inc(loaded, 16)

        @block.vector
        def _(dve):
            do = in_turn(dve, step)
            dve.wait_ge(loaded, 32)
            do(dve.tensor_copy(pos_f[:], pos_i[:]))
            shape = [P, NT, RD // 2]
            do(dve.tensor_tensor(ang[:], bcast(pos_f[:].unsqueeze(2), shape), bcast(freq[:].unsqueeze(1), shape), ALU.mult))
            reduce_angle(dve, do, sin1[:], kk[:], ang[:], False)
            reduce_angle(dve, do, cos1[:], kk[:], ang[:], True)
            dve.sem_inc(reduced, 1)

        @block.scalar
        def _(act):
            act.wait_ge(reduced, 1)
            act.activation(sin1[:], sin1[:], ACT.Sin).then_inc(done, 1)
            act.activation(cos1[:], cos1[:], ACT.Sin).then_inc(done, 1)


def project_1(nc, I, D, C, cos1, sin1):
    with ExitStack() as ctx:
        k = Kit(nc, ctx, "p1")
        w_in = k.sb("w_in", [P, KC, D_IN])
        w_uq = k.sb("w_uq", [P, QR // P, H1 * (DN + RD)])
        w_ukv = k.sb("w_ukv", [P, H1 * (DN + DV)])
        pre_g, q_g, kv_g = k.sb("pre_g", [P, KC]), k.sb("q_g", [P, QR // P]), k.sb("kv_g", [P, 1])
        X = [k.sb(f"X{b}", [P, DM]) for b in range(2)]
        square = k.sb("square", [P, DM])
        HT = [k.sb(f"HT{b}", [P, KC, P]) for b in range(2)]
        Z = [k.sb(f"Z{b}", [P, ZC]) for b in range(2)]
        ZT = k.sb("ZT", [P, 3, P])
        GA = [k.sb(f"GA{b}", [P, AW]) for b in range(2)]
        GS = [k.sb(f"GS{b}", [P, SM, P]) for b in range(2)]
        U = k.sb("U", [P, SM, T8, NCH])
        QN = [k.sb(f"QN{b}", [P, H1, P]) for b in range(2)]
        KN = [k.sb(f"KN{b}", [P, H1, P]) for b in range(2)]
        VB = [k.sb(f"VB{b}", [P, AW]) for b in range(2)]
        QRO = k.sb("QRO", [P, H1, RD])
        KRO = k.sb("KRO", [P, 2, RD])
        ROT = k.sb("ROT", [P, H1, RD])
        QRT = [k.sb(f"QRT{b}", [P, 2, P]) for b in range(2)]
        KRT = [k.sb(f"KRT{b}", [P, P]) for b in range(2)]
        ssq, std, rstd = ([k.sb(f"{n}{b}", [P, 1]) for b in range(2)] for n in ("ssq", "std", "rstd"))
        zss, zstd, zrstd = ([k.sb(f"{n}{b}", [P, 2]) for b in range(2)] for n in ("zss", "zstd", "zrstd"))
        pT = [k.ps(f"pT{b}") for b in range(2)]
        pA, pB, pC, pD, pE, pF = (k.ps(f"p{n}") for n in "ABCDEF")
        names = """weights_loaded ssq_done std_ready rstd_ready h_ready hT_ps hT_ready mmA mmB mmC mmD
            z_ready ga_copied u_copied gs_copied zss_done zstd_ready zrstd_ready zn_ready znT_ps znT_ready
            qn_ps qn_copied v_ps v_copied kn_ps kn_copied qr_ps rope_a rope_b qrope_ready krope_ready qrT_ps qrT_copied
            krT_ps krT_copied u_stored sp_turn""".split()
        S = {n: k.sem(n) for n in names}
        x_loaded, stored_1, stored_2 = ([k.sem(f"{n}{b}") for b in range(2)] for n in ("x_loaded", "stored_1_", "stored_2_"))
        block = ctx.enter_context(nc.Block())

        @block.sync
        def _(sp):
            def wait(sem, value):
                sp.wait_ge(sem, value)
                sp.sem_inc(S["sp_turn"], 1)

            def load_x(i, b):
                sp.dma_start(X[b][:], I["x"][ds(i * P, P), :]).then_inc(x_loaded[b], 16)

            for b in range(2):
                sp.sem_inc(stored_1[b], 32)
                sp.sem_inc(stored_2[b], 80)
            load_x(0, 0)
            load_x(1, 1)
            for t, s in ((pre_g, "pre_g"), (q_g, "q_g"), (kv_g, "kv_g")):
                sp.dma_start(t[:], I[s]).then_inc(S["weights_loaded"], 16)
            sp.dma_start(w_in[:], I["w_in"].rearrange("(k p) n -> p k n", p=P)).then_inc(S["weights_loaded"], 16)
            sp.dma_start(w_uq[:], I["w_uq"].rearrange("(k p) n -> p k n", p=P)).then_inc(S["weights_loaded"], 16)
            sp.dma_start(w_ukv[:], I["w_ukv"]).then_inc(S["weights_loaded"], 16)

            def store_first(t):
                wait(S["ga_copied"], t.i + 1)
                sp.dma_start(D["ga"][t.tokens(), :], GA[t.b][:]).then_inc(stored_1[t.b], 16)
                wait(S["gs_copied"], t.i + 1)
                sp.dma_start(D["gs"].rearrange("(m p) t -> p m t", p=P)[:, :, t.tokens()], GS[t.b][:]).then_inc(stored_1[t.b], 16)

            def store_second(t):
                tok, b = t.tokens(), t.b
                for ready, credit, dst, src in (
                    ("qn_copied", 0, D["qn"].rearrange("(h p) t -> p h t", p=P)[:, :, tok], QN[b]),
                    ("v_copied", 1, D["v"][tok, :], VB[b]),
                    ("kn_copied", 1, D["kn"].rearrange("(h p) t -> p h t", p=P)[:, :, tok], KN[b]),
                    ("qrT_copied", 1, D["qr"].rearrange("(c p) t -> p c t", p=P)[:, :, tok], QRT[b]),
                    ("krT_copied", 1, D["kr"][:, tok], KRT[b]),
                ):
                    wait(S[ready], t.i + 1 + credit)
                    sp.dma_start(dst, src[:]).then_inc(stored_2[b], 16)

            def tile(t):
                if not (isinstance(t.i, int) and t.i >= NT - 2):
                    wait(S["hT_ps"], 2 * t.i + 2)
                    load_x(t.i + 2, t.b)
                store_first(t)
                if not t.first:
                    store_second(t.before())

            tiles(sp, NT, tile, last=3)
            store_second(tile_at(NT - 1))
            wait(S["u_copied"], NT)
            sp.dma_start(D["u"].rearrange("(m p) n -> p m n", p=P), U[:].rearrange("p m t c -> p m (t c)")).then_inc(S["u_stored"], 16)
            sp.wait_ge(S["u_stored"], 16)
            for b in range(2):
                sp.wait_ge(stored_1[b], 32 + 32 * (NT // 2))
                sp.wait_ge(stored_2[b], 80 + 80 * (NT // 2))

        @block.tensor
        def _(pe):
            def stage_two_a(t):
                i, b = t.i, t.b
                pe.wait_ge(S["zn_ready"], i + 1)
                pe.wait_ge(S["krT_copied"], i + 1)
                for c in range(3):
                    tr = pe.transpose(pE[:, c * P:(c + 1) * P], Z[b][:, c * P:(c + 1) * P], C["ident"][:])
                tr.then_inc(S["znT_ps"], 1)

            def stage_two_b(t):
                i, b = t.i, t.b
                pe.wait_ge(S["znT_ready"], i + 1)
                pe.wait_ge(S["qrT_copied"], i + 1)
                for h in range(H1):
                    for c in range(2):
                        w = w_uq[:, c, h * (DN + RD):h * (DN + RD) + DN]
                        m = pe.matmul(pF[:, h * P:(h + 1) * P], w, ZT[:, c, :], start=c == 0, stop=c == 1)
                m.then_inc(S["qn_ps"], 1)
                kv = w_ukv[:].rearrange("p (h x d) -> p h x d", h=H1, x=2)
                pe.matmul(pT[0][:], ZT[:, 2, :], kv[:, :, 1, :], start=True, stop=True).then_inc(S["v_ps"], 1)
                for h in range(H1):
                    m = pe.matmul(pT[1][:, h * P:(h + 1) * P], kv[:, h, 0, :], ZT[:, 2, :], start=True, stop=True)
                m.then_inc(S["kn_ps"], 1)
                wr = w_uq[:].rearrange("p c (h d) -> p c h d", h=H1)
                for c in range(2):
                    m = pe.matmul(pE[:, 0:H1 * RD], ZT[:, c, :], wr[:, c, :, DN:DN + RD], start=c == 0, stop=c == 1)
                m.then_inc(S["qr_ps"], 1)

            def stage_two_c(t):
                i, b = t.i, t.b
                pe.wait_ge(S["qn_copied"], i + 1)
                pe.wait_ge(S["qrope_ready"], i + 1)
                for c in range(2):
                    tr = pe.transpose(pF[:, c * P:(c + 1) * P], QRO[:, 2 * c:2 * c + 2, :].rearrange("p h d -> p (h d)"), C["ident"][:])
                tr.then_inc(S["qrT_ps"], 1)
                pe.wait_ge(S["krope_ready"], i + 1)
                pe.transpose(pE[:, 0:P], KRO[:].rearrange("p a d -> p (a d)"), C["ident"][:]).then_inc(S["krT_ps"], 1)

            def tile(t):
                i, b = t.i, t.b
                pe.wait_ge(S["h_ready"], i + 1)
                if t.first:
                    pe.wait_ge(S["weights_loaded"], 96)
                else:
                    pe.wait_ge(S["v_copied"], i)
                    pe.wait_ge(S["kn_copied"], i)
                for c in range(KC):
                    tr = pe.transpose(pT[c // 4][:, (c % 4) * P:(c % 4 + 1) * P], X[b][:, c * P:(c + 1) * P], C["ident"][:])
                    if c % 4 == 3:
                        tr.then_inc(S["hT_ps"], 1)
                if not t.first:
                    stage_two_a(t.before())
                pe.wait_ge(S["hT_ready"], 2 * i + 2)
                for bank, cols, made, free in ((pA, (0, ZC), "mmA", "z_ready"), (pB, (ZC, ZC + AW), "mmB", "ga_copied")):
                    if not t.first:
                        pe.wait_ge(S[free], i)
                    for c in range(KC):
                        m = pe.matmul(bank[:, 0:cols[1] - cols[0]], HT[b][:, c, :], w_in[:, c, cols[0]:cols[1]], start=c == 0, stop=c == KC - 1)
                    m.then_inc(S[made], 1)
                if not t.first:
                    stage_two_b(t.before())
                for bank, col, made, free in ((pC, ZC + AW, "mmC", "u_copied"), (pD, ZC + AW + SW, "mmD", "gs_copied")):
                    if not t.first:
                        pe.wait_ge(S[free], i)
                    for m4 in range(SM):
                        for c in range(KC):
                            w = w_in[:, c, col + m4 * P:col + (m4 + 1) * P]
                            m = pe.matmul(bank[:, m4 * P:(m4 + 1) * P], w, HT[b][:, c, :], start=c == 0, stop=c == KC - 1)
                    m.then_inc(S[made], 1)
                if not t.first:
                    stage_two_c(t.before())

            tiles(pe, NT, tile)
            stage_two_a(tile_at(NT - 1))
            stage_two_b(tile_at(NT - 1))
            stage_two_c(tile_at(NT - 1))

        @block.scalar
        def _(act):
            def latent_stats(t):
                i, b = t.i, t.b
                act.wait_ge(S["z_ready"], i + 1)
                act.activation(square[:, 0:QR], Z[b][:, 0:QR], ACT.Square, accum_out=zss[b][:, 0:1])
                act.activation(square[:, QR:QR + KVR], Z[b][:, QR:QR + KVR], ACT.Square, accum_out=zss[b][:, 1:2]).then_inc(S["zss_done"], 1)
                act.wait_ge(S["zss_done"], i + 1)
                act.activation(zstd[b][:, 0:1], zss[b][:, 0:1], ACT.Sqrt, bias=C["eps"][:], scale=1 / QR)
                act.activation(zstd[b][:, 1:2], zss[b][:, 1:2], ACT.Sqrt, bias=C["eps"][:], scale=1 / KVR).then_inc(S["zstd_ready"], 1)

            def latent_evac(t):
                i, b = t.i, t.b
                act.wait_ge(S["znT_ps"], i + 1)
                for c in range(3):
                    g = q_g[:, c:c + 1] if c < 2 else kv_g[:]
                    a = act.activation(ZT[:, c, :], pE[:, c * P:(c + 1) * P], ACT.Copy, scale=g)
                a.then_inc(S["znT_ready"], 1)

            def stage_two_copies(t):
                i, b = t.i, t.b
                act.wait_ge(stored_2[b], 80 * t.n + 80)
                for bank, dst, made, done in ((pF, QN[b], "qn_ps", "qn_copied"), (pT[0], VB[b], "v_ps", "v_copied"), (pT[1], KN[b], "kn_ps", "kn_copied")):
                    act.wait_ge(S[made], i + 1)
                    out = dst[:] if dst is VB[b] else dst[:].rearrange("p h t -> p (h t)")
                    act.activation(out, bank[:], ACT.Copy).then_inc(S[done], 1)

            def tile(t):
                i, b = t.i, t.b
                act.wait_ge(x_loaded[b], 16 * t.n + 16)
                act.activation(square[:], X[b][:], ACT.Square, accum_out=ssq[b][:]).then_inc(S["ssq_done"], 1)
                act.wait_ge(S["ssq_done"], i + 1)
                act.activation(std[b][:], ssq[b][:], ACT.Sqrt, bias=C["eps"][:], scale=1 / DM).then_inc(S["std_ready"], 1)
                if t.first:
                    act.sem_inc(S["v_copied"], 1)
                    act.sem_inc(S["kn_copied"], 1)
                    act.wait_ge(S["weights_loaded"], 96)
                else:
                    latent_stats(t.before())
                for half in range(2):
                    act.wait_ge(S["hT_ps"], 2 * i + half + 1)
                    for c in range(4 * half, 4 * half + 4):
                        a = act.activation(HT[b][:, c, :], pT[half][:, (c % 4) * P:(c % 4 + 1) * P], ACT.Copy, scale=pre_g[:, c:c + 1])
                    a.then_inc(S["hT_ready"], 1)
                if not t.first:
                    latent_evac(t.before())
                act.wait_ge(stored_1[b], 32 * t.n + 32)
                act.wait_ge(S["mmB"], i + 1)
                act.activation(GA[b][:], pB[:], ACT.Copy).then_inc(S["ga_copied"], 1)
                if not t.first:
                    stage_two_copies(t.before())
                act.wait_ge(S["mmD"], i + 1)
                act.activation(GS[b][:].rearrange("p m t -> p (m t)"), pD[:], ACT.Copy).then_inc(S["gs_copied"], 1)

            tiles(act, NT, tile)
            latent_stats(tile_at(NT - 1))
            latent_evac(tile_at(NT - 1))
            stage_two_copies(tile_at(NT - 1))

        @block.vector
        def _(dve):
            dve.sem_inc(S["qrT_copied"], 1)
            dve.sem_inc(S["krT_copied"], 1)
            half = RD // 2

            def rotate(i, src, dst, heads, done):
                shape = [P, heads, half]
                cos = bcast(cos1[:, ds(i, 1), :], shape)
                sin = bcast(sin1[:, ds(i, 1), :], shape)
                a, b = src[:, :, 0:half], src[:, :, half:RD]
                r = ROT[:, 0:heads, :]
                dve.tensor_tensor(dst[:, 0:heads, 0:half], a, cos, ALU.mult)
                dve.tensor_tensor(dst[:, 0:heads, half:RD], b, cos, ALU.mult)
                dve.tensor_tensor(r[:, :, 0:half], b, sin, ALU.mult)
                dve.tensor_tensor(r[:, :, half:RD], a, sin, ALU.mult).then_inc(S["rope_a"], 1)
                return r, dst[:, 0:heads, :]

            def combine(n, r, dst, done):
                dve.wait_ge(S["rope_a"], n)
                dve.tensor_tensor(dst[:, :, 0:half], dst[:, :, 0:half], r[:, :, 0:half], ALU.subtract)
                return dve.tensor_tensor(dst[:, :, half:RD], dst[:, :, half:RD], r[:, :, half:RD], ALU.add).then_inc(S[done], 1)

            def latent_norm(t):
                i, b = t.i, t.b
                dve.wait_ge(S["zstd_ready"], i + 1)
                dve.reciprocal(zrstd[b][:], zstd[b][:]).then_inc(S["zrstd_ready"], 1)
                dve.wait_ge(S["zrstd_ready"], i + 1)
                dve.tensor_scalar(Z[b][:, 0:QR], Z[b][:, 0:QR], zrstd[b][:, 0:1], None, ALU.mult)
                dve.tensor_scalar(Z[b][:, QR:QR + KVR], Z[b][:, QR:QR + KVR], zrstd[b][:, 1:2], None, ALU.mult).then_inc(S["zn_ready"], 1)
                if not t.first:
                    dve.wait_ge(S["krT_ps"], i)
                src = Z[b][:, QR + KVR:ZC].unsqueeze(1)
                r, d = rotate(i, src, KRO, 1, None)
                combine(2 * i + 1, r, d, "rope_b")
                dve.wait_ge(S["rope_b"], i + 1)
                dve.tensor_scalar(KRO[:, 1, :], KRO[:, 0, :], 1.0, None, ALU.mult).then_inc(S["krope_ready"], 1)

            def query_rope(t):
                i, b = t.i, t.b
                dve.wait_ge(S["qr_ps"], i + 1)
                if not t.first:
                    dve.wait_ge(S["qrT_ps"], i)
                r, d = rotate(i, pE[:, 0:H1 * RD].rearrange("p (h d) -> p h d", h=H1), QRO, H1, None)
                combine(2 * i + 2, r, d, "qrope_ready")

            def rope_copies(t):
                i, b = t.i, t.b
                dve.wait_ge(stored_2[b], 80 * t.n + 80)
                dve.wait_ge(S["qrT_ps"], i + 1)
                dve.tensor_copy(QRT[b][:].rearrange("p h t -> p (h t)"), pF[:, 0:2 * P]).then_inc(S["qrT_copied"], 1)
                dve.wait_ge(S["krT_ps"], i + 1)
                dve.tensor_copy(KRT[b][:], pE[:, 0:P]).then_inc(S["krT_copied"], 1)

            def tile(t):
                i, b = t.i, t.b
                dve.wait_ge(S["std_ready"], i + 1)
                dve.reciprocal(rstd[b][:], std[b][:]).then_inc(S["rstd_ready"], 1)
                dve.wait_ge(S["rstd_ready"], i + 1)
                dve.tensor_scalar(X[b][:], X[b][:], rstd[b][:], None, ALU.mult).then_inc(S["h_ready"], 1)
                if not t.first:
                    latent_norm(t.before())
                dve.wait_ge(S["mmA"], i + 1)
                dve.tensor_copy(Z[b][:], pA[:, 0:ZC]).then_inc(S["z_ready"], 1)
                if not t.first:
                    query_rope(t.before())
                dve.wait_ge(S["mmC"], i + 1)
                for m in range(SM):
                    out = U[:, m, :, ds(i * (P // T8), P // T8)].rearrange("p t c -> p c t")
                    src = pC[:, m * P:(m + 1) * P].rearrange("p (c t) -> p c t", t=T8)
                    d = dve.tensor_scalar(out, src, 1.0, None, ALU.mult)
                d.then_inc(S["u_copied"], 1)
                if not t.first:
                    rope_copies(t.before())

            tiles(dve, NT, tile)
            latent_norm(tile_at(NT - 1))
            query_rope(tile_at(NT - 1))
            rope_copies(tile_at(NT - 1))


def attention(nc, C, stage, heads, dv, key_tiles, scale, load_keys, loads, load_query, keys, values, out):
    with ExitStack() as ctx:
        k = Kit(nc, ctx, stage)
        nk = key_tiles * P
        groups = [(g, min(4, key_tiles - 4 * g)) for g in range((key_tiles + 3) // 4)]
        banks = len(groups)
        parts, query_dmas, load_kv = load_keys(k)
        Q = [k.sb(f"Q{h}", [P, parts, P]) for h in range(heads)]
        PR = [k.sb(f"PR{b}", [P, nk]) for b in range(2)]
        PT = k.sb("PT", [P, key_tiles, P])
        OB = [k.sb(f"OB{b}", [P, heads * dv]) for b in range(2)]
        top, bias, total, inverse = ([k.sb(f"{n}{b}", [P, 1]) for b in range(2)] for n in ("top", "bias", "total", "inverse"))
        sums = [k.sb(f"sums{b}", [P, banks]) for b in range(2)]
        pS = k.ps("pS", (P, banks, BANK))
        pT = [k.ps(f"pT{b}") for b in range(2)]
        pO = k.ps("pO")
        names = """kv_loaded q_cleared s_ps maxima_ready top_ready bias_ready p_ready t_ps act_moved dve_moved o_ps total_ready
            inverse_ready o_ready sp_turn""".split()
        S = {n: k.sem(n) for n in names}
        q_loaded = [k.sem(f"q_loaded{h}") for h in range(heads)]
        stored = [k.sem(f"stored{b}") for b in range(2)]
        act_moves, dve_moves = [2, 3], [g for g in range(banks) if g not in (2, 3)]
        maxima = [k.sb(f"maxima{b}", [P, banks]) for b in range(2)]
        block = ctx.enter_context(nc.Block())

        def unit(t, h):
            return t.i * heads + h

        def before(t, h):
            return (t, h - 1) if h else (t.before(), heads - 1)

        @block.sync
        def _(sp):
            def wait(sem, value):
                sp.wait_ge(sem, value)
                sp.sem_inc(S["sp_turn"], 1)

            for b in range(2):
                sp.sem_inc(stored[b], 16)
            sp.wait_ge(S["q_cleared"], 1)
            for h in range(heads):
                load_query(sp, Q[h], h, ds(0, P), q_loaded[h])
            loads = load_kv(sp, S["kv_loaded"])

            def tile(t):
                if not (isinstance(t.i, int) and t.i == NT - 1):
                    for h in range(heads):
                        wait(S["s_ps"], (unit(t, h) + 1) * banks)
                        load_query(sp, Q[h], h, ds((t.i + 1) * P, P), q_loaded[h])
                if not t.first:
                    store(t.before())

            def store(t):
                wait(S["o_ready"], (t.i + 1) * heads)
                sp.dma_start(out[t.tokens(), :], OB[t.b][:]).then_inc(stored[t.b], 16)

            tiles(sp, NT, tile)
            store(tile_at(NT - 1))
            for b in range(2):
                sp.wait_ge(stored[b], 16 + 16 * (NT // 2))

        @block.gpsimd
        def _(pool):
            if query_dmas[1]:
                for h in range(heads):
                    last = pool.memset(Q[h][:], 0.0)
                last.then_inc(S["q_cleared"], 1)
            else:
                pool.sem_inc(S["q_cleared"], 1)

        @block.tensor
        def _(pe):
            def scores(t, h, g):
                u = unit(t, h)
                m = groups[g][1]
                if g == 0:
                    pe.wait_ge(q_loaded[h], 16 * query_dmas[0] * (t.i + 1))
                if not (t.first and h == 0):
                    pe.wait_ge(S["p_ready"], (u - 1) * banks + g + 1)
                for part in range(parts):
                    mm = pe.matmul(pS[:, g, 0:m * P], Q[h][:, part, :], keys(h, part)[:, g * BANK:g * BANK + m * P],
                                   start=part == 0, stop=part == parts - 1)
                mm.then_inc(S["s_ps"], 1)

            def moved(u, g):
                if g in act_moves:
                    pe.wait_ge(S["act_moved"], u * len(act_moves) + act_moves.index(g) + 1)
                else:
                    pe.wait_ge(S["dve_moved"], u * len(dve_moves) + dve_moves.index(g) + 1)

            def turn(t, h, b, g):
                u = unit(t, h)
                pe.wait_ge(S["p_ready"], u * banks + g + 1)
                if g >= 2:
                    moved(u, g - 2)
                for j in range(groups[g][1]):
                    x = PR[b][:, (4 * g + j) * P:(4 * g + j + 1) * P]
                    tr = pe.transpose(pT[g % 2][:, j * P:(j + 1) * P], x, C["ident"][:])
                tr.then_inc(S["t_ps"], 1)

            def apply(t, h, g):
                u = unit(t, h)
                moved(u, g)
                if g == 0 and not (t.first and h == 0):
                    pe.wait_ge(S["o_ready"], u)
                for j in range(groups[g][1]):
                    jj = 4 * g + j
                    mm = pe.matmul(pO[:, 0:dv], PT[:, jj, :], values(h, jj), start=jj == 0, stop=jj == key_tiles - 1)
                if g == banks - 1:
                    mm.then_inc(S["o_ps"], 1)

            between = [[(turn, 0)], [(turn, 1)], [(apply, 0)], [], []][:banks]
            between[-1] = between[-1] + [(turn, 2), (turn, 3), (apply, 1), (apply, 2)] + [(turn, g) for g in range(4, banks)] + \
                [(apply, g) for g in range(3, banks)]

            def of_unit_before(steps, t, h):
                pt, ph = before(t, h)
                for what, g in steps:
                    if what is turn:
                        turn(pt, ph, (h - 1) % 2, g)
                    else:
                        apply(pt, ph, g)

            def tile(t):
                for h in range(heads):
                    for g in range(banks):
                        scores(t, h, g)
                        if not (t.first and h == 0):
                            of_unit_before(between[g], t, h)

            pe.wait_ge(S["kv_loaded"], 16 * loads)
            tiles(pe, NT, tile)
            for steps in between:
                of_unit_before(steps, tile_at(NT), 0)

        @block.scalar
        def _(act):
            def move(t, h):
                u = unit(t, h)
                for g in act_moves:
                    m = groups[g][1]
                    act.wait_ge(S["t_ps"], u * banks + g + 1)
                    act.activation(PT[:, 4 * g:4 * g + m, :].rearrange("p a b -> p (a b)"), pT[g % 2][:, 0:m * P], ACT.Copy).then_inc(S["act_moved"], 1)

            def exps(t, h, b):
                u = unit(t, h)
                act.wait_ge(S["bias_ready"], u + 1)
                if not (t.first and h < 2):
                    act.wait_ge(S["t_ps"], (u - 1) * banks)
                for g, m in groups:
                    act.activation(PR[b][:, g * BANK:g * BANK + m * P], pS[:, g, 0:m * P], ACT.Exp, bias=bias[b][:], scale=scale,
                                   accum_out=sums[b][:, g:g + 1]).then_inc(S["p_ready"], 1)

            def tile(t):
                for h in range(heads):
                    if not (t.first and h == 0):
                        move(*before(t, h))
                    exps(t, h, h % 2)

            tiles(act, NT, tile)
            move(tile_at(NT - 1), heads - 1)

        @block.vector
        def _(dve):
            def maximum(t, h, b, g):
                u = unit(t, h)
                dve.wait_ge(S["s_ps"], u * banks + g + 1)
                dve.tensor_reduce(maxima[b][:, g:g + 1], pS[:, g, 0:groups[g][1] * P], AX_X, ALU.max).then_inc(S["maxima_ready"], 1)

            def top_of(t, h, b):
                u = unit(t, h)
                dve.wait_ge(S["maxima_ready"], (u + 1) * banks)
                dve.tensor_reduce(top[b][:], maxima[b][:], AX_X, ALU.max).then_inc(S["top_ready"], 1)
                dve.wait_ge(S["top_ready"], u + 1)
                dve.tensor_scalar(bias[b][:], top[b][:], -scale, None, ALU.mult).then_inc(S["bias_ready"], 1)

            def move(t, h, g):
                u = unit(t, h)
                m = groups[g][1]
                dve.wait_ge(S["t_ps"], u * banks + g + 1)
                dve.tensor_copy(PT[:, 4 * g:4 * g + m, :].rearrange("p a b -> p (a b)"), pT[g % 2][:, 0:m * P]).then_inc(S["dve_moved"], 1)

            def finish(t, h, b):
                u = unit(t, h)
                dve.wait_ge(S["p_ready"], (u + 1) * banks)
                dve.tensor_reduce(total[b][:], sums[b][:], AX_X, ALU.add).then_inc(S["total_ready"], 1)
                dve.wait_ge(S["total_ready"], u + 1)
                dve.reciprocal(inverse[b][:], total[b][:]).then_inc(S["inverse_ready"], 1)
                dve.wait_ge(S["inverse_ready"], u + 1)
                dve.wait_ge(S["o_ps"], u + 1)
                if h == 0:
                    dve.wait_ge(stored[t.b], 16 * t.n + 16)
                dve.tensor_scalar(OB[t.b][:, h * dv:(h + 1) * dv], pO[:, 0:dv], inverse[b][:], None, ALU.mult).then_inc(S["o_ready"], 1)

            def tile(t):
                for h in range(heads):
                    any_before = not (t.first and h == 0)
                    for g in range(banks):
                        maximum(t, h, h % 2, g)
                        if g < 2 and any_before:
                            move(*before(t, h), g)
                    top_of(t, h, h % 2)
                    if any_before:
                        for g in range(4, banks):
                            move(*before(t, h), g)
                        finish(*before(t, h), (h - 1) % 2)

            tiles(dve, NT, tile)
            for g in dve_moves:
                move(tile_at(NT - 1), heads - 1, g)
            finish(tile_at(NT - 1), heads - 1, 1)


def attention_1(nc, C, D):
    held = {}

    def load_keys(k):
        held["kn"] = k.sb("kn", [P, H1, SEQ])
        held["kr"] = k.sb("kr", [P, SEQ])
        held["v"] = k.sb("v", [P, NT, AW])

        def load(sp, sem):
            sp.dma_start(held["kn"][:], D["kn"].rearrange("(h p) t -> p h t", p=P)).then_inc(sem, 16)
            sp.dma_start(held["kr"][:], D["kr"]).then_inc(sem, 16)
            sp.dma_start(held["v"][:], D["v"].rearrange("(n p) d -> p n d", p=P)).then_inc(sem, 16)
        return 2, (2, True), load

    def load_query(sp, q, h, tok, sem):
        sp.dma_start(q[:, 0, :], D["qn"][h * P:(h + 1) * P, tok]).then_inc(sem, 16)
        sp.dma_start(q[0:RD, 1, :], D["qr"][h * RD:(h + 1) * RD, tok]).then_inc(sem, 16)

    attention(nc, C, "a1", H1, DV, NT, (DN + RD) ** -0.5, load_keys, 3, load_query,
              lambda h, part: held["kr"][:] if part else held["kn"][:, h, :],
              lambda h, j: held["v"][:, j, h * DV:(h + 1) * DV], D["ao"])


GB = 8
DG = 2 * GB


def s5(nc, I, D, C):
    with ExitStack() as ctx:
        k = Kit(nc, ctx, "s5")
        small = {n: k.sb(n, [P, DG]) for n in """lam_re lam_im log_dt dt mag_arg ang mag mag8 kk sin cos lr lr1 li t1 t2 den fr fi
            sin8 cos8 m1 m2""".split()}
        coef_a, coef_b = k.sb("coef_a", [P, 2 * DG]), k.sb("coef_b", [P, 2 * DG])
        raw = {n: k.sb(n, [P, DG, GC]) for n in ("b_v", "b_u", "c_v", "c_u")}
        d_col = k.sb("d_col", [P, GB])
        X = k.sb("X", [P, GB, NCH])
        TV, TU = (k.sb(n, [P, 2 * DG, T8 + 1, GC]) for n in ("TV", "TU"))
        column = {"Bb": 0, "Cf": GB, "Bf": 2 * GB, "Cb": 3 * GB}
        q1, q2, q3, q4 = (k.sb(f"q{n}", [P, 2 * DG, GC]) for n in range(4))
        WB = k.sb("WB", [P, 2 * DG, P])
        KS = k.sb("KS", [GC, DG, P])
        LF, LB, LL = (k.sb(n, [P, GB, P]) for n in ("LF", "LB", "LL"))
        COS, SIN = k.sb("COS", [P, DG, NCH]), k.sb("SIN", [P, DG, NCH])
        R1, R2 = k.sb("R1", [P, DG, NCH]), k.sb("R2", [P, DG, NCH])
        Y = k.sb("Y", [P, GB, NCH])
        pW = [k.ps(f"pW{b}") for b in range(2)]
        pX = [k.ps(f"pX{b}") for b in range(4)]
        pY = [k.ps(f"pY{b}") for b in range(2)]
        names = """loaded x_loaded dt_ready angle_ready reduced sines_ready powers_ready w_ps w_moved k_moved L_dma L_ready s_ps turned
            scanned products_1 products_2 y_ps y_moved y_stored step pool_step""".split()
        S = {n: k.sem(n) for n in names}
        zeroed = k.sem("zeroed")

        with nc.Block() as block:
            @block.gpsimd
            def _(pool):
                pool.memset(LF[:], 0.0)
                pool.memset(LB[:], 0.0).then_inc(zeroed, 1)
                pool.wait_ge(zeroed, 1)

        u_view = D["u"].rearrange("(g c) (t n) -> t c g n", c=GC, t=T8)
        y_view = D["y"].rearrange("(g c) (t n) -> t c g n", c=GC, t=T8)

        with nc.Fori(0, NG // GB) as q:
            with nc.Block() as block:
                @block.sync
                def _(sp):
                    for n in ("lam_re", "lam_im", "log_dt"):
                        sp.dma_start(small[n][:], I[n][:, q, :]).then_inc(S["loaded"], 16)
                    for n in raw:
                        sp.dma_start(raw[n][:], I[n][:, q, :, :]).then_inc(S["loaded"], 16)
                    sp.dma_start(d_col[:], I["d_col"][:, q, :]).then_inc(S["loaded"], 16)
                    for t in range(T8):
                        sp.dma_start(X[t * GC:(t + 1) * GC, :, :], u_view[t, :, ds(q * GB, GB), :]).then_inc(S["x_loaded"], 16)
                    sp.wait_ge(S["loaded"], 128)
                    sp.wait_ge(S["k_moved"], 4)
                    for t in range(T8):
                        rows = slice(t * GC, (t + 1) * GC)
                        sp.dma_start(LF[rows, :, t * GC:P], KS[:, 0:GB, 0:P - t * GC]).then_inc(S["L_dma"], 16)
                        sp.dma_start(LB[rows, :, 0:(t + 1) * GC], KS[:, GB:DG, P - (t + 1) * GC:P]).then_inc(S["L_dma"], 16)
                    sp.wait_ge(S["L_dma"], 256)
                    sp.wait_ge(S["x_loaded"], 128)
                    sp.wait_ge(S["y_moved"], 4)
                    for t in range(T8):
                        sp.dma_start(y_view[t, :, ds(q * GB, GB), :], Y[t * GC:(t + 1) * GC, :, :]).then_inc(S["y_stored"], 16)
                    sp.wait_ge(S["y_stored"], 128)

                @block.vector
                def _(dve):
                    m = {n: small[n][:] for n in small}
                    do = in_turn(dve, S["step"])

                    def tt(out, a, b, op):
                        return do(dve.tensor_tensor(out, a, b, op))

                    dve.wait_ge(S["loaded"], 128)
                    dve.wait_ge(S["dt_ready"], 1)
                    do(dve.tensor_scalar(m["lam_re"], m["lam_re"], -1e-4, None, ALU.min))
                    tt(m["ang"], m["lam_im"], m["dt"], ALU.mult)
                    dve.tensor_tensor(m["mag_arg"], m["lam_re"], m["dt"], ALU.mult).then_inc(S["angle_ready"], 1)
                    reduce_angle(dve, do, m["sin"], m["kk"], m["ang"], False)
                    reduce_angle(dve, do, m["cos"], m["kk"], m["ang"], True)
                    dve.sem_inc(S["reduced"], 1)
                    do(dve.tensor_scalar(raw["b_u"][:], raw["b_u"][:], C["half_sign"][:], None, ALU.mult))
                    F, B = slice(0, GB), slice(GB, DG)

                    def power_0(table, what):
                        at = column[what]
                        return table[:, at:at + GB, 0 if at < DG else T8, :]

                    for what, d in (("Cf", F), ("Cb", B)):
                        do(dve.tensor_scalar(power_0(TV, what), raw["c_v"][:, d], C["half_sign"][:], None, ALU.mult))
                        do(dve.tensor_scalar(power_0(TU, what), raw["c_u"][:, d], -1.0, None, ALU.mult))
                    dve.wait_ge(S["sines_ready"], 1)
                    tt(m["lr"], m["mag"], m["cos"], ALU.mult)
                    tt(m["li"], m["mag"], m["sin"], ALU.mult)
                    do(dve.tensor_scalar(m["lr1"], m["lr"], 1.0, None, ALU.subtract))
                    tt(m["t1"], m["lam_re"], m["lam_re"], ALU.mult)
                    tt(m["t2"], m["lam_im"], m["lam_im"], ALU.mult)
                    tt(m["den"], m["t1"], m["t2"], ALU.add)
                    do(dve.reciprocal(m["den"], m["den"]))
                    tt(m["t1"], m["lr1"], m["lam_re"], ALU.mult)
                    tt(m["t2"], m["li"], m["lam_im"], ALU.mult)
                    tt(m["fr"], m["t1"], m["t2"], ALU.add)
                    tt(m["fr"], m["fr"], m["den"], ALU.mult)
                    tt(m["t1"], m["li"], m["lam_re"], ALU.mult)
                    tt(m["t2"], m["lr1"], m["lam_im"], ALU.mult)
                    tt(m["fi"], m["t1"], m["t2"], ALU.subtract)
                    tt(m["fi"], m["fi"], m["den"], ALU.mult)
                    shape = [P, DG, GC]
                    fr, fi = (bcast(m[n].unsqueeze(2), shape) for n in ("fr", "fi"))
                    a, b = q1[:, 0:DG, :], q2[:, 0:DG, :]
                    tt(a, raw["b_v"][:], fr, ALU.mult)
                    tt(b, raw["b_u"][:], fi, ALU.mult)
                    for what, d in (("Bf", F), ("Bb", B)):
                        tt(power_0(TV, what), a[:, d], b[:, d], ALU.subtract)
                    tt(a, raw["b_u"][:], fr, ALU.mult)
                    tt(b, raw["b_v"][:], fi, ALU.mult)
                    for what, d in (("Bf", F), ("Bb", B)):
                        tt(power_0(TU, what), a[:, d], b[:, d], ALU.add)
                    for what, d, sign in (("Bb", B, 1.0), ("Cf", F, -1.0), ("Bf", F, 1.0), ("Cb", B, -1.0)):
                        at = slice(column[what], column[what] + GB)
                        do(dve.tensor_copy(coef_a[:, at], m["lr"][:, d]))
                        do(dve.tensor_scalar(coef_b[:, at], m["li"][:, d], sign, None, ALU.mult))
                    shape = [P, DG, GC]
                    for n in range(T8):
                        halves = ((slice(0, DG), n, n + 1), (slice(DG, 2 * DG), T8 - n, T8 - n - 1))
                        for cols, old, new in halves:
                            ca, cb = (bcast(x[:, cols].unsqueeze(2), shape) for x in (coef_a, coef_b))
                            dve.tensor_tensor(q1[:, cols], TV[:, cols, old], ca, ALU.mult)
                            dve.tensor_tensor(q2[:, cols], TU[:, cols, old], cb, ALU.mult)
                            dve.tensor_tensor(q3[:, cols], TU[:, cols, old], ca, ALU.mult)
                            last = dve.tensor_tensor(q4[:, cols], TV[:, cols, old], cb, ALU.mult)
                        do(last)
                        for cols, old, new in halves:
                            dve.tensor_tensor(TV[:, cols, new], q1[:, cols], q2[:, cols], ALU.subtract)
                            last = dve.tensor_tensor(TU[:, cols, new], q3[:, cols], q4[:, cols], ALU.add)
                        do(last)
                    dve.sem_inc(S["powers_ready"], 1)
                    c8, s8, m1, m2 = m["cos8"], m["sin8"], m["m1"], m["m2"]
                    def square(c, s):
                        tt(m1, c, c, ALU.mult)
                        tt(m2, s, s, ALU.mult)
                        do(dve.scalar_tensor_tensor(s8, c, 2.0, s, ALU.mult, ALU.mult))
                        tt(c8, m1, m2, ALU.subtract)
                    square(m["cos"], m["sin"])
                    square(c8, s8)
                    square(c8, s8)
                    do(dve.memset(COS[:, :, 0:1], 1.0))
                    do(dve.memset(SIN[:, :, 0:1], 0.0))
                    n = 1
                    while n < NCH:
                        shape = [P, DG, n]
                        c, s = bcast(c8.unsqueeze(2), shape), bcast(s8.unsqueeze(2), shape)
                        cos, sin = COS[:, :, 0:n], SIN[:, :, 0:n]
                        a, b = R1[:, :, 0:n], R1[:, :, n:2 * n]
                        a2, b2 = R2[:, :, 0:n], R2[:, :, n:2 * n]
                        dve.tensor_tensor(a, cos, c, ALU.mult)
                        dve.tensor_tensor(b, sin, s, ALU.mult)
                        dve.tensor_tensor(a2, sin, c, ALU.mult)
                        tt(b2, cos, s, ALU.mult)
                        dve.tensor_tensor(COS[:, :, n:2 * n], a, b, ALU.subtract)
                        tt(SIN[:, :, n:2 * n], a2, b2, ALU.add)
                        n *= 2
                        if n < NCH:
                            square(c8, s8)
                    dve.wait_ge(S["L_dma"], 256)
                    tt(LL[:], LF[:], LB[:], ALU.add)
                    for g in range(GB):
                        d = dve.scalar_tensor_tensor(LL[:, g, :], C["ident"][:], d_col[:, g:g + 1], LL[:, g, :], ALU.mult, ALU.add)
                    d.then_inc(S["L_ready"], 1)
                    for j in range(DG):
                        dve.wait_ge(S["s_ps"], j + 1)
                        dve.tensor_tensor(R1[:, j, :], pX[j % 4][:, 0:NCH], COS[:, j, :], ALU.mult)
                        dve.tensor_tensor(R2[:, j, :], pX[j % 4][:, NCH:2 * NCH], SIN[:, j, :], ALU.mult).then_inc(S["turned"], 1)
                    dve.wait_ge(S["turned"], DG)
                    tt(R1[:], R1[:], R2[:], ALU.add)
                    for j in range(DG):
                        d = dve.tensor_tensor_scan(R2[:, j, :], bcast(m["mag8"][:, j:j + 1], [P, NCH]), R1[:, j, :], 0.0, ALU.mult, ALU.add)
                    d.then_inc(S["scanned"], 1)
                    dve.wait_ge(S["scanned"], 1)
                    dve.tensor_tensor(R1[:], R2[:], COS[:], ALU.mult).then_inc(S["products_1"], 1)

                @block.gpsimd
                def _(pool):
                    pool.wait_ge(S["scanned"], 1)
                    pool.tensor_tensor(SIN[:], R2[:], SIN[:], ALU.mult).then_inc(S["products_2"], 1)

                @block.scalar
                def _(act):
                    act.wait_ge(S["loaded"], 128)
                    act.activation(small["dt"][:], small["log_dt"][:], ACT.Exp).then_inc(S["dt_ready"], 1)
                    act.wait_ge(S["angle_ready"], 1)
                    act.activation(small["mag"][:], small["mag_arg"][:], ACT.Exp)
                    act.activation(small["mag8"][:], small["mag_arg"][:], ACT.Exp, scale=float(T8))
                    act.wait_ge(S["reduced"], 1)
                    act.activation(small["sin"][:], small["sin"][:], ACT.Sin)
                    act.activation(small["cos"][:], small["cos"][:], ACT.Sin).then_inc(S["sines_ready"], 1)
                    for j in range(8):
                        act.wait_ge(S["w_ps"], j + 1)
                        act.activation(WB[:, 4 * j:4 * j + 4, :].rearrange("p a b -> p (a b)"), pW[j % 2][:], ACT.Copy).then_inc(S["w_moved"], 1)
                    for j in range(4):
                        act.wait_ge(S["w_ps"], 8 + j + 1)
                        act.activation(KS[:, 4 * j:4 * j + 4, :].rearrange("p a b -> p (a b)"), pW[j % 2][0:GC, :], ACT.Copy).then_inc(S["k_moved"], 1)
                    for j in range(GB // 2):
                        act.wait_ge(S["y_ps"], j + 1)
                        act.activation(Y[:, 2 * j:2 * j + 2, :].rearrange("p a b -> p (a b)"), pY[j % 2][:], ACT.Copy).then_inc(S["y_moved"], 1)

                @block.tensor
                def _(pe):
                    def eight(table, what, g, late):
                        return table[:, column[what] + g, late:late + T8, :].rearrange("p t c -> p (t c)")

                    pe.wait_ge(S["powers_ready"], 1)
                    for j in range(8):
                        if j >= 2:
                            pe.wait_ge(S["w_moved"], j - 1)
                        for jj in range(4):
                            dg = (4 * j + jj) % DG
                            w = eight((TV, TU)[j // 4], "Bf" if dg < GB else "Bb", dg % GB, dg < GB)
                            w = pe.transpose(pW[j % 2][:, jj * P:(jj + 1) * P], w, C["ident"][:])
                        w.then_inc(S["w_ps"], 1)
                    for j in range(4):
                        if j < 2:
                            pe.wait_ge(S["w_moved"], 7 + j)
                        else:
                            pe.wait_ge(S["k_moved"], j - 1)
                        for jj in range(4):
                            dg = 4 * j + jj
                            f = dg < GB
                            b0 = TV[:, column["Bf"] + dg, T8, :] if f else TV[:, column["Bb"] + dg - GB, 0, :]
                            r = eight(TV, "Cf" if f else "Cb", dg % GB, not f)
                            w = pe.matmul(pW[j % 2][0:GC, jj * P:(jj + 1) * P], b0, r, start=True, stop=True)
                        w.then_inc(S["w_ps"], 1)
                    pe.wait_ge(S["w_moved"], 8)
                    pe.wait_ge(S["x_loaded"], 128)
                    for j in range(DG):
                        if j >= 4:
                            pe.wait_ge(S["turned"], j - 3)
                        x = X[:, j % GB, :] if j < GB else X[:, j % GB, ::-1]
                        pe.matmul(pX[j % 4][:, 0:NCH], WB[:, j, :], x, start=True, stop=True)
                        pe.matmul(pX[j % 4][:, NCH:2 * NCH], WB[:, DG + j, :], x, start=True, stop=True).then_inc(S["s_ps"], 1)
                    pe.wait_ge(S["L_ready"], 1)
                    pe.wait_ge(S["products_1"], 1)
                    pe.wait_ge(S["products_2"], 1)
                    for g in range(GB):
                        if g % 2 == 0 and g >= 4:
                            pe.wait_ge(S["y_moved"], g // 2 - 1)
                        y = pY[g // 2 % 2][:, (g % 2) * NCH:(g % 2 + 1) * NCH]
                        pe.matmul(y, LL[:, g, :], X[:, g, :], start=True, stop=False)
                        pe.matmul(y[:, 1:NCH], eight(TV, "Cf", g, True), R1[:, g, 0:NCH - 1], start=False, stop=False)
                        pe.matmul(y[:, 1:NCH], eight(TU, "Cf", g, True), SIN[:, g, 0:NCH - 1], start=False, stop=False)
                        pe.matmul(y[:, 0:NCH - 1], eight(TV, "Cb", g, False), R1[:, GB + g, NCH - 2::-1], start=False, stop=False)
                        mm = pe.matmul(y[:, 0:NCH - 1], eight(TU, "Cb", g, False), SIN[:, GB + g, NCH - 2::-1], start=False, stop=True)
                        if g % 2:
                            mm.then_inc(S["y_ps"], 1)

            with nc.Block() as block:
                @block.sync
                def _(sp):
                    for s in S.values():
                        sp.sem_clear(s)


def waiting_sp(sp, turn):
    def wait(sem, value):
        sp.wait_ge(sem, value)
        sp.sem_inc(turn, 1)
    return wait


def mix_1(nc, I, D, C):
    with ExitStack() as ctx:
        k = Kit(nc, ctx, "m1")
        w_out = k.sb("w_out", [P, KC, DM])
        w_glu = k.sb("w_glu", [P, SM, SW])
        out_g, b_glu, half_b = k.sb("out_g", [P, KC]), k.sb("b_glu", [P, SM]), k.sb("half_b", [P, SM])
        post_g = k.sb("post_g", [P, DM])
        YS = k.sb("YS", [P, SM, T8, NCH])
        eps4, eps16 = k.sb("eps4", [P, 1]), k.sb("eps16", [P, 1])
        XT = [k.sb(f"XT{b}", [P, DM]) for b in range(2)]
        AO = [k.sb(f"AO{b}", [P, AW]) for b in range(2)]
        GA = [k.sb(f"GA{b}", [P, AW]) for b in range(2)]
        GS = [k.sb(f"GS{b}", [P, SM, P]) for b in range(2)]
        CA = [k.sb(f"CA{b}", [P, SM, P]) for b in range(2)]
        CS = [k.sb(f"CS{b}", [P, SM, P]) for b in range(2)]
        X1 = [k.sb(f"X1{b}", [P, DM]) for b in range(2)]
        yt, yh, y2, th, v, th2, a, sq, thg, tha, junk = (k.sb(n, [P, SM, P]) for n in "yt yh y2 th v th2 a sq thg tha junk".split())
        junk2 = k.sb("junk2", [P, DM])
        r2 = k.sb("r2", [P, P])
        sd2 = k.sb("sd2", [P, P])
        ss_a, sd_a, r_a = (k.sb(n, [P, 1]) for n in ("ss_a", "sd_a", "r_a"))
        ss_m, ss_mt, sd_m, r_m = (k.sb(n, [P, w]) for n, w in (("ss_m", 2), ("ss_mt", 1), ("sd_m", 1), ("r_m", 1)))
        pG, pN, pTr = k.ps("pG"), k.ps("pN"), k.ps("pTr")
        pM = k.ps("pM", (P, 2, BANK))
        names = """weights_loaded folded y_loaded turn yt_ready inner_ready tanh_gelu v_ready glu_ps tanh_glu a_ready sq_ready norm_ps
            tanh_gates ssq_a std_ready std_n rs_ready cs_ready av_ready at_ps ca_ready m_ps ssm_ready sum_m std_m rm_ready tmp_ready
            x1_ready step""".split()
        S = {n: k.sem(n) for n in names}
        loaded, x_loaded, stored = ([k.sem(f"{n}{b}") for b in range(2)] for n in ("loaded", "x_loaded", "stored"))
        block = ctx.enter_context(nc.Block())
        flat = lambda t: t[:].rearrange("p a b -> p (a b)")

        @block.sync
        def _(sp):
            wait = waiting_sp(sp, S["turn"])
            for b in range(2):
                sp.sem_inc(stored[b], 16)

            def load(t):
                tok, b = t.tokens(), t.b
                sp.dma_start(AO[b][:], D["ao"][tok, :]).then_inc(loaded[b], 16)
                sp.dma_start(GA[b][:], D["ga"][tok, :]).then_inc(loaded[b], 16)
                sp.dma_start(GS[b][:], D["gs"].rearrange("(m p) t -> p m t", p=P)[:, :, tok]).then_inc(loaded[b], 16)

            def load_x(t):
                sp.dma_start(XT[t.b][:], I["x"][t.tokens(), :]).then_inc(x_loaded[t.b], 16)

            sp.dma_start(YS[:].rearrange("p m t c -> p m (t c)"), D["y"].rearrange("(m p) n -> p m n", p=P)).then_inc(S["y_loaded"], 16)
            load(tile_at(0))
            load_x(tile_at(0))
            load(tile_at(1))
            load_x(tile_at(1))
            for dst, src in ((b_glu, "b_glu"), (out_g, "out_g"), (post_g, "post_g")):
                sp.dma_start(dst[:], I[src]).then_inc(S["weights_loaded"], 16)
            sp.dma_start(w_glu[:], I["w_glu"].rearrange("(k p) n -> p k n", p=P)).then_inc(S["weights_loaded"], 16)
            sp.dma_start(w_out[:], I["w_out"].rearrange("(k p) n -> p k n", p=P)).then_inc(S["weights_loaded"], 16)

            def store(t):
                wait(S["x1_ready"], t.i + 1)
                sp.dma_start(D["x1"][t.tokens(), :], X1[t.b][:]).then_inc(stored[t.b], 16)

            def tile(t):
                if not t.first:
                    store(t.before())
                    if not (isinstance(t.i, int) and t.i == NT - 1):
                        nxt = Tile(t.i + 1, 1 - t.b, t.n + t.b)
                        load_x(nxt)
                if not (isinstance(t.i, int) and t.i >= NT - 2):
                    wait(S["cs_ready"], t.i + 1)
                    wait(S["av_ready"], t.i + 1)
                    load(Tile(t.i + 2, t.b, t.n + 1))

            tiles(sp, NT, tile, last=3)
            store(tile_at(NT - 1))
            for b in range(2):
                sp.wait_ge(stored[b], 16 + 16 * (NT // 2))

        @block.vector
        def _(dve):
            dve.memset(eps4[:], 4 * EPS)
            dve.memset(eps16[:], 16 * EPS).then_inc(S["step"], 1)
            dve.wait_ge(S["weights_loaded"], 80)
            dve.tensor_scalar(half_b[:], b_glu[:], 0.5, None, ALU.mult)
            for c in range(KC):
                d = dve.tensor_scalar(w_out[:, c, :], w_out[:, c, :], out_g[:, c:c + 1], None, ALU.mult)
            d.then_inc(S["folded"], 1)
            dve.wait_ge(S["y_loaded"], 16)

            def last_stage(t):
                i, b = t.i, t.b
                dve.wait_ge(S["ssm_ready"], i + 1)
                dve.tensor_tensor(ss_mt[:], ss_m[:, 0:1], ss_m[:, 1:2], ALU.add).then_inc(S["sum_m"], 1)
                dve.wait_ge(S["std_m"], i + 1)
                dve.reciprocal(r_m[:], sd_m[:]).then_inc(S["rm_ready"], 1)
                dve.wait_ge(S["rm_ready"], i + 1)
                dve.wait_ge(stored[b], 16 * t.n + 16)
                dve.scalar_tensor_tensor(X1[b][:], pM[:].rearrange("p a b -> p (a b)"), r_m[:], post_g[:], ALU.mult, ALU.mult).then_inc(S["tmp_ready"], 1)
                dve.wait_ge(S["tmp_ready"], i + 1)
                dve.wait_ge(x_loaded[b], 16 * t.n + 16)
                dve.tensor_tensor(X1[b][:], X1[b][:], XT[b][:], ALU.add).then_inc(S["x1_ready"], 1)

            def tile(t):
                i, b = t.i, t.b
                for m in range(SM):
                    src = YS[:, m, :, ds(i * (P // T8), P // T8)].rearrange("p t c -> p c t")
                    d = dve.tensor_scalar(yt[:, m, :].rearrange("p (c t) -> p c t", t=T8), src, 1.0, None, ALU.mult)
                d.then_inc(S["yt_ready"], 1)
                dve.wait_ge(S["yt_ready"], 2 * i + 1)
                dve.tensor_tensor(y2[:], yt[:], yt[:], ALU.mult)
                dve.tensor_scalar(yh[:], yt[:], 0.5, None, ALU.mult).then_inc(S["yt_ready"], 1)
                dve.wait_ge(S["yt_ready"], 2 * i + 2)
                dve.tensor_scalar(y2[:], y2[:], 0.044715, 1.0, ALU.mult, ALU.add).then_inc(S["inner_ready"], 1)
                dve.wait_ge(S["inner_ready"], 2 * i + 1)
                dve.tensor_tensor(y2[:], y2[:], yt[:], ALU.mult).then_inc(S["inner_ready"], 1)
                dve.wait_ge(S["tanh_gelu"], i + 1)
                if not t.first:
                    dve.wait_ge(S["glu_ps"], i)
                dve.scalar_tensor_tensor(v[:], th[:], 1.0, yh[:], ALU.add, ALU.mult).then_inc(S["v_ready"], 1)
                if not t.first:
                    last_stage(t.before())
                dve.wait_ge(S["tanh_gates"], i + 1)
                dve.wait_ge(loaded[b], 48 * t.n + 48)
                dve.scalar_tensor_tensor(thg[:], thg[:], 1.0, GS[b][:], ALU.add, ALU.mult)
                dve.scalar_tensor_tensor(flat(tha), flat(tha), 1.0, GA[b][:], ALU.add, ALU.mult).then_inc(S["step"], 1)
                dve.wait_ge(S["tanh_glu"], i + 1)
                dve.wait_ge(S["v_ready"], i + 1)
                dve.scalar_tensor_tensor(a[:], th2[:], 1.0, v[:], ALU.add, ALU.mult).then_inc(S["a_ready"], 1)
                dve.wait_ge(S["a_ready"], i + 1)
                dve.tensor_tensor(sq[:], a[:], a[:], ALU.mult).then_inc(S["sq_ready"], 1)
                dve.wait_ge(S["step"], 2 * i + 2)
                dve.tensor_tensor(a[:], a[:], thg[:], ALU.mult).then_inc(S["step"], 1)
                dve.wait_ge(S["std_ready"], i + 1)
                dve.reciprocal(r_a[:], sd_a[:]).then_inc(S["rs_ready"], 1)
                dve.wait_ge(S["rs_ready"], 2 * i + 1)
                dve.scalar_tensor_tensor(flat(tha), AO[b][:], r_a[:], flat(tha), ALU.mult, ALU.mult).then_inc(S["av_ready"], 1)
                dve.wait_ge(S["std_n"], i + 1)
                dve.reciprocal(r2[:], sd2[:]).then_inc(S["rs_ready"], 1)
                dve.wait_ge(S["rs_ready"], 2 * i + 2)
                dve.wait_ge(S["step"], 2 * i + 3)
                dve.tensor_tensor(CS[b][:], a[:], bcast(r2[:].unsqueeze(1), [P, SM, P]), ALU.mult).then_inc(S["cs_ready"], 1)

            tiles(dve, NT, tile)
            last_stage(tile_at(NT - 1))

        @block.scalar
        def _(act):
            def last_stage(t):
                act.wait_ge(S["m_ps"], t.i + 1)
                for h in range(2):
                    s = act.activation(junk2[:, h * BANK:(h + 1) * BANK], pM[:, h, :], ACT.Square, accum_out=ss_m[:, h:h + 1])
                s.then_inc(S["ssm_ready"], 1)

            act.wait_ge(S["folded"], 1)

            def tile(t):
                i, b = t.i, t.b
                act.wait_ge(S["inner_ready"], 2 * i + 2)
                act.activation(flat(th), flat(y2), ACT.Tanh, scale=0.7978845608028654).then_inc(S["tanh_gelu"], 1)
                act.wait_ge(loaded[b], 48 * t.n + 48)
                if not t.first:
                    act.wait_ge(S["at_ps"], i)
                act.activation(flat(thg), flat(GS[b]), ACT.Tanh, scale=0.5)
                act.activation(flat(tha), GA[b][:], ACT.Tanh, scale=0.5).then_inc(S["tanh_gates"], 1)
                act.wait_ge(S["glu_ps"], i + 1)
                for m in range(SM):
                    s = act.activation(th2[:, m, :], pG[:, m * P:(m + 1) * P], ACT.Tanh, bias=half_b[:, m:m + 1], scale=0.5)
                s.then_inc(S["tanh_glu"], 1)
                act.activation(flat(junk), AO[b][:], ACT.Square, accum_out=ss_a[:]).then_inc(S["ssq_a"], 1)
                act.wait_ge(S["ssq_a"], i + 1)
                act.activation(sd_a[:], ss_a[:], ACT.Sqrt, bias=eps4[:], scale=4 / AW).then_inc(S["std_ready"], 1)
                if not t.first:
                    last_stage_sqrt(t.before())
                act.wait_ge(S["norm_ps"], i + 1)
                act.activation(sd2[:], pN[:, 0:P], ACT.Sqrt, bias=eps16[:], scale=4 / SW).then_inc(S["std_n"], 1)
                act.wait_ge(S["at_ps"], i + 1)
                act.activation(flat(CA[b]), pTr[:], ACT.Copy).then_inc(S["ca_ready"], 1)

            def last_stage_sqrt(t):
                last_stage(t)
                act.wait_ge(S["sum_m"], t.i + 1)
                act.activation(sd_m[:], ss_mt[:], ACT.Sqrt, bias=C["eps"][:], scale=1 / DM).then_inc(S["std_m"], 1)

            tiles(act, NT, tile)
            last_stage_sqrt(tile_at(NT - 1))

        @block.tensor
        def _(pe):
            def last_stage(t):
                i, b = t.i, t.b
                pe.wait_ge(S["ca_ready"], i + 1)
                pe.wait_ge(S["cs_ready"], i + 1)
                if not t.first:
                    pe.wait_ge(S["tmp_ready"], i)
                for h in range(2):
                    for c in range(KC):
                        src = CA[b][:, c, :] if c < SM else CS[b][:, c - SM, :]
                        mm = pe.matmul(pM[:, h, :], src, w_out[:, c, h * BANK:(h + 1) * BANK], start=c == 0, stop=c == KC - 1)
                mm.then_inc(S["m_ps"], 1)

            pe.wait_ge(S["folded"], 1)

            def tile(t):
                i, b = t.i, t.b
                pe.wait_ge(S["v_ready"], i + 1)
                if not t.first:
                    pe.wait_ge(S["tanh_glu"], i)
                for m in range(SM):
                    for c in range(SM):
                        mm = pe.matmul(pG[:, m * P:(m + 1) * P], w_glu[:, c, m * P:(m + 1) * P], v[:, c, :], start=c == 0, stop=c == SM - 1)
                mm.then_inc(S["glu_ps"], 1)
                if not t.first:
                    last_stage(t.before())
                pe.wait_ge(S["sq_ready"], i + 1)
                for c in range(SM):
                    mm = pe.matmul(pN[:, 0:P], C["ones"][:], sq[:, c, :], start=c == 0, stop=c == SM - 1)
                mm.then_inc(S["norm_ps"], 1)
                pe.wait_ge(S["av_ready"], i + 1)
                if not t.first:
                    pe.wait_ge(S["ca_ready"], i)
                for c in range(SM):
                    tr = pe.transpose(pTr[:, c * P:(c + 1) * P], tha[:, c, :], C["ident"][:])
                tr.then_inc(S["at_ps"], 1)

            tiles(pe, NT, tile)
            last_stage(tile_at(NT - 1))


NMOD = 6


def modulations(nc, I, D, C, M):
    with ExitStack() as ctx:
        k = Kit(nc, ctx, "ada")
        W = [k.sb(f"W{b}", [P, KC, BANK]) for b in range(2)]
        cc, half, cs = (k.sb(n, [P, KC, 2]) for n in ("cc", "half", "cs"))
        csb = k.sb("csb", [P, KC, P])
        b_col, b_row, g12 = k.sb("b_col", [P, NMOD * KC]), k.sb("b_row", [P, 2, DM]), k.sb("g12", [P, 2 * KC])
        G = k.sb("G", [P, 2, DM])
        pc = [k.ps(f"pc{b}") for b in range(2)]
        pr = [k.ps(f"pr{b}") for b in range(2)]
        names = "loaded tanh_done silu cs_ready cols_ps cols_moved rows_ps rows_moved stored gains turn".split()
        S = {n: k.sem(n) for n in names}
        w_loaded = [k.sem(f"w_loaded{b}") for b in range(2)]
        w_used = k.sem("w_used")
        block = ctx.enter_context(nc.Block())
        mod = M["mod"]
        w_view = I["w_ada"].rearrange("(k p) n -> p k n", p=P)

        def parts(eng, part):
            for gate in range(2):
                with eng.Fori(0, 2) as j:
                    part(3 * gate + j, None)
                part(3 * gate + 2, gate)

        @block.sync
        def _(sp):
            wait = waiting_sp(sp, S["turn"])
            for dst, src in ((cc, "c2"), (b_col, "b_ada_col"), (b_row, "b_gates"), (g12, "g12")):
                sp.dma_start(dst[:], I[src]).then_inc(S["loaded"], 16)
            sp.sem_inc(w_used, 2)

            def part(p, gate):
                for b in range(2):
                    wait(w_used, 2 * p + b + 1)
                    sp.dma_start(W[b][:], w_view[:, :, ds(p * DM + b * BANK, BANK)]).then_inc(w_loaded[b], 16)
            parts(sp, part)
            sp.wait_ge(S["rows_moved"], 4)
            sp.dma_start(D["gates"].rearrange("p (a n) -> p a n", a=2), G[:]).then_inc(S["stored"], 16)
            sp.wait_ge(S["stored"], 16)

        @block.scalar
        def _(act):
            act.wait_ge(S["loaded"], 64)
            act.activation(half[:], cc[:], ACT.Tanh, scale=0.5).then_inc(S["tanh_done"], 1)

        @block.tensor
        def _(pe):
            pe.wait_ge(S["cs_ready"], 1)

            def part(p, gate):
                for b in range(2):
                    pe.wait_ge(w_loaded[b], 16 * (p + 1))
                    pe.wait_ge(S["cols_moved"], 2 * p + b + 1)
                    for m in range(4):
                        for c in range(KC):
                            mm = pe.matmul(pc[b][:, 2 * m:2 * m + 2], W[b][:, c, m * P:(m + 1) * P], cs[:, c, :], start=c == 0, stop=c == KC - 1)
                    mm.then_inc(S["cols_ps"], 1)
                    if gate is not None:
                        if gate:
                            pe.wait_ge(S["rows_moved"], b + 1)
                        for c in range(KC):
                            mm = pe.matmul(pr[b][:], csb[:, c, :], W[b][:, c, :], start=c == 0, stop=c == KC - 1)
                        mm.then_inc(S["rows_ps"], 1)
                    pe.drain().then_inc(w_used, 1)
            parts(pe, part)

        @block.vector
        def _(dve):
            dve.sem_inc(S["cols_moved"], 2)
            dve.wait_ge(S["loaded"], 64)
            dve.wait_ge(S["tanh_done"], 1)
            dve.scalar_tensor_tensor(cs[:], half[:], 1.0, cc[:], ALU.add, ALU.mult).then_inc(S["silu"], 1)
            dve.wait_ge(S["silu"], 1)
            dve.tensor_scalar(cs[:], cs[:], 0.5, None, ALU.mult).then_inc(S["silu"], 1)
            dve.wait_ge(S["silu"], 2)
            dve.tensor_copy(csb[:], bcast(cs[:, :, 0:1], [P, KC, P])).then_inc(S["cs_ready"], 1)

            def part(p, gate):
                for b in range(2):
                    dve.wait_ge(S["cols_ps"], 2 * p + b + 1)
                    bias = bcast(b_col[:, ds(p * KC + 4 * b, 4)].unsqueeze(2), [P, 4, 2])
                    out = mod[:, ds(p * KC + 4 * b, 4), :]
                    dve.tensor_tensor(out, pc[b][:, 0:8].rearrange("p (m x) -> p m x", x=2), bias, ALU.add).then_inc(S["cols_moved"], 1)
                    if gate is not None:
                        dve.wait_ge(S["rows_ps"], 2 * gate + b + 1)
                        cols = slice(b * BANK, (b + 1) * BANK)
                        dve.tensor_tensor(G[:, gate, cols], pr[b][:], b_row[:, gate, cols], ALU.add).then_inc(S["rows_moved"], 1)
            parts(dve, part)
            dve.wait_ge(S["cols_moved"], 2 + 2 * NMOD)
            for n, at in ((0, KC), (1, 4 * KC)):
                scale = mod[:, at:at + KC, :]
                dve.tensor_scalar(scale, scale, 1.0, None, ALU.add).then_inc(S["gains"], 1)
                dve.wait_ge(S["gains"], 2 * n + 1)
                g = bcast(g12[:, n * KC:(n + 1) * KC].unsqueeze(2), [P, KC, 2])
                dve.tensor_tensor(scale, scale, g, ALU.mult).then_inc(S["gains"], 1)


HA, HKV, HD = 8, 2, 64
HR, RV = 4, 128
CTX = 256
NC2 = CTX // P
RW = HR * RV
QA, KA, RQ = HA * HD, HKV * HD, HR * HD
PROJ = QA + 2 * KA + 2 * RQ + 2 * RW
BANKS2 = ((0, 512), (512, 1024), (1024, 1280), (1280, 1792), (1792, 2304))


def project_2(nc, I, D, C, M):
    with ExitStack() as ctx:
        k = Kit(nc, ctx, "p2")
        w_in = k.sb("w_in", [P, KC, PROJ])
        gq, gk = k.sb("gq", [P, HD]), k.sb("gk", [P, HD])
        cos, sin = k.sb("cos", [P, NT, HD // 2]), k.sb("sin", [P, NT, HD // 2])
        X = [k.sb(f"X{b}", [P, DM]) for b in range(2)]
        HT = [k.sb(f"HT{b}", [P, KC, P]) for b in range(2)]
        junk = k.sb("junk", [P, DM])
        NH = HA + HKV
        Z = k.sb("Z", [P, NH + 2 * HR, HD])
        ZR = k.sb("ZR", [P, NH + 2 * HR, HD])
        t1, t2 = k.sb("t1", [P, NH + 2 * HR, HD // 2]), k.sb("t2", [P, NH + 2 * HR, HD // 2])
        hss, hsd, hr = (k.sb(n, [P, NH]) for n in ("hss", "hsd", "hr"))
        VA = [k.sb(f"VA{b}", [P, KA]) for b in range(2)]
        VR = [k.sb(f"VR{b}", [P, RW]) for b in range(2)]
        GR = [k.sb(f"GR{b}", [P, RW]) for b in range(2)]
        KR = [k.sb(f"KR{b}", [P, RQ]) for b in range(2)]
        TA = [k.sb(f"TA{b}", [P, 5, P]) for b in range(2)]
        TR = [k.sb(f"TR{b}", [P, 4, P]) for b in range(2)]
        ssq, std, rstd = ([k.sb(f"{n}{b}", [P, 1]) for b in range(2)] for n in ("ssq", "std", "rstd"))
        pT = [k.ps(f"pT{b}") for b in range(2)]
        pZ = [k.ps(f"pZ{b}") for b in range(5)]
        pR = k.ps("pR")
        names = """weights_loaded turn ssq_done std_ready rstd_ready h_ready hT_ps hT_ready z_ps zq_moved zk_moved zr_moved v_moved g_moved
            hss_sq hss_done hsd_ready hr_ready zn_ready rope_ready roped tr_ps tr_moved sq_ready rope_1 rope_2 kr_moved""".split()
        S = {n: k.sem(n) for n in names}
        x_loaded, stored = ([k.sem(f"{n}{b}") for b in range(2)] for n in ("x_loaded", "stored"))
        block = ctx.enter_context(nc.Block())
        NTT = NT + NC2
        STORES = 7

        def tiles2(eng, body):
            tiles(eng, NT, body)
            for i in range(NT, NTT):
                body(tile_at(i))

        def is_ctx(t):
            return isinstance(t.i, int) and t.i >= NT

        @block.sync
        def _(sp):
            wait = waiting_sp(sp, S["turn"])
            for b in range(2):
                sp.sem_inc(stored[b], 16 * STORES)

            def load_x(i, b, ctx_tile=False):
                src = I["ctx"][(i - NT) * P:(i - NT + 1) * P, :] if ctx_tile else D["x1"][ds(i * P, P), :]
                sp.dma_start(X[b][:], src).then_inc(x_loaded[b], 16)

            load_x(0, 0)
            load_x(1, 1)
            for dst, src in ((gq, "gq"), (gk, "gk"), (cos, "cos2"), (sin, "sin2")):
                sp.dma_start(dst[:], I[src]).then_inc(S["weights_loaded"], 16)
            sp.dma_start(w_in[:], I["w_in_2"].rearrange("(k p) n -> p k n", p=P)).then_inc(S["weights_loaded"], 16)

            def store(t):
                tok, b, one = t.tokens(), t.b, S["turn"]
                wait(S["g_moved"], t.i + 1)
                wait(S["v_moved"], t.i + 1)
                wait(S["zk_moved"], t.i + 1)
                sp.dma_start(D["va"][tok, :], VA[b][:]).then_inc(stored[b], 16)
                sp.dma_start(D["vr"][tok, :], VR[b][:]).then_inc(stored[b], 16)
                sp.dma_start(D["gr"][tok, :], GR[b][:]).then_inc(stored[b], 16)
                wait(S["kr_moved"], t.i + 1)
                sp.dma_start(D["krt"][tok, :], KR[b][:]).then_inc(stored[b], 16)
                wait(S["tr_moved"], 3 * t.i + 4)
                sp.dma_start(D["qka"].rearrange("(c p) t -> p c t", p=P)[:, :, tok], TA[b][:]).then_inc(stored[b], 16)
                qk = D["qkr"].rearrange("(c p) t -> p c t", p=P)
                sp.dma_start(qk[:, 0:2, tok], TR[b][:, 0:2, :]).then_inc(stored[b], 16)
                sp.dma_start(qk[:, 2:4, tok], TR[b][:, 2:4, :]).then_inc(stored[b], 16)

            def tile(t):
                if not (isinstance(t.i, int) and t.i >= NTT - 2):
                    wait(S["hT_ps"], 2 * t.i + 2)
                    load_x(t.i + 2, t.b, isinstance(t.i, int) and t.i + 2 >= NT)
                if not t.first:
                    store(t.before())

            tiles(sp, NT, tile, last=3)
            for i in range(NT, NTT):
                tile(tile_at(i))
            store(tile_at(NTT - 1))
            for b in range(2):
                sp.wait_ge(stored[b], 16 * STORES * (NTT // 2 + 1))

        @block.tensor
        def _(pe):
            pe.wait_ge(S["weights_loaded"], 80)

            def turned(t):
                i = t.i
                pe.wait_ge(S["roped"], i + 1)
                for n in range(3):
                    if n == 0:
                        pe.wait_ge(S["tr_moved"], 3 * i + 1)
                    cols = ((0, 4), (4, 5), (5, 9))[n]
                    bank = (pR, pT[0], pT[1])[n]
                    for m in range(*cols):
                        at = (m - cols[0]) * P
                        tr = pe.transpose(bank[:, at:at + P], ZR[:, 2 * m:2 * m + 2, :].rearrange("p h d -> p (h d)"), C["ident"][:])
                    tr.then_inc(S["tr_ps"], 1)

            def tile(t):
                i, b = t.i, t.b
                pe.wait_ge(S["h_ready"], i + 1)
                if not t.first:
                    pe.wait_ge(S["tr_moved"], 3 * i - 2)
                for c in range(KC):
                    tr = pe.transpose(pT[c // 4][:, (c % 4) * P:(c % 4 + 1) * P], X[b][:, c * P:(c + 1) * P], C["ident"][:])
                    if c % 4 == 3:
                        tr.then_inc(S["hT_ps"], 1)
                pe.wait_ge(S["hT_ready"], 2 * i + 2)
                for n, (lo, hi) in enumerate(BANKS2):
                    if not t.first:
                        pe.wait_ge(S[("zq_moved", "zk_moved", "zr_moved", "v_moved", "g_moved")[n]], i)
                    for c in range(KC):
                        mm = pe.matmul(pZ[n][:, 0:hi - lo], HT[b][:, c, :], w_in[:, c, lo:hi], start=c == 0, stop=c == KC - 1)
                    mm.then_inc(S["z_ps"], 1)
                    if n == 2 and not t.first:
                        turned(t.before())

            tiles2(pe, tile)
            turned(tile_at(NTT - 1))

        @block.scalar
        def _(act):
            def tile(t):
                i, b = t.i, t.b
                act.wait_ge(x_loaded[b], 16 * t.n + 16)
                act.activation(junk[:], X[b][:], ACT.Square, accum_out=ssq[b][:]).then_inc(S["ssq_done"], 1)
                act.wait_ge(S["ssq_done"], i + 1)
                act.activation(std[b][:], ssq[b][:], ACT.Sqrt, bias=C["eps"][:], scale=1 / DM).then_inc(S["std_ready"], 1)
                who = 1 if is_ctx(t) else 0
                for half in range(2):
                    act.wait_ge(S["hT_ps"], 2 * i + half + 1)
                    for c in range(4 * half, 4 * half + 4):
                        a = act.activation(HT[b][:, c, :], pT[half][:, (c % 4) * P:(c % 4 + 1) * P], ACT.Identity,
                                           bias=M["mod"][:, c, who:who + 1], scale=M["mod"][:, KC + c, who:who + 1])
                    a.then_inc(S["hT_ready"], 1)
                if not t.first:
                    heads(t.before())
                    moves(t.before())
                act.wait_ge(stored[b], 16 * STORES * (t.n + 1))
                act.wait_ge(S["z_ps"], 5 * i + 4)
                act.activation(VR[b][:], pZ[3][:], ACT.Copy).then_inc(S["v_moved"], 1)
                act.wait_ge(S["z_ps"], 5 * i + 5)
                act.activation(GR[b][:], pZ[4][:], ACT.Copy).then_inc(S["g_moved"], 1)

            def heads(t):
                act.wait_ge(S["hss_done"], t.i + 1)
                act.activation(hsd[:], hss[:], ACT.Sqrt, bias=C["eps"][:], scale=1 / HD).then_inc(S["hsd_ready"], 1)

            def moves(t):
                for n in range(3):
                    act.wait_ge(S["tr_ps"], 3 * t.i + n + 1)
                    dst = (TA[t.b][:, 0:4, :], TA[t.b][:, 4:5, :], TR[t.b][:])[n]
                    width = (4, 1, 4)[n] * P
                    if n == 0:
                        act.wait_ge(stored[t.b], 16 * STORES * (t.n + 1))
                    act.activation(dst.rearrange("p a b -> p (a b)"), (pR, pT[0], pT[1])[n][:, 0:width], ACT.Copy).then_inc(S["tr_moved"], 1)

            act.sem_inc(S["tr_moved"], 1)
            tiles2(act, tile)
            heads(tile_at(NTT - 1))
            moves(tile_at(NTT - 1))

        @block.vector
        def _(dve):
            half = HD // 2

            def tile(t):
                i, b = t.i, t.b
                dve.wait_ge(S["std_ready"], i + 1)
                dve.reciprocal(rstd[b][:], std[b][:]).then_inc(S["rstd_ready"], 1)
                dve.wait_ge(S["rstd_ready"], i + 1)
                dve.tensor_scalar(X[b][:], X[b][:], rstd[b][:], None, ALU.mult).then_inc(S["h_ready"], 1)
                if not t.first:
                    norm_rope(t.before())
                dve.wait_ge(S["z_ps"], 5 * i + 1)
                dve.tensor_copy(Z[:, 0:HA, :].rearrange("p h d -> p (h d)"), pZ[0][:]).then_inc(S["zq_moved"], 1)
                dve.wait_ge(S["z_ps"], 5 * i + 2)
                dve.tensor_copy(Z[:, HA:NH, :].rearrange("p h d -> p (h d)"), pZ[1][:, 0:KA])
                dve.wait_ge(stored[b], 16 * STORES * (t.n + 1))
                dve.tensor_copy(VA[b][:], pZ[1][:, KA:2 * KA])
                dve.tensor_copy(Z[:, NH:NH + HR, :].rearrange("p h d -> p (h d)"), pZ[1][:, 2 * KA:BANK]).then_inc(S["zk_moved"], 1)
                dve.wait_ge(S["z_ps"], 5 * i + 3)
                dve.tensor_copy(Z[:, NH + HR:NH + 2 * HR, :].rearrange("p h d -> p (h d)"), pZ[2][:, 0:RQ]).then_inc(S["zr_moved"], 1)

            def norm_rope(t):
                i, b = t.i, t.b
                dve.wait_ge(S["zr_moved"], i + 1)
                sq = ZR[:, 0:NH, :]
                if not t.first:
                    dve.wait_ge(S["tr_ps"], 3 * i)
                dve.tensor_tensor(sq, Z[:, 0:NH, :], Z[:, 0:NH, :], ALU.mult).then_inc(S["sq_ready"], 1)
                dve.wait_ge(S["sq_ready"], i + 1)
                dve.tensor_reduce(hss[:], sq, AX_X, ALU.add).then_inc(S["hss_done"], 1)
                dve.wait_ge(S["hsd_ready"], i + 1)
                dve.reciprocal(hr[:], hsd[:]).then_inc(S["hr_ready"], 1)
                dve.wait_ge(S["hr_ready"], i + 1)
                dve.tensor_tensor(Z[:, 0:NH, :], Z[:, 0:NH, :], bcast(hr[:].unsqueeze(2), [P, NH, HD]), ALU.mult).then_inc(S["zn_ready"], 1)
                dve.wait_ge(S["zn_ready"], 2 * i + 1)
                dve.tensor_tensor(Z[:, 0:HA, :], Z[:, 0:HA, :], bcast(gq[:].unsqueeze(1), [P, HA, HD]), ALU.mult)
                dve.tensor_tensor(Z[:, HA:NH, :], Z[:, HA:NH, :], bcast(gk[:].unsqueeze(1), [P, HKV, HD]), ALU.mult).then_inc(S["zn_ready"], 1)
                dve.wait_ge(S["zn_ready"], 2 * i + 2)
                all_h = NH + 2 * HR
                z = Z[:].rearrange("p h (d x) -> p h d x", x=2)
                out = ZR[:].rearrange("p h (d x) -> p h d x", x=2)
                if is_ctx(t):
                    dve.tensor_copy(ZR[:], Z[:]).then_inc(S["roped"], 1)
                else:
                    shape = [P, all_h, half]
                    c = bcast(cos[:, ds(i, 1), :], shape)
                    s = bcast(sin[:, ds(i, 1), :], shape)
                    dve.tensor_tensor(out[:, :, :, 0], z[:, :, :, 0], c, ALU.mult)
                    dve.tensor_tensor(out[:, :, :, 1], z[:, :, :, 0], s, ALU.mult)
                    dve.tensor_tensor(t1[:], z[:, :, :, 1], s, ALU.mult)
                    dve.tensor_tensor(t2[:], z[:, :, :, 1], c, ALU.mult).then_inc(S["rope_1"], 1)
                    dve.wait_ge(S["rope_1"], i + 1)
                    dve.tensor_tensor(out[:, :, :, 0], out[:, :, :, 0], t1[:], ALU.subtract)
                    dve.tensor_tensor(out[:, :, :, 1], out[:, :, :, 1], t2[:], ALU.add).then_inc(S["roped"], 1)
                dve.wait_ge(S["roped"], i + 1)
                dve.wait_ge(stored[b], 16 * STORES * (t.n + 1))
                dve.tensor_scalar(KR[b][:], ZR[:, NH + HR:all_h, :].rearrange("p h d -> p (h d)"), 1.0, None, ALU.mult).then_inc(S["kr_moved"], 1)

            tiles2(dve, tile)
            norm_rope(tile_at(NTT - 1))


def attention_2(nc, C, D):
    held = {}
    nk = NT + NC2

    def load_keys(k):
        held["k"] = k.sb("k", [P, nk * P])
        held["v"] = k.sb("v", [P, nk, KA])

        def load(sp, sem):
            sp.dma_start(held["k"][:], D["qka"][QA:QA + KA, :]).then_inc(sem, 16)
            sp.dma_start(held["v"][:], D["va"].rearrange("(n p) d -> p n d", p=P)).then_inc(sem, 16)
        return 1, (1, True), load

    def load_query(sp, q, h, tok, sem):
        at = h // (HA // HKV) * HD
        sp.dma_start(q[at:at + HD, 0, :], D["qka"][h * HD:(h + 1) * HD, tok]).then_inc(sem, 16)

    attention(nc, C, "a2", HA, HD, nk, HD ** -0.5, load_keys, 2, load_query,
              lambda h, part: held["k"][:],
              lambda h, j: held["v"][:, j, h // (HA // HKV) * HD:(h // (HA // HKV) + 1) * HD], D["ao2"])


def retention(nc, I, D, C):
    with ExitStack() as ctx:
        k = Kit(nc, ctx, "r")
        H2 = HD
        expo = k.sb("expo", [P, 5, P])
        ecol = k.sb("ecol", [P, 5])
        dec = k.sb("dec", [P, 3])
        lg, neg, e, l1 = (k.sb(n, [P, 3]) for n in ("lg", "neg", "e", "l1"))
        cols = k.sb("cols", [P, 5])
        DT, DB, XI = (k.sb(n, [P, P]) for n in ("DT", "DB", "XI"))
        Q, K_ = k.sb("Q", [P, SEQ]), k.sb("K", [P, SEQ])
        KT = k.sb("KT", [P, NT + NC2, H2])
        KZ = k.sb("KZ", [P, NT + NC2, 2 * H2])
        V = k.sb("V", [P, NT + NC2, RV])
        G, TG = k.sb("G", [P, NT, RV]), k.sb("TG", [P, NT, RV])
        gn = k.sb("gn", [P, 2, RV])
        UU, SS = k.sb("UU", [P, NT, RV]), k.sb("SS", [P, NT, RV])
        ST = k.sb("ST", [P, NT, P])
        O = k.sb("O", [P, NT, RV])
        stats, aggr = k.sb("stats", [P, NT, 6]), k.sb("aggr", [P, NT, 2])
        sd, rs = k.sb("sd", [P, NT]), k.sb("rs", [P, NT])
        pU = [k.ps(f"pU{b}") for b in range(2)]
        pS = [k.ps(f"pS{b}") for b in range(2)]
        pO = [k.ps(f"pO{b}") for b in range(2)]
        names = """loaded_d loaded_k loaded_q stored neg_ready e_ready l_ready lg_ready exps_ready step kz_ready u_ps u_moved s_ps s_moved o_ps
            o_moved stats_ready std_ready gate_ready qx_ready states_ready out_ready""".split()
        S = {n: k.sem(n) for n in names}
        setup = k.sem("setup")
        with nc.Block() as block:
            @block.sync
            def _(sp):
                sp.dma_start(expo[:], I["ret_expo"]).then_inc(setup, 16)
                sp.dma_start(ecol[:], I["ret_ecol"]).then_inc(setup, 16)
                sp.wait_ge(setup, 32)

            @block.vector
            def _(dve):
                dve.memset(K_[:], 0.0)

        with nc.Fori(0, HR) as h:
            with nc.Block() as block:
                @block.sync
                def _(sp):
                    sp.dma_start(dec[:], I["ret_decay"][:, h, :]).then_inc(S["loaded_d"], 16)
                    sp.dma_start(gn[:], I["ret_gn"][:, h, :, :]).then_inc(S["loaded_d"], 16)
                    sp.dma_start(KT[:], D["krt"].rearrange("(n p) d -> p n d", p=P)[:, :, ds(h * H2, H2)]).then_inc(S["loaded_k"], 16)
                    sp.dma_start(V[:], D["vr"].rearrange("(n p) d -> p n d", p=P)[:, :, ds(h * RV, RV)]).then_inc(S["loaded_k"], 16)
                    for half in range(2):
                        sp.dma_start(Q[half * H2:(half + 1) * H2, :], D["qkr"][ds(h * H2, H2), 0:SEQ]).then_inc(S["loaded_q"], 16)
                    sp.dma_start(K_[0:H2, :], D["qkr"][ds(RQ + h * H2, H2), 0:SEQ]).then_inc(S["loaded_q"], 16)
                    sp.dma_start(G[:], D["gr"].rearrange("(n p) d -> p n d", p=P)[:, 0:NT, ds(h * RV, RV)]).then_inc(S["loaded_q"], 16)
                    sp.wait_ge(S["loaded_d"], 32)
                    sp.wait_ge(S["out_ready"], 1)
                    sp.dma_start(D["ret"].rearrange("(n p) d -> p n d", p=P)[:, :, ds(h * RV, RV)], O[:]).then_inc(S["stored"], 16)
                    sp.wait_ge(S["stored"], 16)

                @block.scalar
                def _(act):
                    act.wait_ge(S["neg_ready"], 1)
                    act.activation(e[:], neg[:], ACT.Exp).then_inc(S["e_ready"], 1)
                    act.wait_ge(S["e_ready"], 1)
                    act.activation(l1[:], e[:], ACT.Ln, bias=C["one"][:]).then_inc(S["l_ready"], 1)
                    act.wait_ge(S["lg_ready"], 1)
                    act.activation(cols[:, 0:2], ecol[:, 0:2], ACT.Exp, scale=lg[:, 0:1])
                    act.activation(cols[:, 2:4], ecol[:, 2:4], ACT.Exp, scale=lg[:, 1:2])
                    act.activation(cols[:, 4:5], ecol[:, 4:5], ACT.Exp, scale=lg[:, 2:3])
                    act.activation(DT[:], expo[:, 0, :], ACT.Exp, scale=lg[:, 0:1])
                    act.activation(DB[:], expo[:, 1, :], ACT.Exp, scale=lg[:, 1:2])
                    act.activation(XI[:], expo[:, 4, :], ACT.Exp, scale=lg[:, 2:3]).then_inc(S["exps_ready"], 1)
                    act.wait_ge(S["loaded_q"], 64)
                    act.activation(TG[:], G[:], ACT.Tanh, scale=0.5).then_inc(S["gate_ready"], 1)
                    for j in range(NT // 4):
                        act.wait_ge(S["o_ps"], j + 1)
                        act.activation(O[:, 4 * j:4 * j + 4, :].rearrange("p a b -> p (a b)"), pO[j % 2][:], ACT.Copy).then_inc(S["o_moved"], 1)
                    act.wait_ge(S["stats_ready"], 1)
                    act.activation(sd[:], aggr[:, :, 1], ACT.Sqrt, bias=C["eps"][:]).then_inc(S["std_ready"], 1)

                @block.vector
                def _(dve):
                    do = in_turn(dve, S["step"])
                    dve.wait_ge(S["loaded_d"], 32)
                    do(dve.tensor_scalar(neg[:], dec[:], -1.0, None, ALU.mult))
                    dve.tensor_tensor(neg[:], neg[:], dec[:], ALU.min).then_inc(S["neg_ready"], 1)
                    dve.wait_ge(S["l_ready"], 1)
                    do(dve.tensor_scalar(lg[:], dec[:], 0.0, None, ALU.min))
                    dve.tensor_tensor(lg[:], lg[:], l1[:], ALU.subtract).then_inc(S["lg_ready"], 1)
                    dve.wait_ge(S["exps_ready"], 1)
                    scale = HD ** -0.5
                    do(dve.tensor_scalar(cols[:, 0:4], cols[:, 0:4], scale, None, ALU.mult))
                    dve.wait_ge(S["loaded_k"], 32)
                    for n0, n1, f, b in ((0, NT, 0, 2), (NT, NT + 1, 1, 2), (NT + 1, NT + 2, 0, 3)):
                        dve.tensor_scalar(KZ[:, n0:n1, 0:H2], KT[:, n0:n1, :], cols[:, f:f + 1], None, ALU.mult)
                        last = dve.tensor_scalar(KZ[:, n0:n1, H2:2 * H2], KT[:, n0:n1, :], cols[:, b:b + 1], None, ALU.mult)
                    last.then_inc(S["kz_ready"], 1)
                    do(dve.scalar_tensor_tensor(DT[:], DT[:], scale, expo[:, 2, :], ALU.mult, ALU.mult))
                    do(dve.scalar_tensor_tensor(DB[:], DB[:], scale, expo[:, 3, :], ALU.mult, ALU.mult))
                    do(dve.tensor_tensor(DT[:], DT[:], DB[:], ALU.add))
                    dve.wait_ge(S["u_ps"], 1)
                    dve.tensor_copy(SS[0:H2, 0, :], pU[0][0:H2, 0:RV])
                    dve.tensor_copy(SS[H2:P, NT - 1, :], pU[0][H2:P, 0:RV]).then_inc(S["u_moved"], 1)
                    for j in range(NT // 4):
                        dve.wait_ge(S["u_ps"], j + 2)
                        dve.tensor_copy(UU[:, 4 * j:4 * j + 4, :].rearrange("p a b -> p (a b)"), pU[(j + 1) % 2][:]).then_inc(S["u_moved"], 1)
                    dve.wait_ge(S["loaded_q"], 64)
                    for j in range(NT // 4):
                        dve.wait_ge(S["s_ps"], j + 1)
                        dve.tensor_tensor(ST[:, 4 * j:4 * j + 4, :], pS[j % 2][:].rearrange("p (a b) -> p a b", a=4),
                                          bcast(DT[:].unsqueeze(1), [P, 4, P]), ALU.mult).then_inc(S["s_moved"], 1)
                    q = Q[:].rearrange("p (n i) -> p n i", i=P)
                    dve.wait_ge(S["s_ps"], NT // 4)
                    dve.tensor_tensor(q, q, bcast(XI[:].unsqueeze(1), [P, NT, P]), ALU.mult).then_inc(S["qx_ready"], 1)
                    dve.wait_ge(S["u_moved"], 5)
                    for n in range(1, NT):
                        m = NT - 1 - n
                        dve.scalar_tensor_tensor(SS[0:H2, n, :], SS[0:H2, n - 1, :], cols[0:H2, 4:5], UU[0:H2, n - 1, :], ALU.mult, ALU.add)
                        do(dve.scalar_tensor_tensor(SS[H2:P, m, :], SS[H2:P, m + 1, :], cols[H2:P, 4:5], UU[H2:P, m + 1, :], ALU.mult, ALU.add))
                    dve.sem_inc(S["states_ready"], 1)
                    dve.wait_ge(S["gate_ready"], 1)
                    do(dve.scalar_tensor_tensor(TG[:], TG[:], 1.0, G[:], ALU.add, ALU.mult))
                    dve.wait_ge(S["o_moved"], NT // 4)
                    for n in range(NT):
                        last = dve.bn_stats(stats[:, n, :], O[:, n, :])
                    do(last)
                    for n in range(NT):
                        last = dve.bn_aggr(aggr[:, n, :], stats[:, n, :])
                    last.then_inc(S["stats_ready"], 1)
                    dve.wait_ge(S["std_ready"], 1)
                    do(dve.reciprocal(rs[:], sd[:]))
                    for n in range(NT):
                        last = dve.tensor_scalar(O[:, n, :], O[:, n, :], aggr[:, n, 0:1], rs[:, n:n + 1], ALU.subtract, ALU.mult)
                    do(last)
                    do(dve.tensor_tensor(O[:], O[:], bcast(gn[:, 0:1, :], [P, NT, RV]), ALU.mult))
                    do(dve.tensor_tensor(O[:], O[:], bcast(gn[:, 1:2, :], [P, NT, RV]), ALU.add))
                    dve.scalar_tensor_tensor(O[:], O[:], 0.5, TG[:], ALU.mult, ALU.mult).then_inc(S["out_ready"], 1)

                @block.tensor
                def _(pe):
                    pe.wait_ge(S["kz_ready"], 1)
                    for c in range(NC2):
                        mm = pe.matmul(pU[0][:, 0:RV], KZ[:, NT + c, :], V[:, NT + c, :], start=c == 0, stop=c == NC2 - 1)
                    mm.then_inc(S["u_ps"], 1)
                    for j in range(NT // 4):
                        if j:
                            pe.wait_ge(S["u_moved"], j)
                        for n in range(4 * j, 4 * j + 4):
                            mm = pe.matmul(pU[(j + 1) % 2][:, n % 4 * RV:(n % 4 + 1) * RV], KZ[:, n, :], V[:, n, :], start=True, stop=True)
                        mm.then_inc(S["u_ps"], 1)
                    pe.wait_ge(S["loaded_q"], 64)
                    for j in range(NT // 4):
                        if j >= 2:
                            pe.wait_ge(S["s_moved"], j - 1)
                        for n in range(4 * j, 4 * j + 4):
                            tok = slice(n * P, (n + 1) * P)
                            mm = pe.matmul(pS[j % 2][:, n % 4 * P:(n % 4 + 1) * P], K_[:, tok], Q[:, tok], start=True, stop=True)
                        mm.then_inc(S["s_ps"], 1)
                    pe.wait_ge(S["qx_ready"], 1)
                    pe.wait_ge(S["states_ready"], 1)
                    for j in range(NT // 4):
                        pe.wait_ge(S["s_moved"], j + 1)
                        if j >= 2:
                            pe.wait_ge(S["o_moved"], j - 1)
                        for n in range(4 * j, 4 * j + 4):
                            o = pO[j % 2][:, n % 4 * RV:(n % 4 + 1) * RV]
                            pe.matmul(o, ST[:, n, :], V[:, n, :], start=True, stop=False)
                            mm = pe.matmul(o, Q[:, n * P:(n + 1) * P], SS[:, n, :], start=False, stop=True)
                        mm.then_inc(S["o_ps"], 1)

            with nc.Block() as block:
                @block.sync
                def _(sp):
                    for s in S.values():
                        sp.sem_clear(s)


NGRP, EPG = 4, 8
NE = NGRP * EPG
DE = 512
NL = NGRP + NE
NB = 2 * SEQ // P + NE
BIG = 1e30


def mix_2(nc, I, D, C, M):
    with ExitStack() as ctx:
        k = Kit(nc, ctx, "m2")
        w_out = k.sb("w_out", [P, KC, DM])
        w_r, b_r, gate = k.sb("w_r", [P, KC, NL]), k.sb("b_r", [P, NL]), k.sb("gate", [P, DM])
        CAT = [k.sb(f"CAT{b}", [P, DM]) for b in range(2)]
        CT = [k.sb(f"CT{b}", [P, KC, P]) for b in range(2)]
        X1 = [k.sb(f"X1{b}", [P, DM]) for b in range(2)]
        X2 = [k.sb(f"X2{b}", [P, DM]) for b in range(2)]
        XH = [k.sb(f"XH{b}", [P, DM]) for b in range(2)]
        HT = k.sb("HT", [P, KC, P])
        junk = k.sb("junk", [P, DM])
        ssq, std, rstd = (k.sb(n, [P, 1]) for n in ("ssq", "std", "rstd"))
        pT = [k.ps(f"pT{b}") for b in range(2)]
        pH = [k.ps(f"pH{b}") for b in range(2)]
        pM, pL = k.ps("pM", (P, 2, BANK)), k.ps("pL")
        names = """weights_loaded turn ct_ps ct_ready m_ps gated x2_ready ssq_done std_ready rstd_ready xh_ready h_ps h_ready l_ps l_moved""".split()
        S = {n: k.sem(n) for n in names}
        loaded, x_loaded, stored = ([k.sem(f"{n}{b}") for b in range(2)] for n in ("loaded", "x_loaded", "stored"))
        block = ctx.enter_context(nc.Block())

        @block.sync
        def _(sp):
            wait = waiting_sp(sp, S["turn"])
            for b in range(2):
                sp.sem_inc(stored[b], 32)

            def load(t):
                tok, b = t.tokens(), t.b
                sp.dma_start(CAT[b][:, 0:QA], D["ao2"][tok, :]).then_inc(loaded[b], 16)
                sp.dma_start(CAT[b][:, QA:DM], D["ret"][tok, :]).then_inc(loaded[b], 16)

            def load_x(t):
                sp.dma_start(X1[t.b][:], D["x1"][t.tokens(), :]).then_inc(x_loaded[t.b], 16)

            for i in range(2):
                load(tile_at(i))
                load_x(tile_at(i))
            for dst, src in ((w_r, "w_router"), (b_r, "b_router")):
                sp.dma_start(dst[:], I[src]).then_inc(S["weights_loaded"], 16)
            sp.dma_start(gate[:], D["gates"][:, 0:DM]).then_inc(S["weights_loaded"], 16)
            sp.dma_start(w_out[:], I["w_out_2"].rearrange("(k p) n -> p k n", p=P)).then_inc(S["weights_loaded"], 16)

            def store(t):
                wait(S["xh_ready"], t.i + 1)
                sp.dma_start(D["x2"][t.tokens(), :], X2[t.b][:]).then_inc(stored[t.b], 16)
                sp.dma_start(D["h"][t.tokens(), :], XH[t.b][:]).then_inc(stored[t.b], 16)

            def tile(t):
                if not (isinstance(t.i, int) and t.i >= NT - 2):
                    wait(S["ct_ps"], 2 * t.i + 2)
                    load(Tile(t.i + 2, t.b, t.n + 1))
                if not t.first:
                    store(t.before())
                    if not (isinstance(t.i, int) and t.i == NT - 1):
                        load_x(Tile(t.i + 1, 1 - t.b, t.n + t.b))

            tiles(sp, NT, tile, last=3)
            store(tile_at(NT - 1))
            for b in range(2):
                sp.wait_ge(stored[b], 32 + 32 * (NT // 2))

        @block.tensor
        def _(pe):
            pe.wait_ge(S["weights_loaded"], 64)

            def transposed(t):
                pe.wait_ge(S["xh_ready"], t.i + 1)
                if not t.first:
                    pe.wait_ge(S["h_ready"], 2 * t.i)
                for c in range(KC):
                    tr = pe.transpose(pH[c // 4][:, (c % 4) * P:(c % 4 + 1) * P], XH[t.b][:, c * P:(c + 1) * P], C["ident"][:])
                    if c % 4 == 3:
                        tr.then_inc(S["h_ps"], 1)

            def logits(t):
                pe.wait_ge(S["h_ready"], 2 * t.i + 2)
                if not t.first:
                    pe.wait_ge(S["l_moved"], t.i)
                for c in range(KC):
                    mm = pe.matmul(pL[:, 0:NL], HT[:, c, :], w_r[:, c, :], start=c == 0, stop=c == KC - 1)
                mm.then_inc(S["l_ps"], 1)

            def tile(t):
                i, b = t.i, t.b
                pe.wait_ge(loaded[b], 32 * t.n + 32)
                if not t.first:
                    pe.wait_ge(S["ct_ready"], 2 * i)
                for c in range(KC):
                    tr = pe.transpose(pT[c // 4][:, (c % 4) * P:(c % 4 + 1) * P], CAT[b][:, c * P:(c + 1) * P], C["ident"][:])
                    if c % 4 == 3:
                        tr.then_inc(S["ct_ps"], 1)
                if not t.first:
                    transposed(t.before())
                    pe.wait_ge(S["gated"], i)
                pe.wait_ge(S["ct_ready"], 2 * i + 2)
                for h in range(2):
                    for c in range(KC):
                        mm = pe.matmul(pM[:, h, :], CT[b][:, c, :], w_out[:, c, h * BANK:(h + 1) * BANK], start=c == 0, stop=c == KC - 1)
                mm.then_inc(S["m_ps"], 1)
                if not t.first:
                    logits(t.before())

            tiles(pe, NT, tile)
            transposed(tile_at(NT - 1))
            logits(tile_at(NT - 1))

        @block.scalar
        def _(act):
            def modulate(t):
                if not t.first:
                    act.wait_ge(S["l_ps"], t.i)
                for half in range(2):
                    act.wait_ge(S["h_ps"], 2 * t.i + half + 1)
                    for c in range(4 * half, 4 * half + 4):
                        a = act.activation(HT[:, c, :], pH[half][:, (c % 4) * P:(c % 4 + 1) * P], ACT.Identity,
                                           bias=M["mod"][:, 3 * KC + c, 0:1], scale=M["mod"][:, 4 * KC + c, 0:1])
                    a.then_inc(S["h_ready"], 1)

            def tile(t):
                i, b = t.i, t.b
                for half in range(2):
                    act.wait_ge(S["ct_ps"], 2 * i + half + 1)
                    act.activation(CT[b][:, 4 * half:4 * half + 4, :].rearrange("p a b -> p (a b)"), pT[half][:], ACT.Copy).then_inc(S["ct_ready"], 1)
                if not t.first:
                    modulate(t.before())
                act.wait_ge(S["x2_ready"], i + 1)
                act.activation(junk[:], X2[b][:], ACT.Square, accum_out=ssq[:]).then_inc(S["ssq_done"], 1)
                act.wait_ge(S["ssq_done"], i + 1)
                act.activation(std[:], ssq[:], ACT.Sqrt, bias=C["eps"][:], scale=1 / DM).then_inc(S["std_ready"], 1)

            tiles(act, NT, tile)
            modulate(tile_at(NT - 1))

        @block.vector
        def _(dve):
            dve.wait_ge(S["weights_loaded"], 64)

            def tile(t):
                i, b = t.i, t.b
                dve.wait_ge(S["m_ps"], i + 1)
                dve.wait_ge(stored[b], 32 * t.n + 32)
                dve.tensor_tensor(X2[b][:], pM[:].rearrange("p a b -> p (a b)"), gate[:], ALU.mult).then_inc(S["gated"], 1)
                dve.wait_ge(S["gated"], i + 1)
                dve.wait_ge(x_loaded[b], 16 * t.n + 16)
                dve.tensor_tensor(X2[b][:], X2[b][:], X1[b][:], ALU.add).then_inc(S["x2_ready"], 1)
                if not t.first:
                    logits(t.before())
                dve.wait_ge(S["std_ready"], i + 1)
                dve.reciprocal(rstd[:], std[:]).then_inc(S["rstd_ready"], 1)
                dve.wait_ge(S["rstd_ready"], i + 1)
                dve.tensor_scalar(XH[b][:], X2[b][:], rstd[:], None, ALU.mult).then_inc(S["xh_ready"], 1)

            def logits(t):
                dve.wait_ge(S["l_ps"], t.i + 1)
                dve.tensor_tensor(M["logits"][:, ds(t.i, 1), :], pL[:, 0:NL].unsqueeze(1), b_r[:].unsqueeze(1), ALU.add).then_inc(S["l_moved"], 1)

            tiles(dve, NT, tile)
            logits(tile_at(NT - 1))


def dispatch(nc, I, D, C, M):
    with ExitStack() as ctx:
        k = Kit(nc, ctx, "d")
        L = M["logits"]
        gl, el = L[:, :, 0:NGRP], L[:, :, NGRP:NL].rearrange("p t (g e) -> p t g e", g=NGRP)
        g1 = [k.sb(f"g1{n}", [P, NT, NGRP]) for n in range(3)]
        s1 = {n: k.sb(n, [P, NT]) for n in "gmax gsum pg m1 m2 r w den".split()}
        e4 = k.sb("e4", [P, NT, NGRP, EPG])
        sel, sel2, oh1, oh2, tmp8 = (k.sb(n, [P, NT, EPG]) for n in "sel sel2 oh1 oh2 tmp8".split())
        M1, M2, MM = (k.sb(n, [P, NT, NE]) for n in ("M1", "M2", "MM"))
        within, before, place = (k.sb(n, [P, NT, NE]) for n in ("within", "before", "place"))
        rev4, rev8 = k.sb("rev4", [P, NGRP]), k.sb("rev8", [P, EPG])
        mult, blocks_c = k.sb("mult", [P, NE, NT]), k.sb("blocks_c", [P, NB])
        cnt, nblk, last, start = (k.sb(n, [P, NE]) for n in "cnt nblk last start".split())
        cmp_ = k.sb("cmp", [P, NE, NT])
        cmpb = k.sb("cmpb", [P, NB, NE])
        dest = k.sb("dest", [P, 2, NT])
        blk = k.sb("blk", [P, NB])
        upper = k.sb("upper", [P, P])
        token = k.sb("token", [P, NT], I32)
        zero_i = k.sb("zero_i", [P, NB], I32)
        pw, pt = k.ps("pw"), k.ps("pt")
        names = "loaded exp1_in exp1 exp2_in exp2 step chosen ranks zeroed filled placed scattered".split()
        S = {n: k.sem(n) for n in names}
        block = ctx.enter_context(nc.Block())

        @block.sync
        def _(sp):
            for dst, src in ((rev4, "rev4"), (rev8, "rev8"), (mult, "mult"), (blocks_c, "block_numbers"), (upper, "upper"), (token, "token_numbers")):
                sp.dma_start(dst[:], I[src]).then_inc(S["loaded"], 16)
            sp.wait_ge(S["zeroed"], 1)
            sp.dma_start(D["slots"].rearrange("(p b) x -> p (b x)", p=P), zero_i[:]).then_inc(S["filled"], 16)

        @block.scalar
        def _(act):
            act.wait_ge(S["exp1_in"], 1)
            act.activation(g1[0][:], g1[0][:], ACT.Exp).then_inc(S["exp1"], 1)
            act.wait_ge(S["exp2_in"], 1)
            act.activation(s1["r"][:], s1["r"][:], ACT.Exp).then_inc(S["exp2"], 1)

        @block.tensor
        def _(pe):
            pe.wait_ge(S["loaded"], 96)
            pe.wait_ge(S["chosen"], 1)
            m = MM[:].rearrange("p t e -> p (t e)")
            pe.matmul(pw[:], upper[:], m, start=True, stop=True)
            pe.matmul(pt[:], C["ones"][:], m, start=True, stop=True).then_inc(S["ranks"], 1)

        @block.vector
        def _(dve):
            do = in_turn(dve, S["step"])
            tt = lambda out, a, b, op: do(dve.tensor_tensor(out, a, b, op))
            dve.memset(zero_i[:], 0).then_inc(S["zeroed"], 1)
            dve.wait_ge(S["loaded"], 96)

            def first_of(out, values, top, rev, scratch, n):
                shape = [P, NT, n]
                tt(scratch, values, bcast(top.unsqueeze(2), shape), ALU.is_equal)
                tt(scratch, scratch, bcast(rev[:].unsqueeze(1), shape), ALU.mult)
                do(dve.tensor_reduce(s1["w"][:], scratch, AX_X, ALU.max))
                tt(out, scratch, bcast(s1["w"][:].unsqueeze(2), shape), ALU.is_equal)

            gmax = s1["gmax"][:]
            do(dve.tensor_reduce(gmax, gl, AX_X, ALU.max))
            dve.tensor_tensor(g1[0][:], gl, bcast(gmax.unsqueeze(2), [P, NT, NGRP]), ALU.subtract).then_inc(S["exp1_in"], 1)
            first_of(g1[1][:], gl, gmax, rev4, g1[2][:], NGRP)
            dve.wait_ge(S["exp1"], 1)
            do(dve.tensor_reduce(s1["gsum"][:], g1[0][:], AX_X, ALU.add))
            do(dve.reciprocal(s1["pg"][:], s1["gsum"][:]))
            for g in range(NGRP):
                d = dve.tensor_tensor(e4[:, :, g, :], el[:, :, g, :], bcast(g1[1][:, :, g:g + 1], [P, NT, EPG]), ALU.mult)
            do(d)
            tt(sel[:], e4[:, :, 0, :], e4[:, :, 1, :], ALU.add)
            tt(sel[:], sel[:], e4[:, :, 2, :], ALU.add)
            tt(sel[:], sel[:], e4[:, :, 3, :], ALU.add)
            do(dve.tensor_reduce(s1["m1"][:], sel[:], AX_X, ALU.max))
            first_of(oh1[:], sel[:], s1["m1"][:], rev8, tmp8[:], EPG)
            do(dve.scalar_tensor_tensor(sel2[:], oh1[:], -BIG, sel[:], ALU.mult, ALU.add))
            do(dve.tensor_reduce(s1["m2"][:], sel2[:], AX_X, ALU.max))
            first_of(oh2[:], sel2[:], s1["m2"][:], rev8, tmp8[:], EPG)
            dve.tensor_tensor(s1["r"][:], s1["m2"][:], s1["m1"][:], ALU.subtract).then_inc(S["exp2_in"], 1)
            for oh, m in ((oh1, M1), (oh2, M2)):
                for g in range(NGRP):
                    d = dve.tensor_tensor(m[:, :, g * EPG:(g + 1) * EPG], oh[:], bcast(g1[1][:, :, g:g + 1], [P, NT, EPG]), ALU.mult)
                do(d)
            dve.tensor_tensor(MM[:], M1[:], M2[:], ALU.add).then_inc(S["chosen"], 1)
            dve.wait_ge(S["exp2"], 1)
            do(dve.tensor_scalar(s1["den"][:], s1["r"][:], 1.0, None, ALU.add))
            do(dve.reciprocal(s1["den"][:], s1["den"][:]))
            tt(M["weights"][:, 0, :], s1["pg"][:], s1["den"][:], ALU.mult)
            tt(M["weights"][:, 1, :], M["weights"][:, 0, :], s1["r"][:], ALU.mult)
            dve.wait_ge(S["ranks"], 1)
            do(dve.tensor_copy(within[:].rearrange("p t e -> p (t e)"), pw[:]))
            do(dve.tensor_copy(MM[:].rearrange("p t e -> p (t e)"), pt[:]))
            do(dve.memset(before[:, 0, :], 0.0))
            for t in range(1, NT):
                tt(before[:, t, :], before[:, t - 1, :], MM[:, t - 1, :], ALU.add)
            tt(cnt[:], before[:, NT - 1, :], MM[:, NT - 1, :], ALU.add)
            tt(cmp_[:], bcast(cnt[:].unsqueeze(2), [P, NE, NT]), mult[:], ALU.is_gt)
            do(dve.tensor_reduce(nblk[:], cmp_[:], AX_X, ALU.add))
            do(dve.tensor_tensor_scan(last[:], C["ones"][:, 0:NE], nblk[:], 0.0, ALU.mult, ALU.add))
            tt(start[:], last[:], nblk[:], ALU.subtract)
            tt(cmpb[:], bcast(blocks_c[:].unsqueeze(2), [P, NB, NE]), bcast(last[:].unsqueeze(1), [P, NB, NE]), ALU.is_ge)
            do(dve.tensor_reduce(blk[:], cmpb[:], AX_X, ALU.add))
            do(dve.tensor_scalar(M["block_expert"][:], blk[:], float(NE - 1), None, ALU.min))
            do(dve.tensor_scalar(start[:], start[:], float(P), None, ALU.mult))
            tt(place[:], within[:], before[:], ALU.add)
            tt(place[:], place[:], bcast(start[:].unsqueeze(1), [P, NT, NE]), ALU.add)
            for n, m in ((0, M1), (1, M2)):
                tt(m[:], m[:], place[:], ALU.mult)
                do(dve.tensor_reduce(dest[:, n, :], m[:], AX_X, ALU.add))
            dve.tensor_copy(M["dest"][:], dest[:]).then_inc(S["placed"], 1)

        @block.gpsimd
        def _(pool):
            pool.wait_ge(S["placed"], 1)
            pool.wait_ge(S["filled"], 16)
            pool.wait_ge(S["loaded"], 96)
            for n in range(2):
                for t in range(NT):
                    pool.indirect_dma_start(out=D["slots"], out_offset=bass.IndirectOffsetOnAxis(ap=M["dest"][:, n, t:t + 1], axis=0),
                                            in_=token[:, t:t + 1], in_offset=None).then_inc(S["scattered"], 16)
            pool.wait_ge(S["scattered"], 16 * 2 * NT)


def experts(nc, I, D, C, M):
    with ExitStack() as ctx:
        k = Kit(nc, ctx, "e")
        WG = [k.sb(f"WG{b}", [P, KC, DE]) for b in range(2)]
        WU = [k.sb(f"WU{b}", [P, KC, DE]) for b in range(2)]
        WD = [k.sb(f"WD{b}", [P, DE // P, DM]) for b in range(2)]
        IDX = [k.sb(f"IDX{b}", [P, 1], I32) for b in range(2)]
        XG = [k.sb(f"XG{b}", [P, DM]) for b in range(2)]
        XT = [k.sb(f"XT{b}", [P, KC, P]) for b in range(2)]
        TH = k.sb("TH", [P, DE])
        HH = [k.sb(f"HH{b}", [P, DE // P, P]) for b in range(2)]
        Y = [k.sb(f"Y{b}", [P, DM]) for b in range(2)]
        pT = [k.ps(f"pT{b}") for b in range(2)]
        pG, pU = k.ps("pG"), k.ps("pU")
        pD = k.ps("pD", (P, 2, BANK))
        names = "turn t_ps t_ready g_ps u_ps th_ready silu_ready hh_ready d_ps y_ready pool_turn".split()
        S = {n: k.sem(n) for n in names}
        g_loaded, u_loaded, d_loaded, i_loaded, x_loaded, stored = ([k.sem(f"{n}{b}") for b in range(2)] for n in
                                                                     ("g_loaded", "u_loaded", "d_loaded", "i_loaded", "x_loaded", "stored"))
        block = ctx.enter_context(nc.Block())
        wg = I["moe_w_gate"].rearrange("e (k p) n -> p e k n", p=P)
        wu = I["moe_w_up"].rearrange("e (k p) n -> p e k n", p=P)
        wd = I["moe_w_down"].rearrange("e (k p) n -> p e k n", p=P)

        @block.sync
        def _(sp):
            wait = waiting_sp(sp, S["turn"])
            for b in range(2):
                sp.sem_inc(stored[b], 16)

            def load(t, waits):
                b = t.b
                e = sp.value_load(M["block_expert"][0:1, ds(t.i, 1)], min_val=0, max_val=NE - 1)
                if waits:
                    wait(S["t_ps"], 2 * t.i - 2)
                sp.dma_start(IDX[b][:], D["slots"][ds(t.i * P, P), :]).then_inc(i_loaded[b], 16)
                for W, w, sem, used in ((WG, wg, g_loaded, "g_ps"), (WU, wu, u_loaded, "u_ps"), (WD, wd, d_loaded, "d_ps")):
                    if waits:
                        wait(S[used], t.i - 1)
                    sp.dma_start(W[b][:], w[:, ds(e, 1), :, :].rearrange("p e k n -> p (e k) n")).then_inc(sem[b], 16)

            def store(t):
                wait(S["y_ready"], t.i + 1)
                sp.dma_start(D["yb"][ds(t.i * P, P), :], Y[t.b][:]).then_inc(stored[t.b], 16)

            load(tile_at(0), False)
            load(tile_at(1), False)

            def tile(t):
                if not (isinstance(t.i, int) and t.i >= NB - 2):
                    load(Tile(t.i + 2, t.b, t.n + 1), True)
                store(t)

            tiles(sp, NB, tile, last=3)
            for b in range(2):
                sp.wait_ge(stored[b], 16 + 16 * (NB // 2))

        @block.gpsimd
        def _(pool):
            def tile(t):
                pool.wait_ge(i_loaded[t.b], 16 * t.n + 16)
                pool.sem_inc(S["pool_turn"], 1)
                pool.indirect_dma_start(out=XG[t.b][:], out_offset=None, in_=D["h"],
                                        in_offset=bass.IndirectOffsetOnAxis(ap=IDX[t.b][:, 0:1], axis=0)).then_inc(x_loaded[t.b], 16)

            tiles(pool, NB, tile)

        @block.tensor
        def _(pe):
            def transposed(t):
                pe.wait_ge(x_loaded[t.b], 16 * t.n + 16)
                if not t.first:
                    pe.wait_ge(S["t_ready"], 2 * t.i)
                for c in range(KC):
                    tr = pe.transpose(pT[c // 4][:, (c % 4) * P:(c % 4 + 1) * P], XG[t.b][:, c * P:(c + 1) * P], C["ident"][:])
                    if c % 4 == 3:
                        tr.then_inc(S["t_ps"], 1)

            def wide(t, bank, W, sem, made):
                pe.wait_ge(sem[t.b], 16 * t.n + 16)
                for m in range(DE // P):
                    for c in range(KC):
                        mm = pe.matmul(bank[:, m * P:(m + 1) * P], W[t.b][:, c, m * P:(m + 1) * P], XT[t.b][:, c, :], start=c == 0, stop=c == KC - 1)
                mm.then_inc(S[made], 1)

            def down(t):
                i, b = t.i, t.b
                pe.wait_ge(d_loaded[b], 16 * t.n + 16)
                pe.wait_ge(S["hh_ready"], i + 1)
                if not t.first:
                    pe.wait_ge(S["y_ready"], i)
                for h in range(2):
                    for c in range(DE // P):
                        mm = pe.matmul(pD[:, h, :], HH[b][:, c, :], WD[b][:, c, h * BANK:(h + 1) * BANK], start=c == 0, stop=c == DE // P - 1)
                mm.then_inc(S["d_ps"], 1)

            transposed(tile_at(0))

            def tile(t):
                i = t.i
                pe.wait_ge(S["t_ready"], 2 * i + 2)
                if not t.first:
                    pe.wait_ge(S["silu_ready"], i)
                wide(t, pG, WG, g_loaded, "g_ps")
                if not t.first:
                    down(t.before())
                wide(t, pU, WU, u_loaded, "u_ps")
                if not (isinstance(i, int) and i == NB - 1):
                    transposed(Tile(i + 1, 1 - t.b, t.n + t.b))

            tiles(pe, NB, tile)
            down(tile_at(NB - 1))

        @block.scalar
        def _(act):
            def move(t):
                for half in range(2):
                    act.wait_ge(S["t_ps"], 2 * t.i + half + 1)
                    for c in range(4 * half, 4 * half + 4):
                        a = act.activation(XT[t.b][:, c, :], pT[half][:, (c % 4) * P:(c % 4 + 1) * P], ACT.Identity,
                                           bias=M["mod"][:, 3 * KC + c, 0:1], scale=M["mod"][:, 4 * KC + c, 0:1])
                    a.then_inc(S["t_ready"], 1)

            def results(t):
                act.wait_ge(stored[t.b], 16 * t.n + 16)
                act.wait_ge(S["d_ps"], t.i + 1)
                act.activation(Y[t.b][:], pD[:].rearrange("p a b -> p (a b)"), ACT.Copy).then_inc(S["y_ready"], 1)

            move(tile_at(0))

            def tile(t):
                i = t.i
                act.wait_ge(S["g_ps"], i + 1)
                if not t.first:
                    act.wait_ge(S["silu_ready"], i)
                act.activation(TH[:], pG[:], ACT.Tanh, scale=0.5).then_inc(S["th_ready"], 1)
                if not t.first:
                    results(t.before())
                if not (isinstance(i, int) and i == NB - 1):
                    move(Tile(i + 1, 1 - t.b, t.n + t.b))

            tiles(act, NB, tile)
            results(tile_at(NB - 1))

        @block.vector
        def _(dve):
            def tile(t):
                i, h = t.i, HH[t.b][:].rearrange("p a b -> p (a b)")
                dve.wait_ge(S["th_ready"], i + 1)
                dve.scalar_tensor_tensor(h, TH[:], 1.0, pG[:], ALU.add, ALU.mult).then_inc(S["silu_ready"], 1)
                dve.wait_ge(S["silu_ready"], i + 1)
                dve.wait_ge(S["u_ps"], i + 1)
                dve.scalar_tensor_tensor(h, h, 0.5, pU[:], ALU.mult, ALU.mult).then_inc(S["hh_ready"], 1)

            tiles(dve, NB, tile)


def combine(nc, I, D, C, M, out):
    with ExitStack() as ctx:
        k = Kit(nc, ctx, "c")
        gate, final_g = k.sb("gate", [P, DM]), k.sb("final_g", [P, DM])
        IDX = [k.sb(f"IDX{b}", [P, 2], I32) for b in range(2)]
        WT = [k.sb(f"WT{b}", [P, 2]) for b in range(2)]
        Y1 = [k.sb(f"Y1{b}", [P, DM]) for b in range(2)]
        Y2 = [k.sb(f"Y2{b}", [P, DM]) for b in range(2)]
        X2 = [k.sb(f"X2{b}", [P, DM]) for b in range(2)]
        junk = k.sb("junk", [P, DM])
        ssq, std, rstd = (k.sb(n, [P, 1]) for n in ("ssq", "std", "rstd"))
        names = "loaded_c turn idx_ready pool_turn y1_ready sum_ready step x3_ready ssq_done std_ready rstd_ready out_ready".split()
        S = {n: k.sem(n) for n in names}
        g_loaded, x_loaded, stored = ([k.sem(f"{n}{b}") for b in range(2)] for n in ("g_loaded", "x_loaded", "stored"))
        block = ctx.enter_context(nc.Block())

        @block.sync
        def _(sp):
            wait = waiting_sp(sp, S["turn"])

            def load(t):
                sp.dma_start(X2[t.b][:], D["x2"][t.tokens(), :]).then_inc(x_loaded[t.b], 16)

            sp.dma_start(gate[:], D["gates"][:, DM:2 * DM]).then_inc(S["loaded_c"], 16)
            sp.dma_start(final_g[:], I["final_g"]).then_inc(S["loaded_c"], 16)
            load(tile_at(0))
            load(tile_at(1))
            for b in range(2):
                sp.sem_inc(stored[b], 16)

            def tile(t):
                if not (isinstance(t.i, int) and t.i >= NT - 2):
                    wait(S["x3_ready"], t.i + 1)
                    load(Tile(t.i + 2, t.b, t.n + 1))
                wait(S["out_ready"], t.i + 1)
                sp.dma_start(out[t.tokens(), :], Y1[t.b][:]).then_inc(stored[t.b], 16)

            tiles(sp, NT, tile, last=3)
            for b in range(2):
                sp.wait_ge(stored[b], 16 + 16 * (NT // 2))

        @block.gpsimd
        def _(pool):
            def tile(t):
                pool.wait_ge(S["idx_ready"], t.i + 1)
                pool.wait_ge(stored[t.b], 16 * t.n + 16)
                pool.sem_inc(S["pool_turn"], 1)
                for n, y in ((0, Y1), (1, Y2)):
                    pool.indirect_dma_start(out=y[t.b][:], out_offset=None, in_=D["yb"],
                                            in_offset=bass.IndirectOffsetOnAxis(ap=IDX[t.b][:, n:n + 1], axis=0)).then_inc(g_loaded[t.b], 16)

            tiles(pool, NT, tile)

        @block.scalar
        def _(act):
            act.wait_ge(S["loaded_c"], 32)

            def tile(t):
                i, b = t.i, t.b
                act.wait_ge(g_loaded[b], 32 * t.n + 32)
                act.activation(Y1[b][:], Y1[b][:], ACT.Copy, scale=WT[b][:, 0:1]).then_inc(S["y1_ready"], 1)
                act.wait_ge(S["x3_ready"], i + 1)
                act.activation(junk[:], Y2[b][:], ACT.Square, accum_out=ssq[:]).then_inc(S["ssq_done"], 1)
                act.wait_ge(S["ssq_done"], i + 1)
                act.activation(std[:], ssq[:], ACT.Sqrt, bias=C["eps"][:], scale=1 / DM).then_inc(S["std_ready"], 1)

            tiles(act, NT, tile)

        @block.vector
        def _(dve):
            def indices(t):
                dve.tensor_scalar(IDX[t.b][:].unsqueeze(2), M["dest"][:, :, ds(t.i, 1)], 1.0, None, ALU.mult)
                dve.tensor_scalar(WT[t.b][:].unsqueeze(2), M["weights"][:, :, ds(t.i, 1)], 1.0, None, ALU.mult).then_inc(S["idx_ready"], 1)

            dve.wait_ge(S["loaded_c"], 32)
            indices(tile_at(0))

            def tile(t):
                i, b = t.i, t.b
                if not (isinstance(i, int) and i == NT - 1):
                    indices(Tile(i + 1, 1 - b, t.n + b))
                dve.wait_ge(S["y1_ready"], i + 1)
                dve.scalar_tensor_tensor(Y1[b][:], Y2[b][:], WT[b][:, 1:2], Y1[b][:], ALU.mult, ALU.add).then_inc(S["sum_ready"], 1)
                dve.wait_ge(S["sum_ready"], i + 1)
                dve.tensor_tensor(Y1[b][:], Y1[b][:], gate[:], ALU.mult).then_inc(S["step"], 1)
                dve.wait_ge(S["step"], i + 1)
                dve.wait_ge(x_loaded[b], 16 * t.n + 16)
                dve.tensor_tensor(Y2[b][:], Y1[b][:], X2[b][:], ALU.add).then_inc(S["x3_ready"], 1)
                dve.wait_ge(S["std_ready"], i + 1)
                dve.reciprocal(rstd[:], std[:]).then_inc(S["rstd_ready"], 1)
                dve.wait_ge(S["rstd_ready"], i + 1)
                dve.scalar_tensor_tensor(Y1[b][:], Y2[b][:], rstd[:], final_g[:], ALU.mult, ALU.mult).then_inc(S["out_ready"], 1)

            tiles(dve, NT, tile)


def block_pair_kernel(nc, I, out):
    D = {}
    for name, rows, cols in (
        ("qn", H1 * DN, SEQ), ("kn", H1 * DN, SEQ), ("qr", H1 * RD, SEQ), ("kr", P, SEQ), ("v", SEQ, AW), ("ga", SEQ, AW),
        ("gs", SW, SEQ), ("u", SW, SEQ), ("y", SW, SEQ), ("ao", SEQ, AW), ("x1", SEQ, DM), ("gates", P, 2 * DM),
        ("va", SEQ + CTX, KA), ("vr", SEQ + CTX, RW), ("gr", SEQ + CTX, RW), ("krt", SEQ + CTX, RQ),
        ("qka", QA + KA, SEQ + CTX), ("qkr", 2 * RQ, SEQ + CTX), ("ao2", SEQ, QA), ("ret", SEQ, RW), ("x2", SEQ, DM),
        ("h", SEQ, DM), ("yb", NB * P, DM),
    ):
        D[name] = nc.dram_tensor("between_" + name, [rows, cols], F32, kind="Internal").ap()
    D["slots"] = nc.dram_tensor("between_slots", [NB * P, 1], I32, kind="Internal").ap()
    with ExitStack() as ctx:
        k = Kit(nc, ctx, "all")
        C = {"ident": k.sb("ident", [P, P]), "ones": k.sb("ones", [P, P]), "eps": k.sb("eps", [P, 1]),
             "one": k.sb("one", [P, 1]), "half_sign": k.sb("half_sign", [P, 1])}
        M = {"mod": k.sb("mod", [P, NMOD * KC, 2])}
        loaded = k.sem("loaded")
        with nc.Block() as block:
            @block.sync
            def _(sp):
                sp.dma_start(C["ident"][:], I["ident"]).then_inc(loaded, 16)
                sp.dma_start(C["half_sign"][:], I["half_sign"]).then_inc(loaded, 16)
                sp.wait_ge(loaded, 32)

            @block.vector
            def _(dve):
                dve.memset(C["ones"][:], 1.0)
                dve.memset(C["eps"][:], EPS)
                dve.memset(C["one"][:], 1.0)
        with ExitStack() as rope_ctx:
            r = Kit(nc, rope_ctx, "tables")
            cos1, sin1 = r.sb("cos1", [P, NT, RD // 2]), r.sb("sin1", [P, NT, RD // 2])
            rope_tables(nc, I, cos1, sin1)
            project_1(nc, I, D, C, cos1, sin1)
        attention_1(nc, C, D)
        s5(nc, I, D, C)
        mix_1(nc, I, D, C)
        modulations(nc, I, D, C, M)
        project_2(nc, I, D, C, M)
        attention_2(nc, C, D)
        retention(nc, I, D, C)
        M["logits"] = k.sb("logits", [P, NT, NL])
        M["weights"] = k.sb("weights", [P, 2, NT])
        M["dest"] = k.sb("dest", [P, 2, NT], I32)
        M["block_expert"] = k.sb("block_expert", [P, NB], I32)
        mix_2(nc, I, D, C, M)
        dispatch(nc, I, D, C, M)
        experts(nc, I, D, C, M)
        combine(nc, I, D, C, M, out)


def laid_out(inp):
    c = np.ascontiguousarray
    f = np.float32

    def rows(a):
        return c(a.reshape(-1, P).T)

    def all_partitions(a):
        return c(np.broadcast_to(a, (P,) + a.shape))

    I = {n: c(inp[n][0]) for n in ("x", "w_in", "w_uq", "w_ukv", "w_glu", "w_out")}
    I["positions"] = rows(inp["positions"][0])
    I["pre_g"], I["q_g"], I["kv_g"] = (rows(inp[n][0]) for n in ("pre_norm_g", "q_norm_g", "kv_norm_g"))
    I["b_glu"] = rows(inp["b_glu"][0])
    I["out_g"] = rows(np.concatenate([inp["attn_out_g"][0], inp["ssm_out_g"][0]]))
    I["post_g"] = all_partitions(inp["post_norm_g"][0])

    nb = NG // GB

    def by_state(a):
        a = a.reshape(2, nb, GB, NS).transpose(3, 1, 0, 2).reshape(NS, nb, DG)
        return c(np.concatenate([a, a]))

    def matrices(a):
        return a.reshape(2, nb, GB, NS, GC).transpose(3, 1, 0, 2, 4).reshape(NS, nb, DG, GC)

    I["lam_re"], I["lam_im"] = by_state(inp["s5_lam_re"][0]), by_state(inp["s5_lam_im"][0])
    I["log_dt"] = by_state(np.broadcast_to(inp["s5_log_dt"][0][..., None], (2, NG, NS)))
    br, bi = matrices(inp["s5_b_re"][0]), matrices(inp["s5_b_im"][0])
    cr, ci = (matrices(inp[n][0].transpose(0, 1, 3, 2)) for n in ("s5_c_re", "s5_c_im"))
    I["b_v"], I["b_u"], I["c_v"], I["c_u"] = (c(np.concatenate(p)) for p in ((br, bi), (bi, br), (cr, ci), (ci, cr)))
    d = inp["s5_d"][0].reshape(nb, GB, GC).transpose(2, 0, 1)
    I["d_col"] = c(np.broadcast_to(d[None], (T8, GC, nb, GB)).reshape(P, nb, GB))

    I["ctx"], I["w_ada"] = c(inp["ctx_2"][0]), c(inp["w_ada_2"][0])
    I["c2"] = c(np.stack([rows(inp["c_2"][0]), rows(inp["c_ctx_2"])], 2))
    ba = inp["b_ada_2"][0]
    I["b_ada_col"], I["b_gates"] = rows(ba), all_partitions(ba.reshape(NMOD, DM)[[2, 5]])
    I["g12"] = c(np.concatenate([rows(inp["norm1_g_2"][0]), rows(inp["norm2_g_2"][0])], 1))
    I["w_in_2"], I["w_out_2"] = c(inp["w_in_2"][0]), c(inp["w_out_2"][0])
    I["gq"], I["gk"] = all_partitions(inp["attn_q_norm_2"][0]), all_partitions(inp["attn_k_norm_2"][0])
    dec = np.empty((P, HR, 3), f)
    df, db = inp["ret_decay_fwd_2"][0], inp["ret_decay_bwd_2"][0]
    dec[:, :, 0], dec[:, :, 1], dec[:HD, :, 2], dec[HD:, :, 2] = df, db, df, db
    I["ret_decay"] = dec
    I["ret_gn"] = all_partitions(np.stack([inp["ret_gn_g_2"][0].reshape(HR, RV), inp["ret_gn_b_2"][0].reshape(HR, RV)], 1))
    wr = np.concatenate([inp["moe_w_grp_2"][0], inp["moe_w_exp_2"][0]], 1)
    I["w_router"] = c(wr.reshape(KC, P, NL).transpose(1, 0, 2))
    I["b_router"] = all_partitions(np.concatenate([inp["moe_b_grp_2"][0], inp["moe_b_exp_2"][0]]))
    for n in ("moe_w_gate", "moe_w_up", "moe_w_down"):
        I[n] = c(inp[n + "_2"][0])
    I["final_g"] = all_partitions(inp["final_norm_g_2"])

    I["ident"] = np.eye(P, dtype=f)
    I["half_sign"] = np.repeat(np.array([[1.0], [-1.0]], f), P // 2, 0)
    I["inv_freq"] = all_partitions((f(10000.0) ** (-np.arange(0, RD, 2, dtype=f) / f(RD))).astype(f))
    t = np.arange(SEQ)
    freq = (f(10000.0) ** (-np.arange(0, HD // 2, 2, dtype=f) / f(HD // 2))).astype(f)
    ang = np.concatenate([(t // 64).astype(f)[:, None] * freq, (t % 64).astype(f)[:, None] * freq], 1)
    I["cos2"], I["sin2"] = (c(g(ang).astype(f).reshape(NT, P, HD // 2).transpose(1, 0, 2)) for g in (np.cos, np.sin))
    j, i = np.arange(P, dtype=f)[:, None], np.arange(P, dtype=f)[None]
    cross = np.where(j < HD, i + 1, P - i)
    I["ret_expo"] = c(np.stack([np.maximum(i - j, 0), np.maximum(j - i, 0), i >= j, j > i, cross], 1).astype(f))
    I["ret_ecol"] = c(np.concatenate([P - 1 - j, 2 * P - 1 - j, j, P + j, 0 * j + P], 1).astype(f))
    I["rev4"], I["rev8"] = (all_partitions(np.arange(n, 0, -1, dtype=f)) for n in (NGRP, EPG))
    I["mult"] = c(np.broadcast_to(P * np.arange(NT, dtype=f), (P, NE, NT)))
    I["block_numbers"] = all_partitions(np.arange(NB, dtype=f))
    I["upper"] = (j < i).astype(f)
    I["token_numbers"] = c(np.arange(SEQ, dtype=np.int32).reshape(NT, P).T)
    return I


def kernel(**inputs):
    import concourse.bacc as bacc
    from concourse.bass_utils import run_bass_kernel_spmd

    arrays = laid_out({n: np.asarray(a) for n, a in inputs.items()})
    nc = bacc.Bacc("TRN2", target_bir_lowering=False, num_devices=1)
    I = {n: nc.dram_tensor("in_" + n, a.shape, mybir.dt.from_np(a.dtype), kind="ExternalInput").ap() for n, a in arrays.items()}
    out = nc.dram_tensor("out", [SEQ, DM], F32, kind="ExternalOutput").ap()
    block_pair_kernel(nc, I, out)
    r = run_bass_kernel_spmd(nc, [{"in_" + n: a for n, a in arrays.items()}], core_ids=[0])
    return r.results[0]["out"].reshape(1, SEQ, DM)
```

```python
import math
from contextlib import ExitStack

import numpy as np

import concourse.bass as bass
from concourse import mybir

F32 = mybir.dt.float32
I32 = mybir.dt.int32
F32R = mybir.dt.float32r
ALU = mybir.AluOpType
ACT = mybir.ActivationFunctionType
AX_X = mybir.AxisListType.X
ds = bass.ds

P = 128
BANK = 512
DM = 1024
KC = DM // P
SEQ = 2048
NT = SEQ // P
EPS = 1e-6

QR, KVR, RD = 256, 128, 64
H1, DN, DV = 4, 128, 128
AW = H1 * DV
SW = 512
SM = SW // P
D_IN = QR + KVR + RD + AW + 2 * SW
ZC = QR + KVR + RD
T8 = 8
NCH = SEQ // T8
NG, GC, NS = 32, 16, 64

TWO_PI_A = 6.28125
TWO_PI_B = float(np.float32(np.floor((2 * math.pi - TWO_PI_A) * 2**21) / 2**21))
TWO_PI_C = 2 * math.pi - TWO_PI_A - TWO_PI_B
ROUND = float(1.5 * 2**23)
PI32 = 3.1415925


def bcast(ap, shape):
    return ap.to_broadcast(shape)


class Tile:

    def __init__(self, i, b, n):
        self.i, self.b, self.n, self.first = i, b, n, isinstance(i, int) and i == 0

    def before(self):
        return Tile(self.i - 1, 1 - self.b, self.n if self.b else self.n - 1)

    def tokens(self):
        return ds(self.i * P, P)


def tile_at(i):
    return Tile(i, i % 2, i // 2)


def tiles(eng, n, body, last=1, up=None):
    body(tile_at(0))
    if up:
        up()
    turns = (n - 1 - last) // 2
    assert 1 + 2 * turns + last == n
    with eng.Fori(0, turns) as j:
        body(Tile(2 * j + 1, 1, j))
        body(Tile(2 * j + 2, 0, j + 1))
    for i in range(n - last, n):
        body(tile_at(i))


def tiles_in_use(eng, n, in_use, body, skipped):
    body(tile_at(0))
    used = eng.value_load(in_use, min_val=1, max_val=n)
    with eng.Fori(0, (n - 4) // 2) as j:
        with eng.If(2 * j < used):
            body(Tile(2 * j + 1, 1, j))
            body(Tile(2 * j + 2, 0, j + 1))
        with eng.Else():
            skipped(Tile(2 * j + 1, 1, j))
            skipped(Tile(2 * j + 2, 0, j + 1))
    for i in range(n - 3, n):
        body(tile_at(i))


class Kit:

    def __init__(self, nc, ctx, stage):
        self.nc, self.ctx, self.stage, self.sems = nc, ctx, stage, []
        ctx.callback(self.release)

    def release(self):
        if not self.sems:
            return
        with self.nc.Block() as block:
            @block.sync
            def _(sp):
                for sem in self.sems:
                    sp.sem_clear(sem)
        for sem in self.sems:
            self.nc.release_semaphore(sem)

    def sb(self, name, shape, dt=F32):
        return self.ctx.enter_context(self.nc.sbuf_tensor(f"{self.stage}_{name}", shape, dt))

    def ps(self, name, shape=(P, BANK), dt=F32):
        return self.ctx.enter_context(self.nc.psum_tensor(f"{self.stage}_{name}", list(shape), dt))

    def sem(self, name):
        self.sems.append(self.nc.alloc_semaphore(f"{self.stage}_{name}"))
        return self.sems[-1]


def in_turn(eng, sem):
    n = [0]

    def do(ins):
        n[0] += 1
        ins.then_inc(sem, 1)
        eng.wait_ge(sem, n[0])
    return do


def reduce_angle(dve, do, out, k, angle, quarter):
    do(dve.tensor_scalar(k, angle, 1 / (2 * math.pi), 0.25 if quarter else 0.0, ALU.mult, ALU.add))
    do(dve.tensor_scalar(k, k, ROUND, None, ALU.add))
    do(dve.tensor_scalar(k, k, ROUND, None, ALU.subtract))
    do(dve.scalar_tensor_tensor(out, k, -TWO_PI_A, angle, ALU.mult, ALU.add))
    do(dve.scalar_tensor_tensor(out, k, -TWO_PI_B, out, ALU.mult, ALU.add))
    do(dve.scalar_tensor_tensor(out, k, -TWO_PI_C, out, ALU.mult, ALU.add))
    if quarter:
        do(dve.tensor_scalar(out, out, math.pi / 2, None, ALU.add))
    do(dve.tensor_scalar(out, out, PI32, -PI32, ALU.min, ALU.max))


def rope_tables(nc, I, cos1, sin1):
    with ExitStack() as ctx:
        k = Kit(nc, ctx, "rope")
        pos_i = k.sb("pos_i", [P, NT], I32)
        pos_f = k.sb("pos_f", [P, NT])
        freq = k.sb("freq", [P, RD // 2])
        ang = k.sb("rope_ang", [P, NT, RD // 2])
        kk = k.sb("rope_k", [P, NT, RD // 2])
        loaded, step, reduced, done = (k.sem(n) for n in ("pos_loaded", "rope_step", "rope_reduced", "rope_done"))
        block = ctx.enter_context(nc.Block())

        @block.sync
        def _(sp):
            sp.dma_start(pos_i[:], I["positions"]).then_inc(loaded, 16)
            sp.dma_start(freq[:], I["inv_freq"]).then_inc(loaded, 16)

        @block.vector
        def _(dve):
            do = in_turn(dve, step)
            dve.wait_ge(loaded, 32)
            do(dve.tensor_copy(pos_f[:], pos_i[:]))
            shape = [P, NT, RD // 2]
            do(dve.tensor_tensor(ang[:], bcast(pos_f[:].unsqueeze(2), shape), bcast(freq[:].unsqueeze(1), shape), ALU.mult))
            reduce_angle(dve, do, sin1[:], kk[:], ang[:], False)
            reduce_angle(dve, do, cos1[:], kk[:], ang[:], True)
            dve.sem_inc(reduced, 1)

        @block.scalar
        def _(act):
            act.wait_ge(reduced, 1)
            act.activation(sin1[:], sin1[:], ACT.Sin).then_inc(done, 1)
            act.activation(cos1[:], cos1[:], ACT.Sin).then_inc(done, 1)


def project_1(nc, I, D, C, cos1, sin1):
    with ExitStack() as ctx:
        k = Kit(nc, ctx, "p1")
        w_in = k.sb("w_in", [P, KC, D_IN])
        w_uq = k.sb("w_uq", [P, QR // P, H1 * (DN + RD)])
        w_ukv = k.sb("w_ukv", [P, H1 * (DN + DV)])
        pre_g, q_g, kv_g = k.sb("pre_g", [P, KC]), k.sb("q_g", [P, QR // P]), k.sb("kv_g", [P, 1])
        X = [k.sb(f"X{b}", [P, DM]) for b in range(2)]
        square = k.sb("square", [P, DM])
        HT = [k.sb(f"HT{b}", [P, KC, P]) for b in range(2)]
        Z = [k.sb(f"Z{b}", [P, ZC]) for b in range(2)]
        ZT = k.sb("ZT", [P, 3, P])
        GA = [k.sb(f"GA{b}", [P, AW]) for b in range(2)]
        GS = [k.sb(f"GS{b}", [P, SM, P]) for b in range(2)]
        U = k.sb("U", [P, SM, T8, NCH])
        QN = [k.sb(f"QN{b}", [P, H1, P]) for b in range(2)]
        KN = [k.sb(f"KN{b}", [P, H1, P]) for b in range(2)]
        VB = [k.sb(f"VB{b}", [P, AW]) for b in range(2)]
        QRO = k.sb("QRO", [P, H1, RD])
        KRO = k.sb("KRO", [P, 2, RD])
        ROT = k.sb("ROT", [P, H1, RD])
        QRT = [k.sb(f"QRT{b}", [P, 2, P]) for b in range(2)]
        KRT = [k.sb(f"KRT{b}", [P, P]) for b in range(2)]
        ssq, std, rstd = ([k.sb(f"{n}{b}", [P, 1]) for b in range(2)] for n in ("ssq", "std", "rstd"))
        zss, zstd, zrstd = ([k.sb(f"{n}{b}", [P, 2]) for b in range(2)] for n in ("zss", "zstd", "zrstd"))
        pT = [k.ps(f"pT{b}") for b in range(2)]
        pA, pB, pC, pD, pE, pF = (k.ps(f"p{n}") for n in "ABCDEF")
        names = """small_loaded weights_loaded ssq_done std_ready rstd_ready h_ready hT_ps hT_ready mmA mmB mmC mmD
            z_ready ga_copied u_copied gs_copied zss_done zstd_ready zrstd_ready zn_ready znT_ps znT_ready
            qn_ps qn_copied v_ps v_copied kn_ps kn_copied qr_ps rope_a rope_b qrope_ready krope_ready qrT_ps qrT_copied
            krT_ps krT_copied u_stored sp_turn""".split()
        S = {n: k.sem(n) for n in names}
        x_loaded, stored_1, stored_2 = ([k.sem(f"{n}{b}") for b in range(2)] for n in ("x_loaded", "stored_1_", "stored_2_"))
        w_cols = [(0, ZC)] + [(ZC + n * AW, ZC + (n + 1) * AW) for n in range(3)]
        w_loaded = [k.sem(f"w_loaded{n}") for n in range(4)]
        block = ctx.enter_context(nc.Block())

        def is_last(t):
            return isinstance(t.i, int) and t.i == NT - 1

        def after(t):
            return Tile(t.i + 1, 1 - t.b, t.n + t.b)

        @block.sync
        def _(sp):
            def wait(sem, value):
                sp.wait_ge(sem, value)
                sp.sem_inc(S["sp_turn"], 1)

            def load_x(i, b):
                sp.dma_start(X[b][:], I["x"][ds(i * P, P), :]).then_inc(x_loaded[b], 16)

            for b in range(2):
                sp.sem_inc(stored_1[b], 32)
                sp.sem_inc(stored_2[b], 80)
            load_x(0, 0)
            load_x(1, 1)
            for t, s in ((pre_g, "pre_g"), (q_g, "q_g"), (kv_g, "kv_g")):
                sp.dma_start(t[:], I[s]).then_inc(S["small_loaded"], 16)
            w_view = I["w_in"].rearrange("(k p) n -> p k n", p=P)
            for n, (lo, hi) in enumerate(w_cols):
                sp.dma_start(w_in[:, :, lo:hi], w_view[:, :, lo:hi]).then_inc(w_loaded[n], 16)
            sp.dma_start(w_uq[:], I["w_uq"].rearrange("(k p) n -> p k n", p=P)).then_inc(S["weights_loaded"], 16)
            sp.dma_start(w_ukv[:], I["w_ukv"]).then_inc(S["weights_loaded"], 16)

            def store_first(t):
                wait(S["ga_copied"], t.i + 1)
                sp.dma_start(D["ga"][t.tokens(), :], GA[t.b][:]).then_inc(stored_1[t.b], 16)
                wait(S["gs_copied"], t.i + 1)
                sp.dma_start(D["gs"].rearrange("(m p) t -> p m t", p=P)[:, :, t.tokens()], GS[t.b][:]).then_inc(stored_1[t.b], 16)

            def store_second(t):
                tok, b = t.tokens(), t.b
                for ready, credit, dst, src in (
                    ("qn_copied", 0, D["qn"].rearrange("(h p) t -> p h t", p=P)[:, :, tok], QN[b]),
                    ("v_copied", 1, D["v"][tok, :], VB[b]),
                    ("kn_copied", 1, D["kn"].rearrange("(h p) t -> p h t", p=P)[:, :, tok], KN[b]),
                    ("qrT_copied", 1, D["qr"].rearrange("(c p) t -> p c t", p=P)[:, :, tok], QRT[b]),
                    ("krT_copied", 1, D["kr"][:, tok], KRT[b]),
                ):
                    wait(S[ready], t.i + 1 + credit)
                    sp.dma_start(dst, src[:]).then_inc(stored_2[b], 16)

            def tile(t):
                if not (isinstance(t.i, int) and t.i >= NT - 2):
                    wait(S["hT_ps"], 2 * t.i + 2)
                    load_x(t.i + 2, t.b)
                store_first(t)
                if not t.first:
                    store_second(t.before())

            tiles(sp, NT, tile, last=3)
            store_second(tile_at(NT - 1))
            wait(S["u_copied"], NT)
            sp.dma_start(D["u"].rearrange("(m p) n -> p m n", p=P), U[:].rearrange("p m t c -> p m (t c)")).then_inc(S["u_stored"], 16)
            sp.wait_ge(S["u_stored"], 16)
            for b in range(2):
                sp.wait_ge(stored_1[b], 32 + 32 * (NT // 2))
                sp.wait_ge(stored_2[b], 80 + 80 * (NT // 2))

        @block.tensor
        def _(pe):
            def stage_two_a(t):
                i, b = t.i, t.b
                pe.wait_ge(S["zn_ready"], i + 1)
                pe.wait_ge(S["krT_copied"], i + 1)
                for c in range(3):
                    tr = pe.transpose(pE[:, c * P:(c + 1) * P], Z[b][:, c * P:(c + 1) * P], C["ident"][:])
                tr.then_inc(S["znT_ps"], 1)

            def stage_two_b(t):
                i, b = t.i, t.b
                pe.wait_ge(S["znT_ready"], i + 1)
                pe.wait_ge(S["qrT_copied"], i + 1)
                for h in range(H1):
                    for c in range(2):
                        w = w_uq[:, c, h * (DN + RD):h * (DN + RD) + DN]
                        m = pe.matmul(pF[:, h * P:(h + 1) * P], w, ZT[:, c, :], start=c == 0, stop=c == 1)
                m.then_inc(S["qn_ps"], 1)
                kv = w_ukv[:].rearrange("p (h x d) -> p h x d", h=H1, x=2)
                pe.matmul(pT[0][:], ZT[:, 2, :], kv[:, :, 1, :], start=True, stop=True).then_inc(S["v_ps"], 1)
                for h in range(H1):
                    m = pe.matmul(pT[1][:, h * P:(h + 1) * P], kv[:, h, 0, :], ZT[:, 2, :], start=True, stop=True)
                m.then_inc(S["kn_ps"], 1)
                wr = w_uq[:].rearrange("p c (h d) -> p c h d", h=H1)
                for c in range(2):
                    m = pe.matmul(pE[:, 0:H1 * RD], ZT[:, c, :], wr[:, c, :, DN:DN + RD], start=c == 0, stop=c == 1)
                m.then_inc(S["qr_ps"], 1)

            def stage_two_c(t):
                i, b = t.i, t.b
                pe.wait_ge(S["qn_copied"], i + 1)
                pe.wait_ge(S["qrope_ready"], i + 1)
                for c in range(2):
                    tr = pe.transpose(pF[:, c * P:(c + 1) * P], QRO[:, 2 * c:2 * c + 2, :].rearrange("p h d -> p (h d)"), C["ident"][:])
                tr.then_inc(S["qrT_ps"], 1)
                pe.wait_ge(S["krope_ready"], i + 1)
                pe.transpose(pE[:, 0:P], KRO[:].rearrange("p a d -> p (a d)"), C["ident"][:]).then_inc(S["krT_ps"], 1)

            def transposed(t):
                i, b = t.i, t.b
                pe.wait_ge(S["h_ready"], i + 1)
                if not t.first:
                    pe.wait_ge(S["v_copied"], i)
                    pe.wait_ge(S["kn_copied"], i)
                for c in range(KC):
                    tr = pe.transpose(pT[c // 4][:, (c % 4) * P:(c % 4 + 1) * P], X[b][:, c * P:(c + 1) * P], C["ident"][:])
                    if c % 4 == 3:
                        tr.then_inc(S["hT_ps"], 1)

            def tile(t):
                i, b = t.i, t.b
                pe.wait_ge(S["hT_ready"], 2 * i + 2)
                for n, (bank, cols, made, free) in enumerate(((pA, (0, ZC), "mmA", "z_ready"), (pB, (ZC, ZC + AW), "mmB", "ga_copied"))):
                    if t.first:
                        pe.wait_ge(w_loaded[n], 16)
                    else:
                        pe.wait_ge(S[free], i)
                    for c in range(KC):
                        m = pe.matmul(bank[:, 0:cols[1] - cols[0]], HT[b][:, c, :], w_in[:, c, cols[0]:cols[1]], start=c == 0, stop=c == KC - 1)
                    m.then_inc(S[made], 1)
                    if n == 0 and not t.first:
                        stage_two_a(t.before())
                if not t.first:
                    stage_two_b(t.before())
                for n, (bank, col, made, free) in enumerate(((pC, ZC + AW, "mmC", "u_copied"), (pD, ZC + AW + SW, "mmD", "gs_copied"))):
                    if t.first:
                        pe.wait_ge(w_loaded[2 + n], 16)
                    else:
                        pe.wait_ge(S[free], i)
                    for m4 in range(SM):
                        for c in range(KC):
                            w = w_in[:, c, col + m4 * P:col + (m4 + 1) * P]
                            m = pe.matmul(bank[:, m4 * P:(m4 + 1) * P], w, HT[b][:, c, :], start=c == 0, stop=c == KC - 1)
                    m.then_inc(S[made], 1)
                    if n == 0 and not is_last(t):
                        transposed(after(t))
                if not t.first:
                    stage_two_c(t.before())

            transposed(tile_at(0))
            tiles(pe, NT, tile, up=lambda: pe.wait_ge(S["weights_loaded"], 32))
            stage_two_a(tile_at(NT - 1))
            stage_two_b(tile_at(NT - 1))
            stage_two_c(tile_at(NT - 1))

        @block.scalar
        def _(act):
            def latent_stats(t):
                i, b = t.i, t.b
                act.wait_ge(S["z_ready"], i + 1)
                act.activation(square[:, 0:QR], Z[b][:, 0:QR], ACT.Square, accum_out=zss[b][:, 0:1])
                act.activation(square[:, QR:QR + KVR], Z[b][:, QR:QR + KVR], ACT.Square, accum_out=zss[b][:, 1:2]).then_inc(S["zss_done"], 1)
                act.wait_ge(S["zss_done"], i + 1)
                act.activation(zstd[b][:, 0:1], zss[b][:, 0:1], ACT.Sqrt, bias=C["eps"][:], scale=1 / QR)
                act.activation(zstd[b][:, 1:2], zss[b][:, 1:2], ACT.Sqrt, bias=C["eps"][:], scale=1 / KVR).then_inc(S["zstd_ready"], 1)

            def latent_evac(t):
                i, b = t.i, t.b
                act.wait_ge(S["znT_ps"], i + 1)
                for c in range(3):
                    g = q_g[:, c:c + 1] if c < 2 else kv_g[:]
                    a = act.activation(ZT[:, c, :], pE[:, c * P:(c + 1) * P], ACT.Copy, scale=g)
                a.then_inc(S["znT_ready"], 1)

            def stage_two_copies(t):
                i, b = t.i, t.b
                act.wait_ge(stored_2[b], 80 * t.n + 80)
                for bank, dst, made, done in ((pF, QN[b], "qn_ps", "qn_copied"), (pT[0], VB[b], "v_ps", "v_copied"), (pT[1], KN[b], "kn_ps", "kn_copied")):
                    act.wait_ge(S[made], i + 1)
                    out = dst[:] if dst is VB[b] else dst[:].rearrange("p h t -> p (h t)")
                    act.activation(out, bank[:], ACT.Copy).then_inc(S[done], 1)

            def square_sum(t):
                i, b = t.i, t.b
                act.wait_ge(x_loaded[b], 16 * t.n + 16)
                act.activation(square[:], X[b][:], ACT.Square, accum_out=ssq[b][:]).then_inc(S["ssq_done"], 1)
                act.wait_ge(S["ssq_done"], i + 1)
                act.activation(std[b][:], ssq[b][:], ACT.Sqrt, bias=C["eps"][:], scale=1 / DM).then_inc(S["std_ready"], 1)

            def gained(t):
                i, b = t.i, t.b
                for half in range(2):
                    act.wait_ge(S["hT_ps"], 2 * i + half + 1)
                    for c in range(4 * half, 4 * half + 4):
                        a = act.activation(HT[b][:, c, :], pT[half][:, (c % 4) * P:(c % 4 + 1) * P], ACT.Copy, scale=pre_g[:, c:c + 1])
                    a.then_inc(S["hT_ready"], 1)

            def tile(t):
                i, b = t.i, t.b
                if not t.first:
                    latent_stats(t.before())
                if not is_last(t):
                    square_sum(after(t))
                if not t.first:
                    latent_evac(t.before())
                act.wait_ge(stored_1[b], 32 * t.n + 32)
                act.wait_ge(S["mmB"], i + 1)
                act.activation(GA[b][:], pB[:], ACT.Copy).then_inc(S["ga_copied"], 1)
                if not t.first:
                    stage_two_copies(t.before())
                if not is_last(t):
                    gained(after(t))
                act.wait_ge(S["mmD"], i + 1)
                act.activation(GS[b][:].rearrange("p m t -> p (m t)"), pD[:], ACT.Copy).then_inc(S["gs_copied"], 1)

            act.sem_inc(S["v_copied"], 1)
            act.sem_inc(S["kn_copied"], 1)
            square_sum(tile_at(0))
            act.wait_ge(S["small_loaded"], 48)
            gained(tile_at(0))
            tiles(act, NT, tile)
            latent_stats(tile_at(NT - 1))
            latent_evac(tile_at(NT - 1))
            stage_two_copies(tile_at(NT - 1))

        @block.vector
        def _(dve):
            dve.sem_inc(S["qrT_copied"], 1)
            dve.sem_inc(S["krT_copied"], 1)
            half = RD // 2

            def rotate(i, src, dst, heads):
                shape = [P, heads, half]
                cos = bcast(cos1[:, ds(i, 1), :], shape)
                sin = bcast(sin1[:, ds(i, 1), :], shape)
                a, b = src[:, :, 0:half], src[:, :, half:RD]
                r = ROT[:, 0:heads, :]
                dve.tensor_tensor(dst[:, 0:heads, 0:half], a, cos, ALU.mult)
                dve.tensor_tensor(dst[:, 0:heads, half:RD], b, cos, ALU.mult)
                dve.tensor_tensor(r[:, :, 0:half], b, sin, ALU.mult)
                dve.tensor_tensor(r[:, :, half:RD], a, sin, ALU.mult).then_inc(S["rope_a"], 1)
                return r, dst[:, 0:heads, :]

            def combine(n, r, dst, done):
                dve.wait_ge(S["rope_a"], n)
                dve.tensor_tensor(dst[:, :, 0:half], dst[:, :, 0:half], r[:, :, 0:half], ALU.subtract)
                return dve.tensor_tensor(dst[:, :, half:RD], dst[:, :, half:RD], r[:, :, half:RD], ALU.add).then_inc(S[done], 1)

            def latent_norm(t):
                i, b = t.i, t.b
                dve.wait_ge(S["zstd_ready"], i + 1)
                dve.reciprocal(zrstd[b][:], zstd[b][:]).then_inc(S["zrstd_ready"], 1)
                dve.wait_ge(S["zrstd_ready"], i + 1)
                dve.tensor_scalar(Z[b][:, 0:QR], Z[b][:, 0:QR], zrstd[b][:, 0:1], None, ALU.mult)
                dve.tensor_scalar(Z[b][:, QR:QR + KVR], Z[b][:, QR:QR + KVR], zrstd[b][:, 1:2], None, ALU.mult).then_inc(S["zn_ready"], 1)
                if not t.first:
                    dve.wait_ge(S["krT_ps"], i)
                src = Z[b][:, QR + KVR:ZC].unsqueeze(1)
                r, d = rotate(i, src, KRO, 1)
                combine(2 * i + 1, r, d, "rope_b")
                dve.wait_ge(S["rope_b"], i + 1)
                dve.tensor_scalar(KRO[:, 1, :], KRO[:, 0, :], 1.0, None, ALU.mult).then_inc(S["krope_ready"], 1)

            def query_rope(t):
                i, b = t.i, t.b
                dve.wait_ge(S["qr_ps"], i + 1)
                if not t.first:
                    dve.wait_ge(S["qrT_ps"], i)
                r, d = rotate(i, pE[:, 0:H1 * RD].rearrange("p (h d) -> p h d", h=H1), QRO, H1)
                combine(2 * i + 2, r, d, "qrope_ready")

            def rope_copies(t):
                i, b = t.i, t.b
                dve.wait_ge(stored_2[b], 80 * t.n + 80)
                dve.wait_ge(S["qrT_ps"], i + 1)
                dve.tensor_copy(QRT[b][:].rearrange("p h t -> p (h t)"), pF[:, 0:2 * P]).then_inc(S["qrT_copied"], 1)
                dve.wait_ge(S["krT_ps"], i + 1)
                dve.tensor_copy(KRT[b][:], pE[:, 0:P]).then_inc(S["krT_copied"], 1)

            def normalise(t):
                i, b = t.i, t.b
                dve.wait_ge(S["std_ready"], i + 1)
                dve.reciprocal(rstd[b][:], std[b][:]).then_inc(S["rstd_ready"], 1)
                dve.wait_ge(S["rstd_ready"], i + 1)
                dve.tensor_scalar(X[b][:], X[b][:], rstd[b][:], None, ALU.mult).then_inc(S["h_ready"], 1)

            def tile(t):
                i, b = t.i, t.b
                if not t.first:
                    latent_norm(t.before())
                if not is_last(t):
                    normalise(after(t))
                dve.wait_ge(S["mmA"], i + 1)
                dve.tensor_copy(Z[b][:], pA[:, 0:ZC]).then_inc(S["z_ready"], 1)
                if not t.first:
                    query_rope(t.before())
                dve.wait_ge(S["mmC"], i + 1)
                for m in range(SM):
                    out = U[:, m, :, ds(i * (P // T8), P // T8)].rearrange("p t c -> p c t")
                    src = pC[:, m * P:(m + 1) * P].rearrange("p (c t) -> p c t", t=T8)
                    d = dve.tensor_scalar(out, src, 1.0, None, ALU.mult)
                d.then_inc(S["u_copied"], 1)
                if not t.first:
                    rope_copies(t.before())

            normalise(tile_at(0))
            tiles(dve, NT, tile)
            latent_norm(tile_at(NT - 1))
            query_rope(tile_at(NT - 1))
            rope_copies(tile_at(NT - 1))


HIGH_BITS = -4096


def high_part(dve, out, x):
    return dve.tensor_scalar(out.bitcast(I32), x.bitcast(I32), HIGH_BITS, None, ALU.bitwise_and)


def attention(nc, C, stage, heads, dv, key_tiles, scale, nope, key_sets, sets_of_head, value_parts, parts_of_head, load_query,
              query_dmas, values, out):
    with ExitStack() as ctx:
        k = Kit(nc, ctx, stage)
        nk = key_tiles * P
        groups = [(g, min(4, key_tiles - 4 * g)) for g in range((key_tiles + 3) // 4)]
        banks = len(groups)
        KX = [k.sb(f"KX{b}", [P, nk]) for b in range(2)]
        KT = k.sb("KT", [P, nk])
        KH = [k.sb(f"KH{n}", [P, nk], F32R) for n in range(len(key_sets))]
        KL = [k.sb(f"KL{n}", [P, nk], F32R) for n in range(len(key_sets))]
        V = k.sb("V", [P, key_tiles, out.shape[1] if nope else KA])
        RQ = k.sb("RQ", [P, nope + 1, heads, P])
        QT = k.sb("QT", [P, nope + 1, heads, P])
        QP = [k.sb(f"QP{b}", [P, heads, P], F32R) for b in range(2)]
        QH, QL = ([k.sb(f"{n}{b}", [P, heads, P], F32R) for b in range(2)] if nope else None for n in ("QH", "QL"))
        PR = [k.sb(f"PR{b}", [P, nk]) for b in range(2)]
        PT = k.sb("PT", [P, key_tiles, P])
        OB = [k.sb(f"OB{b}", [P, heads * dv]) for b in range(2)]
        top, bias, total, inverse = ([k.sb(f"{n}{b}", [P, 1]) for b in range(2)] for n in ("top", "bias", "total", "inverse"))
        sums = [k.sb(f"sums{b}", [P, banks]) for b in range(2)]
        pS = k.ps("pS", (P, banks, BANK))
        pT = [k.ps(f"pT{b}") for b in range(2)]
        pO = k.ps("pO")
        act_moves, dve_moves = [2, 3], [g for g in range(banks) if g not in (2, 3)]
        maxima = [k.sb(f"maxima{b}", [P, banks]) for b in range(2)]
        names = """q_loaded q_masked q_high q_low k_masked q_split k_high k_split s_ps maxima_ready top_ready bias_ready p_ready t_ps act_moved dve_moved
            o_ps total_ready inverse_ready o_ready sp_turn""".split()
        S = {n: k.sem(n) for n in names}
        k_loaded = [k.sem(f"k_loaded{n}") for n in range(len(key_sets))]
        value_loads = value_parts(V)
        v_loaded = [k.sem(f"v_loaded{n}") for n in range(len(value_loads))]
        stored = [k.sem(f"stored{b}") for b in range(2)]
        block = ctx.enter_context(nc.Block())

        def unit(t, h):
            return t.i * heads + h

        def before(t, h):
            return (t, h - 1) if h else (t.before(), heads - 1)

        def new_sets(h):
            return range(sets_of_head(h - 1) if h else 0, sets_of_head(h))

        @block.sync
        def _(sp):
            wait = waiting_sp(sp, S["sp_turn"])
            for b in range(2):
                sp.sem_inc(stored[b], 16)
            load_query(sp, RQ, ds(0, P), S["q_loaded"])
            v_done = 0
            for h in range(heads):
                for n in new_sets(h):
                    if n >= 2:
                        sp.wait_ge(S["k_split"], n - 1)
                    for rows, src in key_sets[n]:
                        sp.dma_start(KX[n % 2][rows, :], src).then_inc(k_loaded[n], 16)
                for dst, src in value_loads[v_done:parts_of_head(h)]:
                    sp.dma_start(dst, src).then_inc(v_loaded[v_done], 16)
                    v_done += 1
            sp.wait_ge(S["q_split"], 1)
            load_query(sp, RQ, ds(P, P), S["q_loaded"])

            def tile(t):
                if not (isinstance(t.i, int) and t.i >= NT - 2):
                    wait(S["q_split"], t.i + 2)
                    load_query(sp, RQ, ds((t.i + 2) * P, P), S["q_loaded"])
                if not t.first:
                    store(t.before())

            def store(t):
                wait(S["o_ready"], (t.i + 1) * heads)
                sp.dma_start(out[t.tokens(), :], OB[t.b][:]).then_inc(stored[t.b], 16)

            tiles(sp, NT, tile, last=3)
            store(tile_at(NT - 1))
            for b in range(2):
                sp.wait_ge(stored[b], 16 + 16 * (NT // 2))

        @block.gpsimd
        def _(pool):
            def low_queries(t):
                pool.wait_ge(S["q_high"], t.i + 1)
                if not t.first:
                    pool.wait_ge(S["q_split"], t.i)
                if nope:
                    pool.tensor_tensor(QL[t.b][:], RQ[:, 1], QT[:, 1], ALU.subtract).then_inc(S["q_low"], 1)
                    pool.wait_ge(S["q_low"], t.i + 1)
                pool.tensor_tensor(QP[t.b][RD:P], RQ[RD:P, 0], QT[RD:P, 0], ALU.subtract).then_inc(S["q_split"], 1)

            def low_keys(h):
                for n in new_sets(h):
                    pool.wait_ge(S["k_high"], n + 1)
                    pool.tensor_tensor(KL[n][:], KX[n % 2][:], KT[:], ALU.subtract).then_inc(S["k_split"], 1)

            low_queries(tile_at(0))
            pool.wait_ge(S["q_split"], 1)
            for h in range(heads):
                low_keys(h)
            pool.wait_ge(S["k_split"], len(key_sets))

            def tile(t):
                low_queries(Tile(t.i + 1, 1 - t.b, t.n + t.b))
            tiles(pool, NT - 1, tile, last=2)

        @block.tensor
        def _(pe):
            def scores(t, h, g):
                u = unit(t, h)
                m = groups[g][1]
                if g == 0 and h == 0:
                    pe.wait_ge(S["q_split"], t.i + 1)
                if g == 0 and t.first:
                    pe.wait_ge(S["k_split"], sets_of_head(h))
                if not (t.first and h == 0):
                    pe.wait_ge(S["p_ready"], (u - 1) * banks + g + 1)
                own = sets_of_head(h) - 1
                q = QP[t.b]
                products = [(q, KH[0 if nope else own]), (q, KL[0 if nope else own])]
                if nope:
                    products += [(QH[t.b], KH[own]), (QH[t.b], KL[own]), (QL[t.b], KH[own])]
                for n, (q, keys) in enumerate(products):
                    mm = pe.matmul(pS[:, g, 0:m * P], q[:, h, :], keys[:, g * BANK:g * BANK + m * P],
                                   start=n == 0, stop=n == len(products) - 1)
                mm.then_inc(S["s_ps"], 1)

            def moved(u, g):
                if g in act_moves:
                    pe.wait_ge(S["act_moved"], u * len(act_moves) + act_moves.index(g) + 1)
                else:
                    pe.wait_ge(S["dve_moved"], u * len(dve_moves) + dve_moves.index(g) + 1)

            def turn(t, h, b, g):
                u = unit(t, h)
                pe.wait_ge(S["p_ready"], u * banks + g + 1)
                if g >= 2:
                    moved(u, g - 2)
                for j in range(groups[g][1]):
                    x = PR[b][:, (4 * g + j) * P:(4 * g + j + 1) * P]
                    tr = pe.transpose(pT[g % 2][:, j * P:(j + 1) * P], x, C["ident"][:])
                tr.then_inc(S["t_ps"], 1)

            def apply(t, h, g):
                u = unit(t, h)
                moved(u, g)
                if g == 0 and t.first:
                    for n in range(parts_of_head(h)):
                        pe.wait_ge(v_loaded[n], 16)
                if g == 0 and not (t.first and h == 0):
                    pe.wait_ge(S["o_ready"], u)
                for j in range(groups[g][1]):
                    jj = 4 * g + j
                    mm = pe.matmul(pO[:, 0:dv], PT[:, jj, :], values(V, h, jj), start=jj == 0, stop=jj == key_tiles - 1)
                if g == banks - 1:
                    mm.then_inc(S["o_ps"], 1)

            between = [[(turn, 0)], [(turn, 1)], [(apply, 0)], [], []][:banks]
            between[-1] = between[-1] + [(turn, 2), (turn, 3), (apply, 1), (apply, 2)] + [(turn, g) for g in range(4, banks)] + \
                [(apply, g) for g in range(3, banks)]

            def of_unit_before(steps, t, h):
                pt, ph = before(t, h)
                for what, g in steps:
                    if what is turn:
                        turn(pt, ph, (h - 1) % 2, g)
                    else:
                        apply(pt, ph, g)

            def tile(t):
                for h in range(heads):
                    for g in range(banks):
                        scores(t, h, g)
                        if not (t.first and h == 0):
                            of_unit_before(between[g], t, h)

            tiles(pe, NT, tile)
            for steps in between:
                of_unit_before(steps, tile_at(NT), 0)

        @block.scalar
        def _(act):
            def move(t, h):
                u = unit(t, h)
                for g in act_moves:
                    m = groups[g][1]
                    act.wait_ge(S["t_ps"], u * banks + g + 1)
                    act.activation(PT[:, 4 * g:4 * g + m, :].rearrange("p a b -> p (a b)"), pT[g % 2][:, 0:m * P], ACT.Copy).then_inc(S["act_moved"], 1)

            def exps(t, h, b):
                u = unit(t, h)
                act.wait_ge(S["bias_ready"], u + 1)
                if not (t.first and h < 2):
                    act.wait_ge(S["t_ps"], (u - 1) * banks)
                for g, m in groups:
                    act.activation(PR[b][:, g * BANK:g * BANK + m * P], pS[:, g, 0:m * P], ACT.Exp, bias=bias[b][:], scale=scale,
                                   accum_out=sums[b][:, g:g + 1]).then_inc(S["p_ready"], 1)

            def tile(t):
                for h in range(heads):
                    if not (t.first and h == 0):
                        move(*before(t, h))
                    exps(t, h, h % 2)

            tiles(act, NT, tile)
            move(tile_at(NT - 1), heads - 1)

        @block.vector
        def _(dve):
            def maximum(t, h, b, g):
                u = unit(t, h)
                dve.wait_ge(S["s_ps"], u * banks + g + 1)
                dve.tensor_reduce(maxima[b][:, g:g + 1], pS[:, g, 0:groups[g][1] * P], AX_X, ALU.max).then_inc(S["maxima_ready"], 1)

            def top_of(t, h, b):
                u = unit(t, h)
                dve.wait_ge(S["maxima_ready"], (u + 1) * banks)
                dve.tensor_reduce(top[b][:], maxima[b][:], AX_X, ALU.max).then_inc(S["top_ready"], 1)
                dve.wait_ge(S["top_ready"], u + 1)
                dve.tensor_scalar(bias[b][:], top[b][:], -scale, None, ALU.mult).then_inc(S["bias_ready"], 1)

            def move(t, h, g):
                u = unit(t, h)
                m = groups[g][1]
                dve.wait_ge(S["t_ps"], u * banks + g + 1)
                dve.tensor_copy(PT[:, 4 * g:4 * g + m, :].rearrange("p a b -> p (a b)"), pT[g % 2][:, 0:m * P]).then_inc(S["dve_moved"], 1)

            def finish(t, h, b):
                u = unit(t, h)
                dve.wait_ge(S["p_ready"], (u + 1) * banks)
                dve.tensor_reduce(total[b][:], sums[b][:], AX_X, ALU.add).then_inc(S["total_ready"], 1)
                dve.wait_ge(S["total_ready"], u + 1)
                dve.reciprocal(inverse[b][:], total[b][:]).then_inc(S["inverse_ready"], 1)
                dve.wait_ge(S["inverse_ready"], u + 1)
                dve.wait_ge(S["o_ps"], u + 1)
                if h == 0:
                    dve.wait_ge(stored[t.b], 16 * t.n + 16)
                dve.tensor_scalar(OB[t.b][:, h * dv:(h + 1) * dv], pO[:, 0:dv], inverse[b][:], None, ALU.mult).then_inc(S["o_ready"], 1)

            def high_queries(t):
                dve.wait_ge(S["q_loaded"], 16 * query_dmas * (t.i + 1))
                if not t.first:
                    dve.wait_ge(S["q_split"], t.i)
                high_part(dve, QT[:], RQ[:]).then_inc(S["q_masked"], 1)
                dve.wait_ge(S["q_masked"], t.i + 1)
                if nope:
                    dve.tensor_copy(QH[t.b][:], QT[:, 1])
                dve.tensor_copy(QP[t.b][0:RD], QT[0:RD, 0]).then_inc(S["q_high"], 1)

            def high_keys(h):
                for n in new_sets(h):
                    dve.wait_ge(k_loaded[n], 16 * len(key_sets[n]))
                    if n:
                        dve.wait_ge(S["k_split"], n)
                    high_part(dve, KT[:], KX[n % 2][:]).then_inc(S["k_masked"], 1)
                    dve.wait_ge(S["k_masked"], n + 1)
                    dve.tensor_copy(KH[n][:], KT[:]).then_inc(S["k_high"], 1)

            high_queries(tile_at(0))
            high_keys(0)

            def tile(t):
                for h in range(heads):
                    if h == 2 and not (isinstance(t.i, int) and t.i == NT - 1):
                        high_queries(Tile(t.i + 1, 1 - t.b, t.n + t.b))
                    any_before = not (t.first and h == 0)
                    for g in range(banks):
                        maximum(t, h, h % 2, g)
                        if g < 2 and any_before:
                            move(*before(t, h), g)
                    top_of(t, h, h % 2)
                    if t.first and h + 1 < heads:
                        high_keys(h + 1)
                    if any_before:
                        for g in range(4, banks):
                            move(*before(t, h), g)
                        finish(*before(t, h), (h - 1) % 2)

            tiles(dve, NT, tile)
            for g in dve_moves:
                move(tile_at(NT - 1), heads - 1, g)
            finish(tile_at(NT - 1), heads - 1, 1)


def attention_1(nc, C, D):
    every = slice(0, P)
    key_sets = [[(every, D["kr"])]] + [[(every, D["kn"][h * P:(h + 1) * P, :])] for h in range(H1)]

    def value_parts(V):
        v = D["v"].rearrange("(n p) d -> p n d", p=P)
        return [(V[:, :, h * DV:(h + 1) * DV], v[:, :, h * DV:(h + 1) * DV]) for h in range(H1)]

    def load_query(sp, q, tok, sem):
        sp.dma_start(q[:, 1], D["qn"].rearrange("(h p) t -> p h t", p=P)[:, :, tok]).then_inc(sem, 16)
        for half in range(2):
            sp.dma_start(q[half * RD:(half + 1) * RD, 0], D["qr"].rearrange("(h p) t -> p h t", p=RD)[:, :, tok]).then_inc(sem, 16)

    attention(nc, C, "a1", H1, DV, NT, (DN + RD) ** -0.5, 1, key_sets, lambda h: h + 2, value_parts, lambda h: h + 1, load_query, 3,
              lambda V, h, j: V[:, j, h * DV:(h + 1) * DV], D["ao"])


GB = 8
DG = 2 * GB


def s5(nc, I, D, C):
    with ExitStack() as ctx:
        k = Kit(nc, ctx, "s5")
        small = {n: k.sb(n, [P, DG]) for n in """lam_re lam_im log_dt dt mag_arg ang mag mag8 kk sin cos lr lr1 li t1 t2 den fr fi
            sin8 cos8 m1 m2""".split()}
        coef_a, coef_b = k.sb("coef_a", [P, 2 * DG]), k.sb("coef_b", [P, 2 * DG])
        raw = {n: k.sb(n, [P, DG, GC]) for n in ("b_v", "b_u", "c_v", "c_u")}
        d_col = k.sb("d_col", [P, GB])
        X = k.sb("X", [P, GB, NCH])
        TV, TU = (k.sb(n, [P, 2 * DG, T8 + 1, GC]) for n in ("TV", "TU"))
        column = {"Bb": 0, "Cf": GB, "Bf": 2 * GB, "Cb": 3 * GB}
        q1, q2, q3, q4 = (k.sb(f"q{n}", [P, 2 * DG, GC]) for n in range(4))
        WB = k.sb("WB", [P, 2 * DG, P])
        KS = k.sb("KS", [GC, DG, P])
        LF, LB, LL = (k.sb(n, [P, GB, P]) for n in ("LF", "LB", "LL"))
        COS, SIN = k.sb("COS", [P, DG, NCH]), k.sb("SIN", [P, DG, NCH])
        R1, R2 = k.sb("R1", [P, DG, NCH]), k.sb("R2", [P, DG, NCH])
        Y = k.sb("Y", [P, GB, NCH])
        pW = [k.ps(f"pW{b}") for b in range(2)]
        pX = [k.ps(f"pX{b}") for b in range(4)]
        pY = [k.ps(f"pY{b}") for b in range(2)]
        names = """loaded x_loaded dt_ready angle_ready reduced sines_ready powers_ready w_ps w_moved k_moved L_dma L_ready s_ps turned
            scanned products_1 products_2 y_ps y_moved y_stored step pool_step tables_ready""".split()
        S = {n: k.sem(n) for n in names}
        zeroed = k.sem("zeroed")

        with nc.Block() as block:
            @block.gpsimd
            def _(pool):
                pool.memset(LF[:], 0.0)
                pool.memset(LB[:], 0.0).then_inc(zeroed, 1)
                pool.wait_ge(zeroed, 1)

        u_view = D["u"].rearrange("(g c) (t n) -> t c g n", c=GC, t=T8)
        y_view = D["y"].rearrange("(g c) (t n) -> t c g n", c=GC, t=T8)

        def double(tt, n):
            shape = [P, DG, n]
            c, s = (bcast(small[x][:].unsqueeze(2), shape) for x in ("cos8", "sin8"))
            cos, sin = COS[:, :, 0:n], SIN[:, :, 0:n]
            a, b, a2, b2 = (R[:, :, at:at + n] for R in (R1, R2) for at in (0, n))
            tt(a, cos, c, ALU.mult)
            tt(b, sin, s, ALU.mult)
            tt(a2, sin, c, ALU.mult)
            tt(b2, cos, s, ALU.mult)
            tt(COS[:, :, n:2 * n], a, b, ALU.subtract)
            tt(SIN[:, :, n:2 * n], a2, b2, ALU.add)

        with nc.Fori(0, NG // GB) as q:
            with nc.Block() as block:
                @block.sync
                def _(sp):
                    for n in ("lam_re", "lam_im", "log_dt"):
                        sp.dma_start(small[n][:], I[n][:, q, :]).then_inc(S["loaded"], 16)
                    for n in raw:
                        sp.dma_start(raw[n][:], I[n][:, q, :, :]).then_inc(S["loaded"], 16)
                    sp.dma_start(d_col[:], I["d_col"][:, q, :]).then_inc(S["loaded"], 16)
                    for t in range(T8):
                        sp.dma_start(X[t * GC:(t + 1) * GC, :, :], u_view[t, :, ds(q * GB, GB), :]).then_inc(S["x_loaded"], 16)
                    sp.wait_ge(S["loaded"], 128)
                    sp.wait_ge(S["k_moved"], 4)
                    for t in range(T8):
                        rows = slice(t * GC, (t + 1) * GC)
                        sp.dma_start(LF[rows, :, t * GC:P], KS[:, 0:GB, 0:P - t * GC]).then_inc(S["L_dma"], 16)
                        sp.dma_start(LB[rows, :, 0:(t + 1) * GC], KS[:, GB:DG, P - (t + 1) * GC:P]).then_inc(S["L_dma"], 16)
                    sp.wait_ge(S["L_dma"], 256)
                    sp.wait_ge(S["x_loaded"], 128)
                    sp.wait_ge(S["y_moved"], 4)
                    for t in range(T8):
                        sp.dma_start(y_view[t, :, ds(q * GB, GB), :], Y[t * GC:(t + 1) * GC, :, :]).then_inc(S["y_stored"], 16)
                    sp.wait_ge(S["y_stored"], 128)

                @block.vector
                def _(dve):
                    m = {n: small[n][:] for n in small}
                    do = in_turn(dve, S["step"])

                    def tt(out, a, b, op):
                        return do(dve.tensor_tensor(out, a, b, op))

                    dve.wait_ge(S["loaded"], 128)
                    dve.wait_ge(S["dt_ready"], 1)
                    do(dve.tensor_scalar(m["lam_re"], m["lam_re"], -1e-4, None, ALU.min))
                    tt(m["ang"], m["lam_im"], m["dt"], ALU.mult)
                    dve.tensor_tensor(m["mag_arg"], m["lam_re"], m["dt"], ALU.mult).then_inc(S["angle_ready"], 1)
                    reduce_angle(dve, do, m["sin"], m["kk"], m["ang"], False)
                    reduce_angle(dve, do, m["cos"], m["kk"], m["ang"], True)
                    dve.sem_inc(S["reduced"], 1)
                    do(dve.tensor_scalar(raw["b_u"][:], raw["b_u"][:], C["half_sign"][:], None, ALU.mult))
                    F, B = slice(0, GB), slice(GB, DG)

                    def power_0(table, what):
                        at = column[what]
                        return table[:, at:at + GB, 0 if at < DG else T8, :]

                    for what, d in (("Cf", F), ("Cb", B)):
                        do(dve.tensor_scalar(power_0(TV, what), raw["c_v"][:, d], C["half_sign"][:], None, ALU.mult))
                        do(dve.tensor_scalar(power_0(TU, what), raw["c_u"][:, d], -1.0, None, ALU.mult))
                    dve.wait_ge(S["sines_ready"], 1)
                    tt(m["lr"], m["mag"], m["cos"], ALU.mult)
                    tt(m["li"], m["mag"], m["sin"], ALU.mult)
                    do(dve.tensor_scalar(m["lr1"], m["lr"], 1.0, None, ALU.subtract))
                    tt(m["t1"], m["lam_re"], m["lam_re"], ALU.mult)
                    tt(m["t2"], m["lam_im"], m["lam_im"], ALU.mult)
                    tt(m["den"], m["t1"], m["t2"], ALU.add)
                    do(dve.reciprocal(m["den"], m["den"]))
                    tt(m["t1"], m["lr1"], m["lam_re"], ALU.mult)
                    tt(m["t2"], m["li"], m["lam_im"], ALU.mult)
                    tt(m["fr"], m["t1"], m["t2"], ALU.add)
                    tt(m["fr"], m["fr"], m["den"], ALU.mult)
                    tt(m["t1"], m["li"], m["lam_re"], ALU.mult)
                    tt(m["t2"], m["lr1"], m["lam_im"], ALU.mult)
                    tt(m["fi"], m["t1"], m["t2"], ALU.subtract)
                    tt(m["fi"], m["fi"], m["den"], ALU.mult)
                    shape = [P, DG, GC]
                    fr, fi = (bcast(m[n].unsqueeze(2), shape) for n in ("fr", "fi"))
                    a, b = q1[:, 0:DG, :], q2[:, 0:DG, :]
                    tt(a, raw["b_v"][:], fr, ALU.mult)
                    tt(b, raw["b_u"][:], fi, ALU.mult)
                    for what, d in (("Bf", F), ("Bb", B)):
                        tt(power_0(TV, what), a[:, d], b[:, d], ALU.subtract)
                    tt(a, raw["b_u"][:], fr, ALU.mult)
                    tt(b, raw["b_v"][:], fi, ALU.mult)
                    for what, d in (("Bf", F), ("Bb", B)):
                        tt(power_0(TU, what), a[:, d], b[:, d], ALU.add)
                    for what, d, sign in (("Bb", B, 1.0), ("Cf", F, -1.0), ("Bf", F, 1.0), ("Cb", B, -1.0)):
                        at = slice(column[what], column[what] + GB)
                        do(dve.tensor_copy(coef_a[:, at], m["lr"][:, d]))
                        do(dve.tensor_scalar(coef_b[:, at], m["li"][:, d], sign, None, ALU.mult))
                    shape = [P, DG, GC]
                    for n in range(T8):
                        halves = ((slice(0, DG), n, n + 1), (slice(DG, 2 * DG), T8 - n, T8 - n - 1))
                        for cols, old, new in halves:
                            ca, cb = (bcast(x[:, cols].unsqueeze(2), shape) for x in (coef_a, coef_b))
                            dve.tensor_tensor(q1[:, cols], TV[:, cols, old], ca, ALU.mult)
                            dve.tensor_tensor(q2[:, cols], TU[:, cols, old], cb, ALU.mult)
                            dve.tensor_tensor(q3[:, cols], TU[:, cols, old], ca, ALU.mult)
                            last = dve.tensor_tensor(q4[:, cols], TV[:, cols, old], cb, ALU.mult)
                        do(last)
                        for cols, old, new in halves:
                            dve.tensor_tensor(TV[:, cols, new], q1[:, cols], q2[:, cols], ALU.subtract)
                            last = dve.tensor_tensor(TU[:, cols, new], q3[:, cols], q4[:, cols], ALU.add)
                        do(last)
                    dve.sem_inc(S["powers_ready"], 1)
                    dve.wait_ge(S["tables_ready"], 1)
                    double(tt, NCH // 2)
                    for j in range(DG):
                        dve.wait_ge(S["s_ps"], j + 1)
                        dve.tensor_tensor(R1[:, j, :], pX[j % 4][:, 0:NCH], COS[:, j, :], ALU.mult)
                        dve.tensor_tensor(R2[:, j, :], pX[j % 4][:, NCH:2 * NCH], SIN[:, j, :], ALU.mult).then_inc(S["turned"], 1)
                    dve.wait_ge(S["turned"], DG)
                    tt(R1[:], R1[:], R2[:], ALU.add)
                    for j in range(DG):
                        d = dve.tensor_tensor_scan(R2[:, j, :], bcast(m["mag8"][:, j:j + 1], [P, NCH]), R1[:, j, :], 0.0, ALU.mult, ALU.add)
                    d.then_inc(S["scanned"], 1)
                    dve.wait_ge(S["scanned"], 1)
                    dve.tensor_tensor(R1[:], R2[:], COS[:], ALU.mult).then_inc(S["products_1"], 1)
                    dve.wait_ge(S["L_dma"], 256)
                    tt(LL[:], LF[:], LB[:], ALU.add)
                    for g in range(GB):
                        d = dve.scalar_tensor_tensor(LL[:, g, :], C["ident"][:], d_col[:, g:g + 1], LL[:, g, :], ALU.mult, ALU.add)
                    d.then_inc(S["L_ready"], 1)

                @block.gpsimd
                def _(pool):
                    do = in_turn(pool, S["pool_step"])
                    c8, s8, m1, m2 = (small[n][:] for n in ("cos8", "sin8", "m1", "m2"))

                    def tt(out, a, b, op):
                        do(pool.tensor_tensor(out, a, b, op))

                    def square(c, s):
                        tt(m1, c, c, ALU.mult)
                        tt(m2, s, s, ALU.mult)
                        tt(s8, c, s, ALU.mult)
                        tt(s8, s8, s8, ALU.add)
                        tt(c8, m1, m2, ALU.subtract)

                    pool.wait_ge(S["sines_ready"], 1)
                    square(small["cos"][:], small["sin"][:])
                    square(c8, s8)
                    square(c8, s8)
                    do(pool.memset(COS[:, :, 0:1], 1.0))
                    do(pool.memset(SIN[:, :, 0:1], 0.0))
                    n = 1
                    while n < NCH // 2:
                        double(tt, n)
                        n *= 2
                        square(c8, s8)
                    pool.sem_inc(S["tables_ready"], 1)
                    pool.wait_ge(S["scanned"], 1)
                    pool.tensor_tensor(SIN[:], R2[:], SIN[:], ALU.mult).then_inc(S["products_2"], 1)

                @block.scalar
                def _(act):
                    act.wait_ge(S["loaded"], 128)
                    act.activation(small["dt"][:], small["log_dt"][:], ACT.Exp).then_inc(S["dt_ready"], 1)
                    act.wait_ge(S["angle_ready"], 1)
                    act.activation(small["mag"][:], small["mag_arg"][:], ACT.Exp)
                    act.activation(small["mag8"][:], small["mag_arg"][:], ACT.Exp, scale=float(T8))
                    act.wait_ge(S["reduced"], 1)
                    act.activation(small["sin"][:], small["sin"][:], ACT.Sin)
                    act.activation(small["cos"][:], small["cos"][:], ACT.Sin).then_inc(S["sines_ready"], 1)
                    for j in range(8):
                        act.wait_ge(S["w_ps"], j + 1)
                        act.activation(WB[:, 4 * j:4 * j + 4, :].rearrange("p a b -> p (a b)"), pW[j % 2][:], ACT.Copy).then_inc(S["w_moved"], 1)
                    for j in range(4):
                        act.wait_ge(S["w_ps"], 8 + j + 1)
                        act.activation(KS[:, 4 * j:4 * j + 4, :].rearrange("p a b -> p (a b)"), pW[j % 2][0:GC, :], ACT.Copy).then_inc(S["k_moved"], 1)
                    for j in range(GB // 2):
                        act.wait_ge(S["y_ps"], j + 1)
                        act.activation(Y[:, 2 * j:2 * j + 2, :].rearrange("p a b -> p (a b)"), pY[j % 2][:], ACT.Copy).then_inc(S["y_moved"], 1)

                @block.tensor
                def _(pe):
                    def eight(table, what, g, late):
                        return table[:, column[what] + g, late:late + T8, :].rearrange("p t c -> p (t c)")

                    pe.wait_ge(S["powers_ready"], 1)
                    for j in range(8):
                        if j >= 2:
                            pe.wait_ge(S["w_moved"], j - 1)
                        for jj in range(4):
                            dg = (4 * j + jj) % DG
                            w = eight((TV, TU)[j // 4], "Bf" if dg < GB else "Bb", dg % GB, dg < GB)
                            w = pe.transpose(pW[j % 2][:, jj * P:(jj + 1) * P], w, C["ident"][:])
                        w.then_inc(S["w_ps"], 1)
                    for j in range(4):
                        if j < 2:
                            pe.wait_ge(S["w_moved"], 7 + j)
                        else:
                            pe.wait_ge(S["k_moved"], j - 1)
                        for jj in range(4):
                            dg = 4 * j + jj
                            f = dg < GB
                            b0 = TV[:, column["Bf"] + dg, T8, :] if f else TV[:, column["Bb"] + dg - GB, 0, :]
                            r = eight(TV, "Cf" if f else "Cb", dg % GB, not f)
                            w = pe.matmul(pW[j % 2][0:GC, jj * P:(jj + 1) * P], b0, r, start=True, stop=True)
                        w.then_inc(S["w_ps"], 1)
                    pe.wait_ge(S["w_moved"], 8)
                    pe.wait_ge(S["x_loaded"], 128)
                    for j in range(DG):
                        if j >= 4:
                            pe.wait_ge(S["turned"], j - 3)
                        x = X[:, j % GB, :] if j < GB else X[:, j % GB, ::-1]
                        pe.matmul(pX[j % 4][:, 0:NCH], WB[:, j, :], x, start=True, stop=True)
                        pe.matmul(pX[j % 4][:, NCH:2 * NCH], WB[:, DG + j, :], x, start=True, stop=True).then_inc(S["s_ps"], 1)
                    pe.wait_ge(S["L_ready"], 1)
                    pe.wait_ge(S["products_1"], 1)
                    pe.wait_ge(S["products_2"], 1)
                    for g in range(GB):
                        if g % 2 == 0 and g >= 4:
                            pe.wait_ge(S["y_moved"], g // 2 - 1)
                        y = pY[g // 2 % 2][:, (g % 2) * NCH:(g % 2 + 1) * NCH]
                        pe.matmul(y, LL[:, g, :], X[:, g, :], start=True, stop=False)
                        pe.matmul(y[:, 1:NCH], eight(TV, "Cf", g, True), R1[:, g, 0:NCH - 1], start=False, stop=False)
                        pe.matmul(y[:, 1:NCH], eight(TU, "Cf", g, True), SIN[:, g, 0:NCH - 1], start=False, stop=False)
                        pe.matmul(y[:, 0:NCH - 1], eight(TV, "Cb", g, False), R1[:, GB + g, NCH - 2::-1], start=False, stop=False)
                        mm = pe.matmul(y[:, 0:NCH - 1], eight(TU, "Cb", g, False), SIN[:, GB + g, NCH - 2::-1], start=False, stop=True)
                        if g % 2:
                            mm.then_inc(S["y_ps"], 1)

            with nc.Block() as block:
                @block.sync
                def _(sp):
                    for s in S.values():
                        sp.sem_clear(s)


def waiting_sp(sp, turn):
    def wait(sem, value):
        sp.wait_ge(sem, value)
        sp.sem_inc(turn, 1)
    return wait


def mix_1(nc, I, D, C):
    with ExitStack() as ctx:
        k = Kit(nc, ctx, "m1")
        w_out = k.sb("w_out", [P, KC, DM])
        w_glu = k.sb("w_glu", [P, SM, SW])
        out_g, b_glu, half_b = k.sb("out_g", [P, KC]), k.sb("b_glu", [P, SM]), k.sb("half_b", [P, SM])
        post_g = k.sb("post_g", [P, DM])
        YS = k.sb("YS", [P, SM, T8, NCH])
        eps4, eps16 = k.sb("eps4", [P, 1]), k.sb("eps16", [P, 1])
        XT = [k.sb(f"XT{b}", [P, DM]) for b in range(2)]
        AO = [k.sb(f"AO{b}", [P, AW]) for b in range(2)]
        GA = [k.sb(f"GA{b}", [P, AW]) for b in range(2)]
        GS = [k.sb(f"GS{b}", [P, SM, P]) for b in range(2)]
        CA = [k.sb(f"CA{b}", [P, SM, P]) for b in range(2)]
        CS = [k.sb(f"CS{b}", [P, SM, P]) for b in range(2)]
        X1 = [k.sb(f"X1{b}", [P, DM]) for b in range(2)]
        yt, yh, y2, th, v, th2, a, sq, thg, tha, junk = (k.sb(n, [P, SM, P]) for n in "yt yh y2 th v th2 a sq thg tha junk".split())
        junk2 = k.sb("junk2", [P, DM])
        r2 = k.sb("r2", [P, P])
        sd2 = k.sb("sd2", [P, P])
        ss_a, sd_a, r_a = (k.sb(n, [P, 1]) for n in ("ss_a", "sd_a", "r_a"))
        ss_m, ss_mt, sd_m, r_m = (k.sb(n, [P, w]) for n, w in (("ss_m", 2), ("ss_mt", 1), ("sd_m", 1), ("r_m", 1)))
        pG, pN, pTr = k.ps("pG"), k.ps("pN"), k.ps("pTr")
        pM = k.ps("pM", (P, 2, BANK))
        names = """small_loaded glu_loaded out_loaded folded y_loaded turn yt_ready inner_ready tanh_gelu v_ready glu_ps tanh_glu a_ready sq_ready norm_ps
            tanh_gates ssq_a std_ready std_n rs_ready cs_ready av_ready at_ps ca_ready m_ps ssm_ready sum_m std_m rm_ready tmp_ready
            x1_ready step half_ready""".split()
        S = {n: k.sem(n) for n in names}
        loaded, x_loaded, stored = ([k.sem(f"{n}{b}") for b in range(2)] for n in ("loaded", "x_loaded", "stored"))
        block = ctx.enter_context(nc.Block())
        flat = lambda t: t[:].rearrange("p a b -> p (a b)")

        @block.sync
        def _(sp):
            wait = waiting_sp(sp, S["turn"])
            for b in range(2):
                sp.sem_inc(stored[b], 16)

            def load(t):
                tok, b = t.tokens(), t.b
                sp.dma_start(AO[b][:], D["ao"][tok, :]).then_inc(loaded[b], 16)
                sp.dma_start(GA[b][:], D["ga"][tok, :]).then_inc(loaded[b], 16)
                sp.dma_start(GS[b][:], D["gs"].rearrange("(m p) t -> p m t", p=P)[:, :, tok]).then_inc(loaded[b], 16)

            def load_x(t):
                sp.dma_start(XT[t.b][:], I["x"][t.tokens(), :]).then_inc(x_loaded[t.b], 16)

            sp.dma_start(YS[:].rearrange("p m t c -> p m (t c)"), D["y"].rearrange("(m p) n -> p m n", p=P)).then_inc(S["y_loaded"], 16)
            load(tile_at(0))
            load_x(tile_at(0))
            load(tile_at(1))
            load_x(tile_at(1))
            for dst, src in ((b_glu, "b_glu"), (out_g, "out_g"), (post_g, "post_g")):
                sp.dma_start(dst[:], I[src]).then_inc(S["small_loaded"], 16)
            sp.dma_start(w_glu[:], I["w_glu"].rearrange("(k p) n -> p k n", p=P)).then_inc(S["glu_loaded"], 16)
            sp.dma_start(w_out[:], I["w_out"].rearrange("(k p) n -> p k n", p=P)).then_inc(S["out_loaded"], 16)

            def store(t):
                wait(S["x1_ready"], t.i + 1)
                sp.dma_start(D["x1"][t.tokens(), :], X1[t.b][:]).then_inc(stored[t.b], 16)

            def tile(t):
                if not t.first:
                    store(t.before())
                    if not (isinstance(t.i, int) and t.i == NT - 1):
                        nxt = Tile(t.i + 1, 1 - t.b, t.n + t.b)
                        load_x(nxt)
                if not (isinstance(t.i, int) and t.i >= NT - 2):
                    wait(S["cs_ready"], t.i + 1)
                    wait(S["av_ready"], t.i + 1)
                    load(Tile(t.i + 2, t.b, t.n + 1))

            tiles(sp, NT, tile, last=3)
            store(tile_at(NT - 1))
            for b in range(2):
                sp.wait_ge(stored[b], 16 + 16 * (NT // 2))

        @block.vector
        def _(dve):
            dve.memset(eps4[:], 4 * EPS)
            dve.memset(eps16[:], 16 * EPS).then_inc(S["step"], 1)
            dve.wait_ge(S["y_loaded"], 16)

            def last_stage(t):
                i, b = t.i, t.b
                dve.wait_ge(S["ssm_ready"], i + 1)
                dve.tensor_tensor(ss_mt[:], ss_m[:, 0:1], ss_m[:, 1:2], ALU.add).then_inc(S["sum_m"], 1)
                dve.wait_ge(S["std_m"], i + 1)
                dve.reciprocal(r_m[:], sd_m[:]).then_inc(S["rm_ready"], 1)
                dve.wait_ge(S["rm_ready"], i + 1)
                dve.wait_ge(stored[b], 16 * t.n + 16)
                dve.scalar_tensor_tensor(X1[b][:], pM[:].rearrange("p a b -> p (a b)"), r_m[:], post_g[:], ALU.mult, ALU.mult).then_inc(S["tmp_ready"], 1)

            def add_x(t):
                dve.wait_ge(S["tmp_ready"], t.i + 1)
                dve.wait_ge(x_loaded[t.b], 16 * t.n + 16)
                dve.tensor_tensor(X1[t.b][:], X1[t.b][:], XT[t.b][:], ALU.add).then_inc(S["x1_ready"], 1)

            def gelu_inner(t):
                i = t.i
                for m in range(SM):
                    src = YS[:, m, :, ds(i * (P // T8), P // T8)].rearrange("p t c -> p c t")
                    d = dve.tensor_scalar(yt[:, m, :].rearrange("p (c t) -> p c t", t=T8), src, 1.0, None, ALU.mult)
                d.then_inc(S["yt_ready"], 1)
                dve.wait_ge(S["yt_ready"], 2 * i + 1)
                dve.tensor_tensor(y2[:], yt[:], yt[:], ALU.mult)
                dve.tensor_scalar(yh[:], yt[:], 0.5, None, ALU.mult).then_inc(S["yt_ready"], 1)
                dve.wait_ge(S["yt_ready"], 2 * i + 2)
                dve.tensor_scalar(y2[:], y2[:], 0.044715, 1.0, ALU.mult, ALU.add).then_inc(S["inner_ready"], 1)
                dve.wait_ge(S["inner_ready"], 2 * i + 1)
                dve.tensor_tensor(y2[:], y2[:], yt[:], ALU.mult).then_inc(S["inner_ready"], 1)

            def gelu(t):
                dve.wait_ge(S["tanh_gelu"], t.i + 1)
                if not t.first:
                    dve.wait_ge(S["glu_ps"], t.i)
                dve.scalar_tensor_tensor(v[:], th[:], 1.0, yh[:], ALU.add, ALU.mult).then_inc(S["v_ready"], 1)

            def tile(t):
                i, b = t.i, t.b
                more = not (isinstance(i, int) and i == NT - 1)
                dve.wait_ge(S["tanh_gates"], i + 1)
                dve.wait_ge(loaded[b], 48 * t.n + 48)
                dve.scalar_tensor_tensor(thg[:], thg[:], 1.0, GS[b][:], ALU.add, ALU.mult)
                dve.scalar_tensor_tensor(flat(tha), flat(tha), 1.0, GA[b][:], ALU.add, ALU.mult).then_inc(S["step"], 1)
                if more:
                    gelu_inner(Tile(i + 1, 1 - b, t.n + b))
                dve.wait_ge(S["tanh_glu"], i + 1)
                dve.wait_ge(S["v_ready"], i + 1)
                if not t.first:
                    dve.wait_ge(S["cs_ready"], i)
                dve.scalar_tensor_tensor(a[:], th2[:], 1.0, v[:], ALU.add, ALU.mult).then_inc(S["a_ready"], 1)
                dve.wait_ge(S["a_ready"], i + 1)
                dve.tensor_tensor(sq[:], a[:], a[:], ALU.mult).then_inc(S["sq_ready"], 1)
                dve.wait_ge(S["step"], 2 * i + 2)
                dve.tensor_tensor(a[:], a[:], thg[:], ALU.mult).then_inc(S["step"], 1)
                if more:
                    gelu(Tile(i + 1, 1 - b, t.n + b))
                dve.wait_ge(S["std_ready"], i + 1)
                dve.reciprocal(r_a[:], sd_a[:]).then_inc(S["rs_ready"], 1)
                dve.wait_ge(S["rs_ready"], 2 * i + 1)
                dve.scalar_tensor_tensor(flat(tha), AO[b][:], r_a[:], flat(tha), ALU.mult, ALU.mult).then_inc(S["av_ready"], 1)
                if t.first:
                    dve.wait_ge(S["out_loaded"], 16)
                    for c in range(KC):
                        d = dve.tensor_scalar(w_out[:, c, :], w_out[:, c, :], out_g[:, c:c + 1], None, ALU.mult)
                    d.then_inc(S["folded"], 1)
                else:
                    last_stage(t.before())
                dve.wait_ge(S["std_n"], i + 1)
                dve.reciprocal(r2[:], sd2[:]).then_inc(S["rs_ready"], 1)
                dve.wait_ge(S["rs_ready"], 2 * i + 2)
                dve.wait_ge(S["step"], 2 * i + 3)
                dve.tensor_tensor(CS[b][:], a[:], bcast(r2[:].unsqueeze(1), [P, SM, P]), ALU.mult).then_inc(S["cs_ready"], 1)
                if not t.first:
                    add_x(t.before())

            gelu_inner(tile_at(0))
            dve.wait_ge(S["small_loaded"], 48)
            dve.tensor_scalar(half_b[:], b_glu[:], 0.5, None, ALU.mult).then_inc(S["half_ready"], 1)
            gelu(tile_at(0))
            tiles(dve, NT, tile)
            last_stage(tile_at(NT - 1))
            add_x(tile_at(NT - 1))

        @block.scalar
        def _(act):
            def last_stage(t):
                act.wait_ge(S["m_ps"], t.i + 1)
                for h in range(2):
                    s = act.activation(junk2[:, h * BANK:(h + 1) * BANK], pM[:, h, :], ACT.Square, accum_out=ss_m[:, h:h + 1])
                s.then_inc(S["ssm_ready"], 1)

            def gelu_tanh(t):
                act.wait_ge(S["inner_ready"], 2 * t.i + 2)
                act.activation(flat(th), flat(y2), ACT.Tanh, scale=0.7978845608028654).then_inc(S["tanh_gelu"], 1)

            def tile(t):
                i, b = t.i, t.b
                act.wait_ge(loaded[b], 48 * t.n + 48)
                if t.first:
                    act.wait_ge(S["half_ready"], 1)
                    act.wait_ge(S["step"], 1)
                else:
                    act.wait_ge(S["at_ps"], i)
                act.activation(flat(thg), flat(GS[b]), ACT.Tanh, scale=0.5)
                act.activation(flat(tha), GA[b][:], ACT.Tanh, scale=0.5).then_inc(S["tanh_gates"], 1)
                act.wait_ge(S["glu_ps"], i + 1)
                for m in range(SM):
                    s = act.activation(th2[:, m, :], pG[:, m * P:(m + 1) * P], ACT.Tanh, bias=half_b[:, m:m + 1], scale=0.5)
                s.then_inc(S["tanh_glu"], 1)
                if not (isinstance(i, int) and i == NT - 1):
                    gelu_tanh(Tile(i + 1, 1 - b, t.n + b))
                act.activation(flat(junk), AO[b][:], ACT.Square, accum_out=ss_a[:]).then_inc(S["ssq_a"], 1)
                act.wait_ge(S["ssq_a"], i + 1)
                act.activation(sd_a[:], ss_a[:], ACT.Sqrt, bias=eps4[:], scale=4 / AW).then_inc(S["std_ready"], 1)
                if not t.first:
                    last_stage_sqrt(t.before())
                act.wait_ge(S["norm_ps"], i + 1)
                act.activation(sd2[:], pN[:, 0:P], ACT.Sqrt, bias=eps16[:], scale=4 / SW).then_inc(S["std_n"], 1)
                act.wait_ge(S["at_ps"], i + 1)
                act.activation(flat(CA[b]), pTr[:], ACT.Copy).then_inc(S["ca_ready"], 1)

            def last_stage_sqrt(t):
                last_stage(t)
                act.wait_ge(S["sum_m"], t.i + 1)
                act.activation(sd_m[:], ss_mt[:], ACT.Sqrt, bias=C["eps"][:], scale=1 / DM).then_inc(S["std_m"], 1)

            gelu_tanh(tile_at(0))
            tiles(act, NT, tile)
            last_stage_sqrt(tile_at(NT - 1))

        @block.tensor
        def _(pe):
            def last_stage(t):
                i, b = t.i, t.b
                pe.wait_ge(S["ca_ready"], i + 1)
                pe.wait_ge(S["cs_ready"], i + 1)
                if t.first:
                    pe.wait_ge(S["folded"], 1)
                else:
                    pe.wait_ge(S["tmp_ready"], i)
                for h in range(2):
                    for c in range(KC):
                        src = CA[b][:, c, :] if c < SM else CS[b][:, c - SM, :]
                        mm = pe.matmul(pM[:, h, :], src, w_out[:, c, h * BANK:(h + 1) * BANK], start=c == 0, stop=c == KC - 1)
                mm.then_inc(S["m_ps"], 1)

            pe.wait_ge(S["glu_loaded"], 16)

            def tile(t):
                i, b = t.i, t.b
                pe.wait_ge(S["v_ready"], i + 1)
                if not t.first:
                    pe.wait_ge(S["tanh_glu"], i)
                for m in range(SM):
                    for c in range(SM):
                        mm = pe.matmul(pG[:, m * P:(m + 1) * P], w_glu[:, c, m * P:(m + 1) * P], v[:, c, :], start=c == 0, stop=c == SM - 1)
                mm.then_inc(S["glu_ps"], 1)
                if not t.first:
                    last_stage(t.before())
                pe.wait_ge(S["sq_ready"], i + 1)
                for c in range(SM):
                    mm = pe.matmul(pN[:, 0:P], C["ones"][:], sq[:, c, :], start=c == 0, stop=c == SM - 1)
                mm.then_inc(S["norm_ps"], 1)
                pe.wait_ge(S["av_ready"], i + 1)
                if not t.first:
                    pe.wait_ge(S["ca_ready"], i)
                for c in range(SM):
                    tr = pe.transpose(pTr[:, c * P:(c + 1) * P], tha[:, c, :], C["ident"][:])
                tr.then_inc(S["at_ps"], 1)

            tiles(pe, NT, tile)
            last_stage(tile_at(NT - 1))


NMOD = 6


def modulations(nc, I, D, C, M):
    with ExitStack() as ctx:
        k = Kit(nc, ctx, "ada")
        W = [k.sb(f"W{b}", [P, KC, BANK]) for b in range(2)]
        cc, half, cs = (k.sb(n, [P, KC, 2]) for n in ("cc", "half", "cs"))
        both, alone = k.sb("both", [P, KC, 2, P // 2]), k.sb("alone", [P, KC, P])
        R = [k.sb(f"R{b}", [P, BANK]) for b in range(2)]
        b_col, b_row, g12 = k.sb("b_col", [P, NMOD * KC]), k.sb("b_row", [P, 2, DM]), k.sb("g12", [P, 2 * KC])
        G = k.sb("G", [P, 2, DM])
        pc = [k.ps(f"pc{b}") for b in range(2)]
        pr = [k.ps(f"pr{b}") for b in range(2)]
        names = "loaded tanh_done silu cs_ready rows_ps row_moved cols_ps cols_moved gate_rows stored gains turn".split()
        S = {n: k.sem(n) for n in names}
        w_loaded = [k.sem(f"w_loaded{b}") for b in range(2)]
        w_used = k.sem("w_used")
        block = ctx.enter_context(nc.Block())
        mod = M["mod"]
        w_view = I["w_ada"].rearrange("(k p) n -> p k n", p=P)

        def parts(eng, part):
            for gate in range(2):
                with eng.Fori(0, 2) as j:
                    part(3 * gate + j, None, 2 * gate + j)
                part(3 * gate + 2, gate, 2 * gate + 2)

        @block.sync
        def _(sp):
            wait = waiting_sp(sp, S["turn"])
            for dst, src in ((cc, "c2"), (b_col, "b_ada_col"), (b_row, "b_gates"), (g12, "g12")):
                sp.dma_start(dst[:], I[src]).then_inc(S["loaded"], 16)
            sp.sem_inc(w_used, 2)

            def part(p, gate, before):
                for b in range(2):
                    wait(w_used, 2 * p + b + 1)
                    sp.dma_start(W[b][:], w_view[:, :, ds(p * DM + b * BANK, BANK)]).then_inc(w_loaded[b], 16)
            parts(sp, part)
            sp.wait_ge(S["gate_rows"], 4)
            sp.dma_start(D["gates"].rearrange("p (a n) -> p a n", a=2), G[:]).then_inc(S["stored"], 16)
            sp.wait_ge(S["stored"], 16)

        @block.scalar
        def _(act):
            act.wait_ge(S["loaded"], 64)
            act.activation(half[:], cc[:], ACT.Tanh, scale=0.5).then_inc(S["tanh_done"], 1)

            def part(p, gate, before):
                if gate is None:
                    for b in range(2):
                        act.wait_ge(S["rows_ps"], 2 * p + b + 1)
                        act.activation(R[b][:], pr[b][:], ACT.Copy).then_inc(S["row_moved"], 1)
            act.sem_inc(S["row_moved"], 2)
            parts(act, part)

        @block.tensor
        def _(pe):
            pe.wait_ge(S["cs_ready"], 1)

            def part(p, gate, before):
                for b in range(2):
                    pe.wait_ge(w_loaded[b], 16 * (p + 1))
                    pe.wait_ge(S["row_moved"], 2 * before + b + 1)
                    if gate is None:
                        for c in range(KC):
                            mm = pe.matmul(pr[b][:], both[:, c].rearrange("p x y -> p (x y)"), W[b][:, c, :], start=c == 0, stop=c == KC - 1)
                    else:
                        for c in range(KC):
                            mm = pe.matmul(pr[b][:], alone[:, c, :], W[b][:, c, :], start=c == 0, stop=c == KC - 1)
                    mm.then_inc(S["rows_ps"], 1)
                    pe.drain().then_inc(w_used, 1)
                    if b and gate is None:
                        columns(0, before)
                if gate is None:
                    columns(1, before)
                else:
                    pe.wait_ge(S["gate_rows"], 2 * gate + 2)

            def columns(b, before):
                pe.wait_ge(S["row_moved"], 2 * before + b + 3)
                pe.wait_ge(S["cols_moved"], 2 * before + b + 1)
                for m in range(4):
                    tr = pe.transpose(pc[b][:, m * P:(m + 1) * P], R[b][:, m * P:(m + 1) * P], C["ident"][:])
                tr.then_inc(S["cols_ps"], 1)
            parts(pe, part)

        @block.vector
        def _(dve):
            dve.sem_inc(S["cols_moved"], 2)
            dve.wait_ge(S["loaded"], 64)
            dve.wait_ge(S["tanh_done"], 1)
            dve.scalar_tensor_tensor(cs[:], half[:], 1.0, cc[:], ALU.add, ALU.mult).then_inc(S["silu"], 1)
            dve.wait_ge(S["silu"], 1)
            dve.tensor_scalar(cs[:], cs[:], 0.5, None, ALU.mult).then_inc(S["silu"], 1)
            dve.wait_ge(S["silu"], 2)
            dve.tensor_copy(both[:], bcast(cs[:].unsqueeze(3), [P, KC, 2, P // 2]))
            dve.tensor_copy(alone[:], bcast(cs[:, :, 0:1], [P, KC, P])).then_inc(S["cs_ready"], 1)

            def part(p, gate, before):
                for b in range(2):
                    if gate is None:
                        dve.wait_ge(S["cols_ps"], 2 * before + b + 1)
                        bias = bcast(b_col[:, ds(p * KC + 4 * b, 4)].unsqueeze(2), [P, 4, 2])
                        out = mod[:, ds(p * KC + 4 * b, 4), :]
                        columns = pc[b][:].rearrange("p (m x y) -> p m x y", m=4, x=2)[:, :, :, 0]
                        dve.tensor_tensor(out, columns, bias, ALU.add).then_inc(S["cols_moved"], 1)
                    else:
                        dve.wait_ge(S["rows_ps"], 2 * p + b + 1)
                        cols = slice(b * BANK, (b + 1) * BANK)
                        dve.tensor_tensor(G[:, gate, cols], pr[b][:], b_row[:, gate, cols], ALU.add).then_inc(S["gate_rows"], 1)
            parts(dve, part)
            dve.wait_ge(S["cols_moved"], 2 + 8)
            for n, at in ((0, KC), (1, 4 * KC)):
                scale = mod[:, at:at + KC, :]
                dve.tensor_scalar(scale, scale, 1.0, None, ALU.add).then_inc(S["gains"], 1)
                dve.wait_ge(S["gains"], 2 * n + 1)
                g = bcast(g12[:, n * KC:(n + 1) * KC].unsqueeze(2), [P, KC, 2])
                dve.tensor_tensor(scale, scale, g, ALU.mult).then_inc(S["gains"], 1)


HA, HKV, HD = 8, 2, 64
HR, RV = 4, 128
CTX = 256
NC2 = CTX // P
RW = HR * RV
QA, KA, RQ = HA * HD, HKV * HD, HR * HD
PROJ = QA + 2 * KA + 2 * RQ + 2 * RW
BANKS2 = ((0, 512), (512, 1024), (1024, 1280), (1280, 1792), (1792, 2304))


def project_2(nc, I, D, C, M):
    with ExitStack() as ctx:
        k = Kit(nc, ctx, "p2")
        w_in = k.sb("w_in", [P, KC, PROJ])
        gq, gk = k.sb("gq", [P, HD]), k.sb("gk", [P, HD])
        cos, sin = k.sb("cos", [P, NT, HD // 2]), k.sb("sin", [P, NT, HD // 2])
        X = [k.sb(f"X{b}", [P, DM]) for b in range(2)]
        HT = [k.sb(f"HT{b}", [P, KC, P]) for b in range(2)]
        junk = k.sb("junk", [P, DM])
        NH = HA + HKV
        Z = k.sb("Z", [P, NH + 2 * HR, HD])
        ZR = k.sb("ZR", [P, NH + 2 * HR, HD])
        t1, t2 = k.sb("t1", [P, NH + 2 * HR, HD // 2]), k.sb("t2", [P, NH + 2 * HR, HD // 2])
        hss, hsd, hr = (k.sb(n, [P, NH]) for n in ("hss", "hsd", "hr"))
        VA = [k.sb(f"VA{b}", [P, KA]) for b in range(2)]
        VR = [k.sb(f"VR{b}", [P, RW]) for b in range(2)]
        GR = [k.sb(f"GR{b}", [P, RW]) for b in range(2)]
        KR = [k.sb(f"KR{b}", [P, RQ]) for b in range(2)]
        TA = [k.sb(f"TA{b}", [P, 5, P]) for b in range(2)]
        TR = [k.sb(f"TR{b}", [P, 4, P]) for b in range(2)]
        ssq, std, rstd = ([k.sb(f"{n}{b}", [P, 1]) for b in range(2)] for n in ("ssq", "std", "rstd"))
        pT = [k.ps(f"pT{b}") for b in range(2)]
        pZ = [k.ps(f"pZ{b}") for b in range(5)]
        pR = k.ps("pR")
        names = """weights_loaded turn ssq_done std_ready rstd_ready h_ready hT_ps hT_ready z_ps zq_moved zk_moved zr_moved v_moved g_moved
            hss_done hsd_ready hr_ready zn_ready roped tr_ps tr_moved sq_ready rope_1 kr_moved""".split()
        S = {n: k.sem(n) for n in names}
        x_loaded, stored = ([k.sem(f"{n}{b}") for b in range(2)] for n in ("x_loaded", "stored"))
        w_loaded = [k.sem(f"w_loaded{n}") for n in range(5)]
        block = ctx.enter_context(nc.Block())
        NTT = NT + NC2
        STORES = 7

        def tiles2(eng, body):
            tiles(eng, NT, body)
            for i in range(NT, NTT):
                body(tile_at(i))

        def is_last(t):
            return isinstance(t.i, int) and t.i == NTT - 1

        def after(t):
            return Tile(t.i + 1, 1 - t.b, t.n + t.b)

        def is_ctx(t):
            return isinstance(t.i, int) and t.i >= NT

        @block.sync
        def _(sp):
            wait = waiting_sp(sp, S["turn"])
            for b in range(2):
                sp.sem_inc(stored[b], 16 * STORES)

            def load_x(i, b, ctx_tile=False):
                src = I["ctx"][(i - NT) * P:(i - NT + 1) * P, :] if ctx_tile else D["x1"][ds(i * P, P), :]
                sp.dma_start(X[b][:], src).then_inc(x_loaded[b], 16)

            load_x(0, 0)
            load_x(1, 1)
            for dst, src in ((gq, "gq"), (gk, "gk"), (cos, "cos2"), (sin, "sin2")):
                sp.dma_start(dst[:], I[src]).then_inc(S["weights_loaded"], 16)
            w_view = I["w_in_2"].rearrange("(k p) n -> p k n", p=P)
            for n, (lo, hi) in enumerate(BANKS2):
                sp.dma_start(w_in[:, :, lo:hi], w_view[:, :, lo:hi]).then_inc(w_loaded[n], 16)

            def store(t):
                tok, b = t.tokens(), t.b
                wait(S["g_moved"], t.i + 1)
                wait(S["v_moved"], t.i + 1)
                wait(S["zk_moved"], t.i + 1)
                sp.dma_start(D["va"][tok, :], VA[b][:]).then_inc(stored[b], 16)
                sp.dma_start(D["vr"][tok, :], VR[b][:]).then_inc(stored[b], 16)
                sp.dma_start(D["gr"][tok, :], GR[b][:]).then_inc(stored[b], 16)
                wait(S["kr_moved"], t.i + 1)
                sp.dma_start(D["krt"][tok, :], KR[b][:]).then_inc(stored[b], 16)
                wait(S["tr_moved"], 3 * t.i + 4)
                sp.dma_start(D["qka"].rearrange("(c p) t -> p c t", p=P)[:, :, tok], TA[b][:]).then_inc(stored[b], 16)
                qk = D["qkr"].rearrange("(c p) t -> p c t", p=P)
                sp.dma_start(qk[:, 0:2, tok], TR[b][:, 0:2, :]).then_inc(stored[b], 16)
                sp.dma_start(qk[:, 2:4, tok], TR[b][:, 2:4, :]).then_inc(stored[b], 16)

            def tile(t):
                if not (isinstance(t.i, int) and t.i >= NTT - 2):
                    wait(S["hT_ps"], 2 * t.i + 2)
                    load_x(t.i + 2, t.b, isinstance(t.i, int) and t.i + 2 >= NT)
                if not t.first:
                    store(t.before())

            tiles(sp, NT, tile, last=3)
            for i in range(NT, NTT):
                tile(tile_at(i))
            store(tile_at(NTT - 1))
            for b in range(2):
                sp.wait_ge(stored[b], 16 * STORES * (NTT // 2 + 1))

        @block.tensor
        def _(pe):

            def turned(t):
                i = t.i
                pe.wait_ge(S["roped"], i + 1)
                for n in range(3):
                    if n == 0:
                        pe.wait_ge(S["tr_moved"], 3 * i + 1)
                    cols = ((0, 4), (4, 5), (5, 9))[n]
                    bank = (pR, pT[0], pT[1])[n]
                    for m in range(*cols):
                        at = (m - cols[0]) * P
                        tr = pe.transpose(bank[:, at:at + P], ZR[:, 2 * m:2 * m + 2, :].rearrange("p h d -> p (h d)"), C["ident"][:])
                    tr.then_inc(S["tr_ps"], 1)

            def transposed(t):
                i, b = t.i, t.b
                pe.wait_ge(S["h_ready"], i + 1)
                if not t.first:
                    pe.wait_ge(S["tr_moved"], 3 * i - 2)
                for c in range(KC):
                    tr = pe.transpose(pT[c // 4][:, (c % 4) * P:(c % 4 + 1) * P], X[b][:, c * P:(c + 1) * P], C["ident"][:])
                    if c % 4 == 3:
                        tr.then_inc(S["hT_ps"], 1)

            def tile(t):
                i, b = t.i, t.b
                pe.wait_ge(S["hT_ready"], 2 * i + 2)
                for n, (lo, hi) in enumerate(BANKS2):
                    if t.first:
                        pe.wait_ge(w_loaded[n], 16)
                    else:
                        pe.wait_ge(S[("zq_moved", "zk_moved", "zr_moved", "v_moved", "g_moved")[n]], i)
                    for c in range(KC):
                        mm = pe.matmul(pZ[n][:, 0:hi - lo], HT[b][:, c, :], w_in[:, c, lo:hi], start=c == 0, stop=c == KC - 1)
                    mm.then_inc(S["z_ps"], 1)
                    if n == 3 and not is_last(t):
                        transposed(after(t))
                    if n == 2 and not t.first:
                        turned(t.before())

            transposed(tile_at(0))
            tiles2(pe, tile)
            turned(tile_at(NTT - 1))

        @block.scalar
        def _(act):
            def square_sum(t):
                i, b = t.i, t.b
                act.wait_ge(x_loaded[b], 16 * t.n + 16)
                act.activation(junk[:], X[b][:], ACT.Square, accum_out=ssq[b][:]).then_inc(S["ssq_done"], 1)
                act.wait_ge(S["ssq_done"], i + 1)
                act.activation(std[b][:], ssq[b][:], ACT.Sqrt, bias=C["eps"][:], scale=1 / DM).then_inc(S["std_ready"], 1)

            def modulate(t):
                i, b = t.i, t.b
                who = 1 if is_ctx(t) else 0
                for half in range(2):
                    act.wait_ge(S["hT_ps"], 2 * i + half + 1)
                    for c in range(4 * half, 4 * half + 4):
                        a = act.activation(HT[b][:, c, :], pT[half][:, (c % 4) * P:(c % 4 + 1) * P], ACT.Identity,
                                           bias=M["mod"][:, c, who:who + 1], scale=M["mod"][:, KC + c, who:who + 1])
                    a.then_inc(S["hT_ready"], 1)

            def tile(t):
                i, b = t.i, t.b
                if not is_last(t):
                    square_sum(after(t))
                if not t.first:
                    heads(t.before())
                    moves(t.before())
                act.wait_ge(stored[b], 16 * STORES * (t.n + 1))
                act.wait_ge(S["z_ps"], 5 * i + 4)
                act.activation(VR[b][:], pZ[3][:], ACT.Copy).then_inc(S["v_moved"], 1)
                if not is_last(t):
                    modulate(after(t))
                act.wait_ge(S["z_ps"], 5 * i + 5)
                act.activation(GR[b][:], pZ[4][:], ACT.Copy).then_inc(S["g_moved"], 1)

            def heads(t):
                act.wait_ge(S["hss_done"], t.i + 1)
                act.activation(hsd[:], hss[:], ACT.Sqrt, bias=C["eps"][:], scale=1 / HD).then_inc(S["hsd_ready"], 1)

            def moves(t):
                for n in range(3):
                    act.wait_ge(S["tr_ps"], 3 * t.i + n + 1)
                    dst = (TA[t.b][:, 0:4, :], TA[t.b][:, 4:5, :], TR[t.b][:])[n]
                    width = (4, 1, 4)[n] * P
                    if n == 0:
                        act.wait_ge(stored[t.b], 16 * STORES * (t.n + 1))
                    act.activation(dst.rearrange("p a b -> p (a b)"), (pR, pT[0], pT[1])[n][:, 0:width], ACT.Copy).then_inc(S["tr_moved"], 1)

            act.sem_inc(S["tr_moved"], 1)
            square_sum(tile_at(0))
            modulate(tile_at(0))
            tiles2(act, tile)
            heads(tile_at(NTT - 1))
            moves(tile_at(NTT - 1))

        @block.vector
        def _(dve):
            half = HD // 2

            def normalise(t):
                i, b = t.i, t.b
                dve.wait_ge(S["std_ready"], i + 1)
                dve.reciprocal(rstd[b][:], std[b][:]).then_inc(S["rstd_ready"], 1)
                dve.wait_ge(S["rstd_ready"], i + 1)
                dve.tensor_scalar(X[b][:], X[b][:], rstd[b][:], None, ALU.mult).then_inc(S["h_ready"], 1)

            def tile(t):
                i, b = t.i, t.b
                if t.first:
                    dve.wait_ge(S["weights_loaded"], 64)
                if not t.first:
                    norm_rope(t.before())
                if not is_last(t):
                    normalise(after(t))
                dve.wait_ge(S["z_ps"], 5 * i + 1)
                dve.tensor_copy(Z[:, 0:HA, :].rearrange("p h d -> p (h d)"), pZ[0][:]).then_inc(S["zq_moved"], 1)
                dve.wait_ge(S["z_ps"], 5 * i + 2)
                dve.tensor_copy(Z[:, HA:NH, :].rearrange("p h d -> p (h d)"), pZ[1][:, 0:KA])
                dve.wait_ge(stored[b], 16 * STORES * (t.n + 1))
                dve.tensor_copy(VA[b][:], pZ[1][:, KA:2 * KA])
                dve.tensor_copy(Z[:, NH:NH + HR, :].rearrange("p h d -> p (h d)"), pZ[1][:, 2 * KA:BANK]).then_inc(S["zk_moved"], 1)
                dve.wait_ge(S["z_ps"], 5 * i + 3)
                dve.tensor_copy(Z[:, NH + HR:NH + 2 * HR, :].rearrange("p h d -> p (h d)"), pZ[2][:, 0:RQ]).then_inc(S["zr_moved"], 1)

            def norm_rope(t):
                i, b = t.i, t.b
                dve.wait_ge(S["zr_moved"], i + 1)
                sq = ZR[:, 0:NH, :]
                if not t.first:
                    dve.wait_ge(S["tr_ps"], 3 * i)
                dve.tensor_tensor(sq, Z[:, 0:NH, :], Z[:, 0:NH, :], ALU.mult).then_inc(S["sq_ready"], 1)
                dve.wait_ge(S["sq_ready"], i + 1)
                dve.tensor_reduce(hss[:], sq, AX_X, ALU.add).then_inc(S["hss_done"], 1)
                dve.wait_ge(S["hsd_ready"], i + 1)
                dve.reciprocal(hr[:], hsd[:]).then_inc(S["hr_ready"], 1)
                dve.wait_ge(S["hr_ready"], i + 1)
                dve.tensor_tensor(Z[:, 0:NH, :], Z[:, 0:NH, :], bcast(hr[:].unsqueeze(2), [P, NH, HD]), ALU.mult).then_inc(S["zn_ready"], 1)
                dve.wait_ge(S["zn_ready"], 2 * i + 1)
                dve.tensor_tensor(Z[:, 0:HA, :], Z[:, 0:HA, :], bcast(gq[:].unsqueeze(1), [P, HA, HD]), ALU.mult)
                dve.tensor_tensor(Z[:, HA:NH, :], Z[:, HA:NH, :], bcast(gk[:].unsqueeze(1), [P, HKV, HD]), ALU.mult).then_inc(S["zn_ready"], 1)
                dve.wait_ge(S["zn_ready"], 2 * i + 2)
                all_h = NH + 2 * HR
                z = Z[:].rearrange("p h (d x) -> p h d x", x=2)
                out = ZR[:].rearrange("p h (d x) -> p h d x", x=2)
                if is_ctx(t):
                    dve.tensor_copy(ZR[:], Z[:]).then_inc(S["roped"], 1)
                else:
                    shape = [P, all_h, half]
                    c = bcast(cos[:, ds(i, 1), :], shape)
                    s = bcast(sin[:, ds(i, 1), :], shape)
                    dve.tensor_tensor(out[:, :, :, 0], z[:, :, :, 0], c, ALU.mult)
                    dve.tensor_tensor(out[:, :, :, 1], z[:, :, :, 0], s, ALU.mult)
                    dve.tensor_tensor(t1[:], z[:, :, :, 1], s, ALU.mult)
                    dve.tensor_tensor(t2[:], z[:, :, :, 1], c, ALU.mult).then_inc(S["rope_1"], 1)
                    dve.wait_ge(S["rope_1"], i + 1)
                    dve.tensor_tensor(out[:, :, :, 0], out[:, :, :, 0], t1[:], ALU.subtract)
                    dve.tensor_tensor(out[:, :, :, 1], out[:, :, :, 1], t2[:], ALU.add).then_inc(S["roped"], 1)
                dve.wait_ge(S["roped"], i + 1)
                dve.wait_ge(stored[b], 16 * STORES * (t.n + 1))
                dve.tensor_scalar(KR[b][:], ZR[:, NH + HR:all_h, :].rearrange("p h d -> p (h d)"), 1.0, None, ALU.mult).then_inc(S["kr_moved"], 1)

            normalise(tile_at(0))
            tiles2(dve, tile)
            norm_rope(tile_at(NTT - 1))


def attention_2(nc, C, D):
    share = HA // HKV
    key_sets = [[(slice(half * HD, (half + 1) * HD), D["qka"][QA + g * HD:QA + (g + 1) * HD, :]) for half in range(2)] for g in range(HKV)]

    def value_parts(V):
        return [(V[:], D["va"].rearrange("(n p) d -> p n d", p=P))]

    def load_query(sp, q, tok, sem):
        for half in range(2):
            sp.dma_start(q[half * HD:(half + 1) * HD, 0], D["qka"][0:QA, :].rearrange("(h p) t -> p h t", p=HD)[:, :, tok]).then_inc(sem, 16)

    attention(nc, C, "a2", HA, HD, NT + NC2, HD ** -0.5, 0, key_sets, lambda h: h // share + 1, value_parts, lambda h: 1, load_query, 2,
              lambda V, h, j: V[:, j, h // share * HD:(h // share + 1) * HD], D["ao2"])


def retention(nc, I, D, C):
    with ExitStack() as ctx:
        k = Kit(nc, ctx, "r")
        H2 = HD
        expo = k.sb("expo", [P, 5, P])
        ecol = k.sb("ecol", [P, 5])
        dec = k.sb("dec", [P, 3])
        lg, neg, e, l1 = (k.sb(n, [P, 3]) for n in ("lg", "neg", "e", "l1"))
        cols = k.sb("cols", [P, 5])
        DT, DB, XI = (k.sb(n, [P, P]) for n in ("DT", "DB", "XI"))
        Q, K_ = k.sb("Q", [P, SEQ]), k.sb("K", [P, SEQ])
        KT = k.sb("KT", [P, NT + NC2, H2])
        KZ = k.sb("KZ", [P, NT + NC2, 2 * H2])
        V = k.sb("V", [P, NT + NC2, RV])
        G, TG = k.sb("G", [P, NT, RV]), k.sb("TG", [P, NT, RV])
        gn = k.sb("gn", [P, 2, RV])
        UU, SS = k.sb("UU", [P, NT, RV]), k.sb("SS", [P, NT, RV])
        ST = k.sb("ST", [P, NT, P])
        O = k.sb("O", [P, NT, RV])
        stats, aggr = k.sb("stats", [P, NT, 6]), k.sb("aggr", [P, NT, 2])
        sd, rs = k.sb("sd", [P, NT]), k.sb("rs", [P, NT])
        pU = [k.ps(f"pU{b}") for b in range(2)]
        pS = [k.ps(f"pS{b}") for b in range(2)]
        pO = [k.ps(f"pO{b}") for b in range(2)]
        names = """loaded_d loaded_k loaded_q stored neg_ready e_ready l_ready lg_ready exps_ready step kz_ready u_ps u_moved s_ps s_moved o_ps
            o_moved stats_ready std_ready gate_ready qx_ready states_ready out_ready""".split()
        S = {n: k.sem(n) for n in names}
        setup = k.sem("setup")
        with nc.Block() as block:
            @block.sync
            def _(sp):
                sp.dma_start(expo[:], I["ret_expo"]).then_inc(setup, 16)
                sp.dma_start(ecol[:], I["ret_ecol"]).then_inc(setup, 16)
                sp.wait_ge(setup, 32)

            @block.vector
            def _(dve):
                dve.memset(K_[:], 0.0)

        with nc.Fori(0, HR) as h:
            with nc.Block() as block:
                @block.sync
                def _(sp):
                    sp.dma_start(dec[:], I["ret_decay"][:, h, :]).then_inc(S["loaded_d"], 16)
                    sp.dma_start(gn[:], I["ret_gn"][:, h, :, :]).then_inc(S["loaded_d"], 16)
                    sp.dma_start(KT[:], D["krt"].rearrange("(n p) d -> p n d", p=P)[:, :, ds(h * H2, H2)]).then_inc(S["loaded_k"], 16)
                    sp.dma_start(V[:], D["vr"].rearrange("(n p) d -> p n d", p=P)[:, :, ds(h * RV, RV)]).then_inc(S["loaded_k"], 16)
                    for half in range(2):
                        sp.dma_start(Q[half * H2:(half + 1) * H2, :], D["qkr"][ds(h * H2, H2), 0:SEQ]).then_inc(S["loaded_q"], 16)
                    sp.dma_start(K_[0:H2, :], D["qkr"][ds(RQ + h * H2, H2), 0:SEQ]).then_inc(S["loaded_q"], 16)
                    sp.dma_start(G[:], D["gr"].rearrange("(n p) d -> p n d", p=P)[:, 0:NT, ds(h * RV, RV)]).then_inc(S["loaded_q"], 16)
                    sp.wait_ge(S["loaded_d"], 32)
                    sp.wait_ge(S["out_ready"], 1)
                    sp.dma_start(D["ret"].rearrange("(n p) d -> p n d", p=P)[:, :, ds(h * RV, RV)], O[:]).then_inc(S["stored"], 16)
                    sp.wait_ge(S["stored"], 16)

                @block.scalar
                def _(act):
                    act.wait_ge(S["neg_ready"], 1)
                    act.activation(e[:], neg[:], ACT.Exp).then_inc(S["e_ready"], 1)
                    act.wait_ge(S["e_ready"], 1)
                    act.activation(l1[:], e[:], ACT.Ln, bias=C["one"][:]).then_inc(S["l_ready"], 1)
                    act.wait_ge(S["lg_ready"], 1)
                    act.activation(cols[:, 0:2], ecol[:, 0:2], ACT.Exp, scale=lg[:, 0:1])
                    act.activation(cols[:, 2:4], ecol[:, 2:4], ACT.Exp, scale=lg[:, 1:2])
                    act.activation(cols[:, 4:5], ecol[:, 4:5], ACT.Exp, scale=lg[:, 2:3])
                    act.activation(DT[:], expo[:, 0, :], ACT.Exp, scale=lg[:, 0:1])
                    act.activation(DB[:], expo[:, 1, :], ACT.Exp, scale=lg[:, 1:2])
                    act.activation(XI[:], expo[:, 4, :], ACT.Exp, scale=lg[:, 2:3]).then_inc(S["exps_ready"], 1)
                    act.wait_ge(S["loaded_q"], 64)
                    act.activation(TG[:], G[:], ACT.Tanh, scale=0.5).then_inc(S["gate_ready"], 1)
                    for j in range(NT // 4):
                        act.wait_ge(S["o_ps"], j + 1)
                        act.activation(O[:, 4 * j:4 * j + 4, :].rearrange("p a b -> p (a b)"), pO[j % 2][:], ACT.Copy).then_inc(S["o_moved"], 1)
                    act.wait_ge(S["stats_ready"], 1)
                    act.activation(sd[:], aggr[:, :, 1], ACT.Sqrt, bias=C["eps"][:]).then_inc(S["std_ready"], 1)

                @block.vector
                def _(dve):
                    do = in_turn(dve, S["step"])
                    dve.wait_ge(S["loaded_d"], 32)
                    do(dve.tensor_scalar(neg[:], dec[:], -1.0, None, ALU.mult))
                    dve.tensor_tensor(neg[:], neg[:], dec[:], ALU.min).then_inc(S["neg_ready"], 1)
                    dve.wait_ge(S["l_ready"], 1)
                    do(dve.tensor_scalar(lg[:], dec[:], 0.0, None, ALU.min))
                    dve.tensor_tensor(lg[:], lg[:], l1[:], ALU.subtract).then_inc(S["lg_ready"], 1)
                    dve.wait_ge(S["exps_ready"], 1)
                    scale = HD ** -0.5
                    do(dve.tensor_scalar(cols[:, 0:4], cols[:, 0:4], scale, None, ALU.mult))
                    dve.wait_ge(S["loaded_k"], 32)
                    for n0, n1, f, b in ((0, NT, 0, 2), (NT, NT + 1, 1, 2), (NT + 1, NT + 2, 0, 3)):
                        dve.tensor_scalar(KZ[:, n0:n1, 0:H2], KT[:, n0:n1, :], cols[:, f:f + 1], None, ALU.mult)
                        last = dve.tensor_scalar(KZ[:, n0:n1, H2:2 * H2], KT[:, n0:n1, :], cols[:, b:b + 1], None, ALU.mult)
                    last.then_inc(S["kz_ready"], 1)
                    do(dve.scalar_tensor_tensor(DT[:], DT[:], scale, expo[:, 2, :], ALU.mult, ALU.mult))
                    do(dve.scalar_tensor_tensor(DB[:], DB[:], scale, expo[:, 3, :], ALU.mult, ALU.mult))
                    do(dve.tensor_tensor(DT[:], DT[:], DB[:], ALU.add))
                    dve.wait_ge(S["u_ps"], 1)
                    dve.tensor_copy(SS[0:H2, 0, :], pU[0][0:H2, 0:RV])
                    dve.tensor_copy(SS[H2:P, NT - 1, :], pU[0][H2:P, 0:RV]).then_inc(S["u_moved"], 1)
                    for j in range(NT // 4):
                        dve.wait_ge(S["u_ps"], j + 2)
                        dve.tensor_copy(UU[:, 4 * j:4 * j + 4, :].rearrange("p a b -> p (a b)"), pU[(j + 1) % 2][:]).then_inc(S["u_moved"], 1)
                    dve.wait_ge(S["loaded_q"], 64)
                    for j in range(NT // 4):
                        dve.wait_ge(S["s_ps"], j + 1)
                        dve.tensor_tensor(ST[:, 4 * j:4 * j + 4, :], pS[j % 2][:].rearrange("p (a b) -> p a b", a=4),
                                          bcast(DT[:].unsqueeze(1), [P, 4, P]), ALU.mult).then_inc(S["s_moved"], 1)
                    q = Q[:].rearrange("p (n i) -> p n i", i=P)
                    dve.wait_ge(S["s_ps"], NT // 4)
                    dve.tensor_tensor(q, q, bcast(XI[:].unsqueeze(1), [P, NT, P]), ALU.mult).then_inc(S["qx_ready"], 1)
                    dve.wait_ge(S["u_moved"], 5)
                    for n in range(1, NT):
                        m = NT - 1 - n
                        dve.scalar_tensor_tensor(SS[0:H2, n, :], SS[0:H2, n - 1, :], cols[0:H2, 4:5], UU[0:H2, n - 1, :], ALU.mult, ALU.add)
                        do(dve.scalar_tensor_tensor(SS[H2:P, m, :], SS[H2:P, m + 1, :], cols[H2:P, 4:5], UU[H2:P, m + 1, :], ALU.mult, ALU.add))
                    dve.sem_inc(S["states_ready"], 1)
                    dve.wait_ge(S["gate_ready"], 1)
                    do(dve.scalar_tensor_tensor(TG[:], TG[:], 1.0, G[:], ALU.add, ALU.mult))
                    dve.wait_ge(S["o_moved"], NT // 4)
                    for n in range(NT):
                        last = dve.bn_stats(stats[:, n, :], O[:, n, :])
                    do(last)
                    for n in range(NT):
                        last = dve.bn_aggr(aggr[:, n, :], stats[:, n, :])
                    last.then_inc(S["stats_ready"], 1)
                    dve.wait_ge(S["std_ready"], 1)
                    do(dve.reciprocal(rs[:], sd[:]))
                    for n in range(NT):
                        last = dve.tensor_scalar(O[:, n, :], O[:, n, :], aggr[:, n, 0:1], rs[:, n:n + 1], ALU.subtract, ALU.mult)
                    do(last)
                    do(dve.tensor_tensor(O[:], O[:], bcast(gn[:, 0:1, :], [P, NT, RV]), ALU.mult))
                    do(dve.tensor_tensor(O[:], O[:], bcast(gn[:, 1:2, :], [P, NT, RV]), ALU.add))
                    dve.scalar_tensor_tensor(O[:], O[:], 0.5, TG[:], ALU.mult, ALU.mult).then_inc(S["out_ready"], 1)

                @block.tensor
                def _(pe):
                    pe.wait_ge(S["kz_ready"], 1)
                    for c in range(NC2):
                        mm = pe.matmul(pU[0][:, 0:RV], KZ[:, NT + c, :], V[:, NT + c, :], start=c == 0, stop=c == NC2 - 1)
                    mm.then_inc(S["u_ps"], 1)
                    for j in range(NT // 4):
                        if j:
                            pe.wait_ge(S["u_moved"], j)
                        for n in range(4 * j, 4 * j + 4):
                            mm = pe.matmul(pU[(j + 1) % 2][:, n % 4 * RV:(n % 4 + 1) * RV], KZ[:, n, :], V[:, n, :], start=True, stop=True)
                        mm.then_inc(S["u_ps"], 1)
                    pe.wait_ge(S["loaded_q"], 64)
                    for j in range(NT // 4):
                        if j >= 2:
                            pe.wait_ge(S["s_moved"], j - 1)
                        for n in range(4 * j, 4 * j + 4):
                            tok = slice(n * P, (n + 1) * P)
                            mm = pe.matmul(pS[j % 2][:, n % 4 * P:(n % 4 + 1) * P], K_[:, tok], Q[:, tok], start=True, stop=True)
                        mm.then_inc(S["s_ps"], 1)
                    pe.wait_ge(S["qx_ready"], 1)
                    pe.wait_ge(S["states_ready"], 1)
                    for j in range(NT // 4):
                        pe.wait_ge(S["s_moved"], j + 1)
                        if j >= 2:
                            pe.wait_ge(S["o_moved"], j - 1)
                        for n in range(4 * j, 4 * j + 4):
                            o = pO[j % 2][:, n % 4 * RV:(n % 4 + 1) * RV]
                            pe.matmul(o, ST[:, n, :], V[:, n, :], start=True, stop=False)
                            mm = pe.matmul(o, Q[:, n * P:(n + 1) * P], SS[:, n, :], start=False, stop=True)
                        mm.then_inc(S["o_ps"], 1)

            with nc.Block() as block:
                @block.sync
                def _(sp):
                    for s in S.values():
                        sp.sem_clear(s)


NGRP, EPG = 4, 8
NE = NGRP * EPG
DE = 512
NL = NGRP + NE
NB = 2 * SEQ // P + NE
BIG = 1e30


def mix_2(nc, I, D, C, M):
    with ExitStack() as ctx:
        k = Kit(nc, ctx, "m2")
        w_out = k.sb("w_out", [P, KC, DM])
        w_r, b_r, gate = k.sb("w_r", [P, KC, NL]), k.sb("b_r", [P, NL]), k.sb("gate", [P, DM])
        CAT = [k.sb(f"CAT{b}", [P, DM]) for b in range(2)]
        CT = [k.sb(f"CT{b}", [P, KC, P]) for b in range(2)]
        X1 = [k.sb(f"X1{b}", [P, DM]) for b in range(2)]
        X2 = [k.sb(f"X2{b}", [P, DM]) for b in range(2)]
        XH = [k.sb(f"XH{b}", [P, DM]) for b in range(2)]
        HT = k.sb("HT", [P, KC, P])
        junk = k.sb("junk", [P, DM])
        ssq, std, rstd = (k.sb(n, [P, 1]) for n in ("ssq", "std", "rstd"))
        pT = [k.ps(f"pT{b}") for b in range(2)]
        pH = [k.ps(f"pH{b}") for b in range(2)]
        pM, pL = k.ps("pM", (P, 2, BANK)), k.ps("pL")
        names = """weights_loaded turn ct_ps ct_ready m_ps gated x2_ready ssq_done std_ready rstd_ready xh_ready h_ps h_ready l_ps l_moved""".split()
        S = {n: k.sem(n) for n in names}
        loaded, x_loaded, stored = ([k.sem(f"{n}{b}") for b in range(2)] for n in ("loaded", "x_loaded", "stored"))
        w_loaded = [k.sem(f"w_loaded{h}") for h in range(2)]
        block = ctx.enter_context(nc.Block())

        def is_last(t):
            return isinstance(t.i, int) and t.i == NT - 1

        def after(t):
            return Tile(t.i + 1, 1 - t.b, t.n + t.b)

        @block.sync
        def _(sp):
            wait = waiting_sp(sp, S["turn"])
            for b in range(2):
                sp.sem_inc(stored[b], 32)

            def load(t):
                tok, b = t.tokens(), t.b
                sp.dma_start(CAT[b][:, 0:QA], D["ao2"][tok, :]).then_inc(loaded[b], 16)
                sp.dma_start(CAT[b][:, QA:DM], D["ret"][tok, :]).then_inc(loaded[b], 16)

            def load_x(t):
                sp.dma_start(X1[t.b][:], D["x1"][t.tokens(), :]).then_inc(x_loaded[t.b], 16)

            for i in range(2):
                load(tile_at(i))
                load_x(tile_at(i))
            for dst, src in ((w_r, "w_router"), (b_r, "b_router")):
                sp.dma_start(dst[:], I[src]).then_inc(S["weights_loaded"], 16)
            sp.dma_start(gate[:], D["gates"][:, 0:DM]).then_inc(S["weights_loaded"], 16)
            w_view = I["w_out_2"].rearrange("(k p) n -> p k n", p=P)
            for h in range(2):
                sp.dma_start(w_out[:, :, h * BANK:(h + 1) * BANK], w_view[:, :, h * BANK:(h + 1) * BANK]).then_inc(w_loaded[h], 16)

            def store(t):
                wait(S["xh_ready"], t.i + 1)
                sp.dma_start(D["x2"][t.tokens(), :], X2[t.b][:]).then_inc(stored[t.b], 16)
                sp.dma_start(D["h"][t.tokens(), :], XH[t.b][:]).then_inc(stored[t.b], 16)

            def tile(t):
                if not (isinstance(t.i, int) and t.i >= NT - 2):
                    wait(S["ct_ps"], 2 * t.i + 2)
                    load(Tile(t.i + 2, t.b, t.n + 1))
                if not t.first:
                    store(t.before())
                    if not (isinstance(t.i, int) and t.i == NT - 1):
                        load_x(Tile(t.i + 1, 1 - t.b, t.n + t.b))

            tiles(sp, NT, tile, last=3)
            store(tile_at(NT - 1))
            for b in range(2):
                sp.wait_ge(stored[b], 32 + 32 * (NT // 2))

        @block.tensor
        def _(pe):
            pe.wait_ge(S["weights_loaded"], 48)

            def transposed(t):
                pe.wait_ge(S["xh_ready"], t.i + 1)
                if not t.first:
                    pe.wait_ge(S["h_ready"], 2 * t.i)
                for c in range(KC):
                    tr = pe.transpose(pH[c // 4][:, (c % 4) * P:(c % 4 + 1) * P], XH[t.b][:, c * P:(c + 1) * P], C["ident"][:])
                    if c % 4 == 3:
                        tr.then_inc(S["h_ps"], 1)

            def logits(t):
                pe.wait_ge(S["h_ready"], 2 * t.i + 2)
                if not t.first:
                    pe.wait_ge(S["l_moved"], t.i)
                for c in range(KC):
                    mm = pe.matmul(pL[:, 0:NL], HT[:, c, :], w_r[:, c, :], start=c == 0, stop=c == KC - 1)
                mm.then_inc(S["l_ps"], 1)

            def branches_transposed(t):
                i, b = t.i, t.b
                pe.wait_ge(loaded[b], 32 * t.n + 32)
                if not t.first:
                    pe.wait_ge(S["ct_ready"], 2 * i)
                for c in range(KC):
                    tr = pe.transpose(pT[c // 4][:, (c % 4) * P:(c % 4 + 1) * P], CAT[b][:, c * P:(c + 1) * P], C["ident"][:])
                    if c % 4 == 3:
                        tr.then_inc(S["ct_ps"], 1)

            def tile(t):
                i, b = t.i, t.b
                if not t.first:
                    pe.wait_ge(S["gated"], i)
                pe.wait_ge(S["ct_ready"], 2 * i + 2)
                for h in range(2):
                    if t.first:
                        pe.wait_ge(w_loaded[h], 16)
                    for c in range(KC):
                        mm = pe.matmul(pM[:, h, :], CT[b][:, c, :], w_out[:, c, h * BANK:(h + 1) * BANK], start=c == 0, stop=c == KC - 1)
                    if h == 0:
                        if not t.first:
                            transposed(t.before())
                        if not is_last(t):
                            branches_transposed(after(t))
                mm.then_inc(S["m_ps"], 1)
                if not t.first:
                    logits(t.before())

            branches_transposed(tile_at(0))
            tiles(pe, NT, tile)
            transposed(tile_at(NT - 1))
            logits(tile_at(NT - 1))

        @block.scalar
        def _(act):
            def modulate(t):
                if not t.first:
                    act.wait_ge(S["l_ps"], t.i)
                for half in range(2):
                    act.wait_ge(S["h_ps"], 2 * t.i + half + 1)
                    for c in range(4 * half, 4 * half + 4):
                        a = act.activation(HT[:, c, :], pH[half][:, (c % 4) * P:(c % 4 + 1) * P], ACT.Identity,
                                           bias=M["mod"][:, 3 * KC + c, 0:1], scale=M["mod"][:, 4 * KC + c, 0:1])
                    a.then_inc(S["h_ready"], 1)

            def branches_moved(t):
                i, b = t.i, t.b
                for half in range(2):
                    act.wait_ge(S["ct_ps"], 2 * i + half + 1)
                    act.activation(CT[b][:, 4 * half:4 * half + 4, :].rearrange("p a b -> p (a b)"), pT[half][:], ACT.Copy).then_inc(S["ct_ready"], 1)

            def tile(t):
                i, b = t.i, t.b
                if not t.first:
                    modulate(t.before())
                if not is_last(t):
                    branches_moved(after(t))
                act.wait_ge(S["x2_ready"], i + 1)
                act.activation(junk[:], X2[b][:], ACT.Square, accum_out=ssq[:]).then_inc(S["ssq_done"], 1)
                act.wait_ge(S["ssq_done"], i + 1)
                act.activation(std[:], ssq[:], ACT.Sqrt, bias=C["eps"][:], scale=1 / DM).then_inc(S["std_ready"], 1)

            branches_moved(tile_at(0))
            tiles(act, NT, tile)
            modulate(tile_at(NT - 1))

        @block.vector
        def _(dve):
            dve.wait_ge(S["weights_loaded"], 48)

            def tile(t):
                i, b = t.i, t.b
                dve.wait_ge(S["m_ps"], i + 1)
                dve.wait_ge(stored[b], 32 * t.n + 32)
                dve.tensor_tensor(X2[b][:], pM[:].rearrange("p a b -> p (a b)"), gate[:], ALU.mult).then_inc(S["gated"], 1)
                dve.wait_ge(S["gated"], i + 1)
                dve.wait_ge(x_loaded[b], 16 * t.n + 16)
                dve.tensor_tensor(X2[b][:], X2[b][:], X1[b][:], ALU.add).then_inc(S["x2_ready"], 1)
                if not t.first:
                    logits(t.before())
                dve.wait_ge(S["std_ready"], i + 1)
                dve.reciprocal(rstd[:], std[:]).then_inc(S["rstd_ready"], 1)
                dve.wait_ge(S["rstd_ready"], i + 1)
                dve.tensor_scalar(XH[b][:], X2[b][:], rstd[:], None, ALU.mult).then_inc(S["xh_ready"], 1)

            def logits(t):
                dve.wait_ge(S["l_ps"], t.i + 1)
                dve.tensor_tensor(M["logits"][:, ds(t.i, 1), :], pL[:, 0:NL].unsqueeze(1), b_r[:].unsqueeze(1), ALU.add).then_inc(S["l_moved"], 1)

            tiles(dve, NT, tile)
            logits(tile_at(NT - 1))


def dispatch(nc, I, D, C, M):
    with ExitStack() as ctx:
        k = Kit(nc, ctx, "d")
        L = M["logits"]
        gl, el = L[:, :, 0:NGRP], L[:, :, NGRP:NL].rearrange("p t (g e) -> p t g e", g=NGRP)
        g1 = [k.sb(f"g1{n}", [P, NT, NGRP]) for n in range(3)]
        s1 = {n: k.sb(n, [P, NT]) for n in "gmax gsum pg m1 m2 r w den".split()}
        e4 = k.sb("e4", [P, NT, NGRP, EPG])
        sel, sel2, oh1, oh2, tmp8 = (k.sb(n, [P, NT, EPG]) for n in "sel sel2 oh1 oh2 tmp8".split())
        M1, M2, MM = (k.sb(n, [P, NT, NE]) for n in ("M1", "M2", "MM"))
        within, before, place = (k.sb(n, [P, NT, NE]) for n in ("within", "before", "place"))
        rev4, rev8 = k.sb("rev4", [P, NGRP]), k.sb("rev8", [P, EPG])
        mult, blocks_c = k.sb("mult", [P, NE, NT]), k.sb("blocks_c", [P, NB])
        cnt, nblk, last, start = (k.sb(n, [P, NE]) for n in "cnt nblk last start".split())
        cmp_ = k.sb("cmp", [P, NE, NT])
        cmpb = k.sb("cmpb", [P, NB, NE])
        dest = k.sb("dest", [P, 2, NT])
        blk = k.sb("blk", [P, NB])
        upper = k.sb("upper", [P, P])
        token = k.sb("token", [P, NT], I32)
        zero_i = k.sb("zero_i", [P, NB], I32)
        pw, pt = k.ps("pw"), k.ps("pt")
        names = "loaded exp1_in exp1 exp2_in exp2 step chosen ranks zeroed filled placed scattered".split()
        S = {n: k.sem(n) for n in names}
        block = ctx.enter_context(nc.Block())

        @block.sync
        def _(sp):
            for dst, src in ((rev4, "rev4"), (rev8, "rev8"), (mult, "mult"), (blocks_c, "block_numbers"), (upper, "upper"), (token, "token_numbers")):
                sp.dma_start(dst[:], I[src]).then_inc(S["loaded"], 16)
            sp.wait_ge(S["zeroed"], 1)
            sp.dma_start(D["slots"].rearrange("(p b) x -> p (b x)", p=P), zero_i[:]).then_inc(S["filled"], 16)

        @block.scalar
        def _(act):
            act.wait_ge(S["exp1_in"], 1)
            act.activation(g1[0][:], g1[0][:], ACT.Exp).then_inc(S["exp1"], 1)
            act.wait_ge(S["exp2_in"], 1)
            act.activation(s1["r"][:], s1["r"][:], ACT.Exp).then_inc(S["exp2"], 1)

        @block.tensor
        def _(pe):
            pe.wait_ge(S["loaded"], 96)
            pe.wait_ge(S["chosen"], 1)
            m = MM[:].rearrange("p t e -> p (t e)")
            pe.matmul(pw[:], upper[:], m, start=True, stop=True)
            pe.matmul(pt[:], C["ones"][:], m, start=True, stop=True).then_inc(S["ranks"], 1)

        @block.vector
        def _(dve):
            do = in_turn(dve, S["step"])
            tt = lambda out, a, b, op: do(dve.tensor_tensor(out, a, b, op))
            dve.memset(zero_i[:], 0).then_inc(S["zeroed"], 1)
            dve.wait_ge(S["loaded"], 96)

            def first_of(out, values, top, rev, scratch, n):
                shape = [P, NT, n]
                tt(scratch, values, bcast(top.unsqueeze(2), shape), ALU.is_equal)
                tt(scratch, scratch, bcast(rev[:].unsqueeze(1), shape), ALU.mult)
                do(dve.tensor_reduce(s1["w"][:], scratch, AX_X, ALU.max))
                tt(out, scratch, bcast(s1["w"][:].unsqueeze(2), shape), ALU.is_equal)

            gmax = s1["gmax"][:]
            do(dve.tensor_reduce(gmax, gl, AX_X, ALU.max))
            dve.tensor_tensor(g1[0][:], gl, bcast(gmax.unsqueeze(2), [P, NT, NGRP]), ALU.subtract).then_inc(S["exp1_in"], 1)
            first_of(g1[1][:], gl, gmax, rev4, g1[2][:], NGRP)
            dve.wait_ge(S["exp1"], 1)
            do(dve.tensor_reduce(s1["gsum"][:], g1[0][:], AX_X, ALU.add))
            do(dve.reciprocal(s1["pg"][:], s1["gsum"][:]))
            for g in range(NGRP):
                d = dve.tensor_tensor(e4[:, :, g, :], el[:, :, g, :], bcast(g1[1][:, :, g:g + 1], [P, NT, EPG]), ALU.mult)
            do(d)
            tt(sel[:], e4[:, :, 0, :], e4[:, :, 1, :], ALU.add)
            tt(sel[:], sel[:], e4[:, :, 2, :], ALU.add)
            tt(sel[:], sel[:], e4[:, :, 3, :], ALU.add)
            do(dve.tensor_reduce(s1["m1"][:], sel[:], AX_X, ALU.max))
            first_of(oh1[:], sel[:], s1["m1"][:], rev8, tmp8[:], EPG)
            do(dve.scalar_tensor_tensor(sel2[:], oh1[:], -BIG, sel[:], ALU.mult, ALU.add))
            do(dve.tensor_reduce(s1["m2"][:], sel2[:], AX_X, ALU.max))
            first_of(oh2[:], sel2[:], s1["m2"][:], rev8, tmp8[:], EPG)
            dve.tensor_tensor(s1["r"][:], s1["m2"][:], s1["m1"][:], ALU.subtract).then_inc(S["exp2_in"], 1)
            for oh, m in ((oh1, M1), (oh2, M2)):
                for g in range(NGRP):
                    d = dve.tensor_tensor(m[:, :, g * EPG:(g + 1) * EPG], oh[:], bcast(g1[1][:, :, g:g + 1], [P, NT, EPG]), ALU.mult)
                do(d)
            dve.tensor_tensor(MM[:], M1[:], M2[:], ALU.add).then_inc(S["chosen"], 1)
            dve.wait_ge(S["exp2"], 1)
            do(dve.tensor_scalar(s1["den"][:], s1["r"][:], 1.0, None, ALU.add))
            do(dve.reciprocal(s1["den"][:], s1["den"][:]))
            tt(M["weights"][:, 0, :], s1["pg"][:], s1["den"][:], ALU.mult)
            tt(M["weights"][:, 1, :], M["weights"][:, 0, :], s1["r"][:], ALU.mult)
            dve.wait_ge(S["ranks"], 1)
            do(dve.tensor_copy(within[:].rearrange("p t e -> p (t e)"), pw[:]))
            do(dve.tensor_copy(MM[:].rearrange("p t e -> p (t e)"), pt[:]))
            do(dve.memset(before[:, 0, :], 0.0))
            for t in range(1, NT):
                tt(before[:, t, :], before[:, t - 1, :], MM[:, t - 1, :], ALU.add)
            tt(cnt[:], before[:, NT - 1, :], MM[:, NT - 1, :], ALU.add)
            tt(cmp_[:], bcast(cnt[:].unsqueeze(2), [P, NE, NT]), mult[:], ALU.is_gt)
            do(dve.tensor_reduce(nblk[:], cmp_[:], AX_X, ALU.add))
            do(dve.tensor_tensor_scan(last[:], C["ones"][:, 0:NE], nblk[:], 0.0, ALU.mult, ALU.add))
            tt(start[:], last[:], nblk[:], ALU.subtract)
            tt(cmpb[:], bcast(blocks_c[:].unsqueeze(2), [P, NB, NE]), bcast(last[:].unsqueeze(1), [P, NB, NE]), ALU.is_ge)
            do(dve.tensor_reduce(blk[:], cmpb[:], AX_X, ALU.add))
            do(dve.tensor_scalar(M["block_expert"][:], blk[:], float(NE - 1), None, ALU.min))
            do(dve.tensor_copy(M["blocks_in_use"][:], last[:, NE - 1:NE]))
            do(dve.tensor_scalar(start[:], start[:], float(P), None, ALU.mult))
            tt(place[:], within[:], before[:], ALU.add)
            tt(place[:], place[:], bcast(start[:].unsqueeze(1), [P, NT, NE]), ALU.add)
            for n, m in ((0, M1), (1, M2)):
                tt(m[:], m[:], place[:], ALU.mult)
                do(dve.tensor_reduce(dest[:, n, :], m[:], AX_X, ALU.add))
            dve.tensor_copy(M["dest"][:], dest[:]).then_inc(S["placed"], 1)

        @block.gpsimd
        def _(pool):
            pool.wait_ge(S["placed"], 1)
            pool.wait_ge(S["filled"], 16)
            pool.wait_ge(S["loaded"], 96)
            for n in range(2):
                for t in range(NT):
                    pool.indirect_dma_start(out=D["slots"], out_offset=bass.IndirectOffsetOnAxis(ap=M["dest"][:, n, t:t + 1], axis=0),
                                            in_=token[:, t:t + 1], in_offset=None).then_inc(S["scattered"], 16)
            pool.wait_ge(S["scattered"], 16 * 2 * NT)


def experts(nc, I, D, C, M):
    with ExitStack() as ctx:
        k = Kit(nc, ctx, "e")
        WG = [k.sb(f"WG{b}", [P, KC, DE]) for b in range(2)]
        WU = [k.sb(f"WU{b}", [P, KC, DE]) for b in range(2)]
        WD = [k.sb(f"WD{b}", [P, DE // P, DM]) for b in range(2)]
        IDX = [k.sb(f"IDX{b}", [P, 1], I32) for b in range(2)]
        XG = [k.sb(f"XG{b}", [P, DM]) for b in range(2)]
        XT = [k.sb(f"XT{b}", [P, KC, P]) for b in range(2)]
        TH = k.sb("TH", [P, DE])
        HH = [k.sb(f"HH{b}", [P, DE // P, P]) for b in range(2)]
        Y = [k.sb(f"Y{b}", [P, DM]) for b in range(2)]
        pT = [k.ps(f"pT{b}") for b in range(2)]
        pG, pU = k.ps("pG"), k.ps("pU")
        pD = k.ps("pD", (P, 2, BANK))
        names = "turn t_ps t_ready g_ps u_ps th_ready silu_ready hh_ready d_ps y_ready pool_turn".split()
        S = {n: k.sem(n) for n in names}
        g_loaded, u_loaded, d_loaded, i_loaded, x_loaded, stored = ([k.sem(f"{n}{b}") for b in range(2)] for n in
                                                                     ("g_loaded", "u_loaded", "d_loaded", "i_loaded", "x_loaded", "stored"))
        block = ctx.enter_context(nc.Block())
        in_use = M["blocks_in_use"][0:1, 0:1]
        wg = I["moe_w_gate"].rearrange("e (k p) n -> p e k n", p=P)
        wu = I["moe_w_up"].rearrange("e (k p) n -> p e k n", p=P)
        wd = I["moe_w_down"].rearrange("e (k p) n -> p e k n", p=P)

        @block.sync
        def _(sp):
            wait = waiting_sp(sp, S["turn"])
            for b in range(2):
                sp.sem_inc(stored[b], 16)

            def load(t, waits):
                b = t.b
                e = sp.value_load(M["block_expert"][0:1, ds(t.i, 1)], min_val=0, max_val=NE - 1)
                if waits:
                    wait(S["t_ps"], 2 * t.i - 2)
                sp.dma_start(IDX[b][:], D["slots"][ds(t.i * P, P), :]).then_inc(i_loaded[b], 16)
                for W, w, sem, used in ((WG, wg, g_loaded, "g_ps"), (WU, wu, u_loaded, "u_ps"), (WD, wd, d_loaded, "d_ps")):
                    if waits:
                        wait(S[used], t.i - 1)
                    sp.dma_start(W[b][:], w[:, ds(e, 1), :, :].rearrange("p e k n -> p (e k) n")).then_inc(sem[b], 16)

            def store(t):
                wait(S["y_ready"], t.i + 1)
                sp.dma_start(D["yb"][ds(t.i * P, P), :], Y[t.b][:]).then_inc(stored[t.b], 16)

            load(tile_at(0), False)
            load(tile_at(1), False)

            def tile(t):
                if not (isinstance(t.i, int) and t.i >= NB - 2):
                    load(Tile(t.i + 2, t.b, t.n + 1), True)
                store(t)

            def skipped(t):
                wait(S["t_ps"], 2 * t.i + 2)
                sp.sem_inc(i_loaded[t.b], 16)
                for sem, used in ((g_loaded, "g_ps"), (u_loaded, "u_ps"), (d_loaded, "d_ps")):
                    wait(S[used], t.i + 1)
                    sp.sem_inc(sem[t.b], 16)
                store(t)
            tiles_in_use(sp, NB, in_use, tile, skipped)
            for b in range(2):
                sp.wait_ge(stored[b], 16 + 16 * (NB // 2))

        @block.gpsimd
        def _(pool):
            def tile(t):
                pool.wait_ge(i_loaded[t.b], 16 * t.n + 16)
                pool.sem_inc(S["pool_turn"], 1)
                pool.indirect_dma_start(out=XG[t.b][:], out_offset=None, in_=D["h"],
                                        in_offset=bass.IndirectOffsetOnAxis(ap=IDX[t.b][:, 0:1], axis=0)).then_inc(x_loaded[t.b], 16)

            tiles(pool, NB, tile, last=3)

        @block.tensor
        def _(pe):
            def transposed(t):
                pe.wait_ge(x_loaded[t.b], 16 * t.n + 16)
                if not t.first:
                    pe.wait_ge(S["t_ready"], 2 * t.i)
                for c in range(KC):
                    tr = pe.transpose(pT[c // 4][:, (c % 4) * P:(c % 4 + 1) * P], XG[t.b][:, c * P:(c + 1) * P], C["ident"][:])
                    if c % 4 == 3:
                        tr.then_inc(S["t_ps"], 1)

            def wide(t, bank, W, sem, made):
                pe.wait_ge(sem[t.b], 16 * t.n + 16)
                for m in range(DE // P):
                    for c in range(KC):
                        mm = pe.matmul(bank[:, m * P:(m + 1) * P], W[t.b][:, c, m * P:(m + 1) * P], XT[t.b][:, c, :], start=c == 0, stop=c == KC - 1)
                mm.then_inc(S[made], 1)

            def down(t):
                i, b = t.i, t.b
                pe.wait_ge(d_loaded[b], 16 * t.n + 16)
                pe.wait_ge(S["hh_ready"], i + 1)
                if not t.first:
                    pe.wait_ge(S["y_ready"], i)
                for h in range(2):
                    for c in range(DE // P):
                        mm = pe.matmul(pD[:, h, :], HH[b][:, c, :], WD[b][:, c, h * BANK:(h + 1) * BANK], start=c == 0, stop=c == DE // P - 1)
                mm.then_inc(S["d_ps"], 1)

            transposed(tile_at(0))

            def tile(t):
                i = t.i
                pe.wait_ge(S["t_ready"], 2 * i + 2)
                if not t.first:
                    pe.wait_ge(S["silu_ready"], i)
                wide(t, pG, WG, g_loaded, "g_ps")
                if not t.first:
                    down(t.before())
                if not (isinstance(i, int) and i == NB - 1):
                    transposed(Tile(i + 1, 1 - t.b, t.n + t.b))
                wide(t, pU, WU, u_loaded, "u_ps")

            def skipped(t):
                i, nxt = t.i, Tile(t.i + 1, 1 - t.b, t.n + t.b)
                pe.wait_ge(S["t_ready"], 2 * i + 2)
                pe.wait_ge(S["silu_ready"], i)
                pe.wait_ge(g_loaded[t.b], 16 * t.n + 16)
                pe.sem_inc(S["g_ps"], 1)
                pe.wait_ge(S["hh_ready"], i)
                pe.wait_ge(d_loaded[1 - t.b], 16 * t.before().n + 16)
                pe.sem_inc(S["d_ps"], 1)
                pe.wait_ge(x_loaded[nxt.b], 16 * nxt.n + 16)
                pe.sem_inc(S["t_ps"], 2)
                pe.wait_ge(u_loaded[t.b], 16 * t.n + 16)
                pe.sem_inc(S["u_ps"], 1)
            tiles_in_use(pe, NB, in_use, tile, skipped)
            down(tile_at(NB - 1))

        @block.scalar
        def _(act):
            def move(t):
                for half in range(2):
                    act.wait_ge(S["t_ps"], 2 * t.i + half + 1)
                    for c in range(4 * half, 4 * half + 4):
                        a = act.activation(XT[t.b][:, c, :], pT[half][:, (c % 4) * P:(c % 4 + 1) * P], ACT.Identity,
                                           bias=M["mod"][:, 3 * KC + c, 0:1], scale=M["mod"][:, 4 * KC + c, 0:1])
                    a.then_inc(S["t_ready"], 1)

            def results(t):
                act.wait_ge(stored[t.b], 16 * t.n + 16)
                act.wait_ge(S["d_ps"], t.i + 1)
                act.activation(Y[t.b][:], pD[:].rearrange("p a b -> p (a b)"), ACT.Copy).then_inc(S["y_ready"], 1)

            move(tile_at(0))

            def tile(t):
                i = t.i
                act.wait_ge(S["g_ps"], i + 1)
                if not t.first:
                    act.wait_ge(S["silu_ready"], i)
                act.activation(TH[:], pG[:], ACT.Tanh, scale=0.5).then_inc(S["th_ready"], 1)
                if not t.first:
                    results(t.before())
                if not (isinstance(i, int) and i == NB - 1):
                    move(Tile(i + 1, 1 - t.b, t.n + t.b))

            def skipped(t):
                before = t.before()
                act.wait_ge(S["g_ps"], t.i + 1)
                act.wait_ge(S["silu_ready"], t.i)
                act.sem_inc(S["th_ready"], 1)
                act.wait_ge(stored[before.b], 16 * before.n + 16)
                act.wait_ge(S["d_ps"], t.i)
                act.sem_inc(S["y_ready"], 1)
                act.wait_ge(S["t_ps"], 2 * t.i + 4)
                act.sem_inc(S["t_ready"], 2)
            tiles_in_use(act, NB, in_use, tile, skipped)
            results(tile_at(NB - 1))

        @block.vector
        def _(dve):
            def tile(t):
                i, h = t.i, HH[t.b][:].rearrange("p a b -> p (a b)")
                dve.wait_ge(S["th_ready"], i + 1)
                dve.scalar_tensor_tensor(h, TH[:], 1.0, pG[:], ALU.add, ALU.mult).then_inc(S["silu_ready"], 1)
                dve.wait_ge(S["silu_ready"], i + 1)
                dve.wait_ge(S["u_ps"], i + 1)
                dve.scalar_tensor_tensor(h, h, 0.5, pU[:], ALU.mult, ALU.mult).then_inc(S["hh_ready"], 1)

            def skipped(t):
                dve.wait_ge(S["th_ready"], t.i + 1)
                dve.sem_inc(S["silu_ready"], 1)
                dve.wait_ge(S["u_ps"], t.i + 1)
                dve.sem_inc(S["hh_ready"], 1)
            tiles_in_use(dve, NB, in_use, tile, skipped)


def combine(nc, I, D, C, M, out):
    with ExitStack() as ctx:
        k = Kit(nc, ctx, "c")
        gate, final_g = k.sb("gate", [P, DM]), k.sb("final_g", [P, DM])
        IDX = [k.sb(f"IDX{b}", [P, 2], I32) for b in range(2)]
        WT = [k.sb(f"WT{b}", [P, 2]) for b in range(2)]
        Y1 = [k.sb(f"Y1{b}", [P, DM]) for b in range(2)]
        Y2 = [k.sb(f"Y2{b}", [P, DM]) for b in range(2)]
        X2 = [k.sb(f"X2{b}", [P, DM]) for b in range(2)]
        junk = k.sb("junk", [P, DM])
        OB = [k.sb(f"OB{b}", [P, DM]) for b in range(2)]
        ssq, std, rstd = ([k.sb(f"{n}{b}", [P, 1]) for b in range(2)] for n in ("ssq", "std", "rstd"))
        names = "loaded_c turn idx_ready pool_turn y1_ready sum_ready step x3_ready ssq_done std_ready rstd_ready out_ready".split()
        S = {n: k.sem(n) for n in names}
        g_loaded, x_loaded, stored = ([k.sem(f"{n}{b}") for b in range(2)] for n in ("g_loaded", "x_loaded", "stored"))
        block = ctx.enter_context(nc.Block())

        @block.sync
        def _(sp):
            wait = waiting_sp(sp, S["turn"])

            def load(t):
                sp.dma_start(X2[t.b][:], D["x2"][t.tokens(), :]).then_inc(x_loaded[t.b], 16)

            sp.dma_start(gate[:], D["gates"][:, DM:2 * DM]).then_inc(S["loaded_c"], 16)
            sp.dma_start(final_g[:], I["final_g"]).then_inc(S["loaded_c"], 16)
            load(tile_at(0))
            load(tile_at(1))
            for b in range(2):
                sp.sem_inc(stored[b], 16)

            def store(t):
                wait(S["out_ready"], t.i + 1)
                sp.dma_start(out[t.tokens(), :], OB[t.b][:]).then_inc(stored[t.b], 16)

            def tile(t):
                if not t.first:
                    store(t.before())
                    if not (isinstance(t.i, int) and t.i == NT - 1):
                        load(Tile(t.i + 1, 1 - t.b, t.n + t.b))

            tiles(sp, NT, tile)
            store(tile_at(NT - 1))
            for b in range(2):
                sp.wait_ge(stored[b], 16 + 16 * (NT // 2))

        @block.gpsimd
        def _(pool):
            def tile(t):
                pool.wait_ge(S["idx_ready"], t.i + 1)
                if not t.first:
                    pool.wait_ge(S["x3_ready"], t.i)
                pool.sem_inc(S["pool_turn"], 1)
                for n, y in ((0, Y1), (1, Y2)):
                    pool.indirect_dma_start(out=y[t.b][:], out_offset=None, in_=D["yb"],
                                            in_offset=bass.IndirectOffsetOnAxis(ap=IDX[t.b][:, n:n + 1], axis=0)).then_inc(g_loaded[t.b], 16)

            tiles(pool, NT, tile)

        @block.scalar
        def _(act):
            act.wait_ge(S["loaded_c"], 32)

            def tile(t):
                i, b = t.i, t.b
                act.wait_ge(g_loaded[b], 32 * t.n + 32)
                act.activation(Y1[b][:], Y1[b][:], ACT.Copy, scale=WT[b][:, 0:1]).then_inc(S["y1_ready"], 1)
                if not t.first:
                    norm(t.before())

            def norm(t):
                act.wait_ge(S["x3_ready"], t.i + 2)
                act.activation(junk[:], X2[t.b][:], ACT.Square, accum_out=ssq[t.b][:]).then_inc(S["ssq_done"], 1)
                act.wait_ge(S["ssq_done"], t.i + 1)
                act.activation(std[t.b][:], ssq[t.b][:], ACT.Sqrt, bias=C["eps"][:], scale=1 / DM).then_inc(S["std_ready"], 1)

            tiles(act, NT, tile)
            norm(tile_at(NT - 1))

        @block.vector
        def _(dve):
            def indices(t):
                dve.tensor_scalar(IDX[t.b][:].unsqueeze(2), M["dest"][:, :, ds(t.i, 1)], 1.0, None, ALU.mult)
                dve.tensor_scalar(WT[t.b][:].unsqueeze(2), M["weights"][:, :, ds(t.i, 1)], 1.0, None, ALU.mult).then_inc(S["idx_ready"], 1)

            dve.wait_ge(S["loaded_c"], 32)
            dve.sem_inc(S["x3_ready"], 1)
            indices(tile_at(0))

            def tile(t):
                i, b = t.i, t.b
                if not (isinstance(i, int) and i == NT - 1):
                    indices(Tile(i + 1, 1 - b, t.n + b))
                dve.wait_ge(S["y1_ready"], i + 1)
                dve.scalar_tensor_tensor(Y1[b][:], Y2[b][:], WT[b][:, 1:2], Y1[b][:], ALU.mult, ALU.add).then_inc(S["sum_ready"], 1)
                dve.wait_ge(S["sum_ready"], i + 1)
                dve.tensor_tensor(Y1[b][:], Y1[b][:], gate[:], ALU.mult).then_inc(S["step"], 1)
                dve.wait_ge(S["step"], i + 1)
                dve.wait_ge(x_loaded[b], 16 * t.n + 16)
                dve.tensor_tensor(X2[b][:], Y1[b][:], X2[b][:], ALU.add).then_inc(S["x3_ready"], 1)
                if not t.first:
                    finish(t.before())

            def finish(t):
                i, b = t.i, t.b
                dve.wait_ge(S["std_ready"], i + 1)
                dve.reciprocal(rstd[b][:], std[b][:]).then_inc(S["rstd_ready"], 1)
                dve.wait_ge(S["rstd_ready"], i + 1)
                dve.wait_ge(stored[b], 16 * t.n + 16)
                dve.scalar_tensor_tensor(OB[b][:], X2[b][:], rstd[b][:], final_g[:], ALU.mult, ALU.mult).then_inc(S["out_ready"], 1)

            tiles(dve, NT, tile)
            finish(tile_at(NT - 1))


def block_pair_kernel(nc, I, out):
    D = {}
    for name, rows, cols in (
        ("qn", H1 * DN, SEQ), ("kn", H1 * DN, SEQ), ("qr", H1 * RD, SEQ), ("kr", P, SEQ), ("v", SEQ, AW), ("ga", SEQ, AW),
        ("gs", SW, SEQ), ("u", SW, SEQ), ("y", SW, SEQ), ("ao", SEQ, AW), ("x1", SEQ, DM), ("gates", P, 2 * DM),
        ("va", SEQ + CTX, KA), ("vr", SEQ + CTX, RW), ("gr", SEQ + CTX, RW), ("krt", SEQ + CTX, RQ),
        ("qka", QA + KA, SEQ + CTX), ("qkr", 2 * RQ, SEQ + CTX), ("ao2", SEQ, QA), ("ret", SEQ, RW), ("x2", SEQ, DM),
        ("h", SEQ, DM), ("yb", NB * P, DM),
    ):
        D[name] = nc.dram_tensor("between_" + name, [rows, cols], F32, kind="Internal").ap()
    D["slots"] = nc.dram_tensor("between_slots", [NB * P, 1], I32, kind="Internal").ap()
    with ExitStack() as ctx:
        k = Kit(nc, ctx, "all")
        C = {"ident": k.sb("ident", [P, P]), "ones": k.sb("ones", [P, P]), "eps": k.sb("eps", [P, 1]),
             "one": k.sb("one", [P, 1]), "half_sign": k.sb("half_sign", [P, 1])}
        M = {"mod": k.sb("mod", [P, NMOD * KC, 2])}
        loaded = k.sem("loaded")
        with nc.Block() as block:
            @block.sync
            def _(sp):
                sp.dma_start(C["ident"][:], I["ident"]).then_inc(loaded, 16)
                sp.dma_start(C["half_sign"][:], I["half_sign"]).then_inc(loaded, 16)
                sp.wait_ge(loaded, 32)

            @block.vector
            def _(dve):
                dve.memset(C["ones"][:], 1.0)
                dve.memset(C["eps"][:], EPS)
                dve.memset(C["one"][:], 1.0)
        with ExitStack() as rope_ctx:
            r = Kit(nc, rope_ctx, "tables")
            cos1, sin1 = r.sb("cos1", [P, NT, RD // 2]), r.sb("sin1", [P, NT, RD // 2])
            rope_tables(nc, I, cos1, sin1)
            project_1(nc, I, D, C, cos1, sin1)
        attention_1(nc, C, D)
        s5(nc, I, D, C)
        mix_1(nc, I, D, C)
        modulations(nc, I, D, C, M)
        project_2(nc, I, D, C, M)
        attention_2(nc, C, D)
        retention(nc, I, D, C)
        M["logits"] = k.sb("logits", [P, NT, NL])
        M["weights"] = k.sb("weights", [P, 2, NT])
        M["dest"] = k.sb("dest", [P, 2, NT], I32)
        M["block_expert"] = k.sb("block_expert", [P, NB], I32)
        M["blocks_in_use"] = k.sb("blocks_in_use", [P, 1], I32)
        mix_2(nc, I, D, C, M)
        dispatch(nc, I, D, C, M)
        experts(nc, I, D, C, M)
        combine(nc, I, D, C, M, out)


def laid_out(inp):
    c = np.ascontiguousarray
    f = np.float32

    def rows(a):
        return c(a.reshape(-1, P).T)

    def all_partitions(a):
        return c(np.broadcast_to(a, (P,) + a.shape))

    I = {n: c(inp[n][0]) for n in ("x", "w_in", "w_uq", "w_ukv", "w_glu", "w_out")}
    I["positions"] = rows(inp["positions"][0])
    I["pre_g"], I["q_g"], I["kv_g"] = (rows(inp[n][0]) for n in ("pre_norm_g", "q_norm_g", "kv_norm_g"))
    I["b_glu"] = rows(inp["b_glu"][0])
    I["out_g"] = rows(np.concatenate([inp["attn_out_g"][0], inp["ssm_out_g"][0]]))
    I["post_g"] = all_partitions(inp["post_norm_g"][0])

    nb = NG // GB

    def by_state(a):
        a = a.reshape(2, nb, GB, NS).transpose(3, 1, 0, 2).reshape(NS, nb, DG)
        return c(np.concatenate([a, a]))

    def matrices(a):
        return a.reshape(2, nb, GB, NS, GC).transpose(3, 1, 0, 2, 4).reshape(NS, nb, DG, GC)

    I["lam_re"], I["lam_im"] = by_state(inp["s5_lam_re"][0]), by_state(inp["s5_lam_im"][0])
    I["log_dt"] = by_state(np.broadcast_to(inp["s5_log_dt"][0][..., None], (2, NG, NS)))
    br, bi = matrices(inp["s5_b_re"][0]), matrices(inp["s5_b_im"][0])
    cr, ci = (matrices(inp[n][0].transpose(0, 1, 3, 2)) for n in ("s5_c_re", "s5_c_im"))
    I["b_v"], I["b_u"], I["c_v"], I["c_u"] = (c(np.concatenate(p)) for p in ((br, bi), (bi, br), (cr, ci), (ci, cr)))
    d = inp["s5_d"][0].reshape(nb, GB, GC).transpose(2, 0, 1)
    I["d_col"] = c(np.broadcast_to(d[None], (T8, GC, nb, GB)).reshape(P, nb, GB))

    I["ctx"], I["w_ada"] = c(inp["ctx_2"][0]), c(inp["w_ada_2"][0])
    I["c2"] = c(np.stack([rows(inp["c_2"][0]), rows(inp["c_ctx_2"])], 2))
    ba = inp["b_ada_2"][0]
    I["b_ada_col"], I["b_gates"] = rows(ba), all_partitions(ba.reshape(NMOD, DM)[[2, 5]])
    I["g12"] = c(np.concatenate([rows(inp["norm1_g_2"][0]), rows(inp["norm2_g_2"][0])], 1))
    I["w_in_2"], I["w_out_2"] = c(inp["w_in_2"][0]), c(inp["w_out_2"][0])
    I["gq"], I["gk"] = all_partitions(inp["attn_q_norm_2"][0]), all_partitions(inp["attn_k_norm_2"][0])
    dec = np.empty((P, HR, 3), f)
    df, db = inp["ret_decay_fwd_2"][0], inp["ret_decay_bwd_2"][0]
    dec[:, :, 0], dec[:, :, 1], dec[:HD, :, 2], dec[HD:, :, 2] = df, db, df, db
    I["ret_decay"] = dec
    I["ret_gn"] = all_partitions(np.stack([inp["ret_gn_g_2"][0].reshape(HR, RV), inp["ret_gn_b_2"][0].reshape(HR, RV)], 1))
    wr = np.concatenate([inp["moe_w_grp_2"][0], inp["moe_w_exp_2"][0]], 1)
    I["w_router"] = c(wr.reshape(KC, P, NL).transpose(1, 0, 2))
    I["b_router"] = all_partitions(np.concatenate([inp["moe_b_grp_2"][0], inp["moe_b_exp_2"][0]]))
    for n in ("moe_w_gate", "moe_w_up", "moe_w_down"):
        I[n] = c(inp[n + "_2"][0])
    I["final_g"] = all_partitions(inp["final_norm_g_2"])

    I["ident"] = np.eye(P, dtype=f)
    I["half_sign"] = np.repeat(np.array([[1.0], [-1.0]], f), P // 2, 0)
    I["inv_freq"] = all_partitions((f(10000.0) ** (-np.arange(0, RD, 2, dtype=f) / f(RD))).astype(f))
    t = np.arange(SEQ)
    freq = (f(10000.0) ** (-np.arange(0, HD // 2, 2, dtype=f) / f(HD // 2))).astype(f)
    ang = np.concatenate([(t // 64).astype(f)[:, None] * freq, (t % 64).astype(f)[:, None] * freq], 1)
    I["cos2"], I["sin2"] = (c(g(ang).astype(f).reshape(NT, P, HD // 2).transpose(1, 0, 2)) for g in (np.cos, np.sin))
    j, i = np.arange(P, dtype=f)[:, None], np.arange(P, dtype=f)[None]
    cross = np.where(j < HD, i + 1, P - i)
    I["ret_expo"] = c(np.stack([np.maximum(i - j, 0), np.maximum(j - i, 0), i >= j, j > i, cross], 1).astype(f))
    I["ret_ecol"] = c(np.concatenate([P - 1 - j, 2 * P - 1 - j, j, P + j, 0 * j + P], 1).astype(f))
    I["rev4"], I["rev8"] = (all_partitions(np.arange(n, 0, -1, dtype=f)) for n in (NGRP, EPG))
    I["mult"] = c(np.broadcast_to(P * np.arange(NT, dtype=f), (P, NE, NT)))
    I["block_numbers"] = all_partitions(np.arange(NB, dtype=f))
    I["upper"] = (j < i).astype(f)
    I["token_numbers"] = c(np.arange(SEQ, dtype=np.int32).reshape(NT, P).T)
    return I


def kernel(**inputs):
    import concourse.bacc as bacc
    from concourse.bass_utils import run_bass_kernel_spmd

    arrays = laid_out({n: np.asarray(a) for n, a in inputs.items()})
    nc = bacc.Bacc("TRN2", target_bir_lowering=False, num_devices=1)
    I = {n: nc.dram_tensor("in_" + n, a.shape, mybir.dt.from_np(a.dtype), kind="ExternalInput").ap() for n, a in arrays.items()}
    out = nc.dram_tensor("out", [SEQ, DM], F32, kind="ExternalOutput").ap()
    block_pair_kernel(nc, I, out)
    r = run_bass_kernel_spmd(nc, [{"in_" + n: a for n, a in arrays.items()}], core_ids=[0])
    return r.results[0]["out"].reshape(1, SEQ, DM)
```
